# Optimizing a Trainium2 kernel written in Bass

```python
import jax
import jax.numpy as jnp
from jax import lax
import numpy as np

D_MODEL = 1024
BATCH = 1
SEQ = 256
DEPTH = 2

GRID_W = 64
CTX_LEN = 256
Q_BLOCK = 128
ROPE_THETA = 10000.0
HEAD_DIM = 64
A_HEADS = 8
A_KV_HEADS = 2
MLA_HEADS = 8
MLA_Q_RANK = 384
MLA_KV_RANK = 256
MLA_NOPE = 64
MLA_ROPE = 32
MLA_V = 64
NA_HEADS = 8
NBR_ROWS = 8
NBR_COLS = 16
HG_HEADS = 4
HG_EXPAND = 128
HG_WIDTH = HG_HEADS * HG_EXPAND
HG_CHUNK = 64
D_FF = 2816
N_EXPERTS = 8
TOP_K = 2
D_FF_EXPERT = 3584
ALPHA = (2 * DEPTH) ** 0.25
BETA = (8 * DEPTH) ** -0.25
N_EVEN = (DEPTH + 1) // 2
N_ODD = DEPTH // 2
EV_SIZES = (A_HEADS * HEAD_DIM, A_KV_HEADS * HEAD_DIM, A_KV_HEADS * HEAD_DIM, MLA_Q_RANK, MLA_KV_RANK, MLA_ROPE)
EV_IN = sum(EV_SIZES)
EV_OUT = A_HEADS * HEAD_DIM + MLA_HEADS * MLA_V
OD_SIZES = (NA_HEADS * HEAD_DIM,) * 3 + (HG_WIDTH,) * 5
OD_IN = sum(OD_SIZES)
OD_OUT = NA_HEADS * HEAD_DIM + HG_WIDTH
F32 = jnp.float32

kernel_name = 'hybrid_dit_gqa_mla_natten_hgrn2_moe'

def split_cols(p, sizes):
    out, start = [], 0
    for s in sizes:
        out.append(p[..., start:start + s])
        start += s
    return out

def rms_norm(x, g, eps=1e-6):
    xf = x.astype(F32)
    y = xf * lax.rsqrt(jnp.mean(xf * xf, axis=-1, keepdims=True) + eps)
    return (y * g.astype(F32)).astype(x.dtype)

def layer_norm(x, g, b, eps=1e-6):
    xf = x.astype(F32)
    mu = jnp.mean(xf, axis=-1, keepdims=True)
    var = jnp.mean(jnp.square(xf - mu), axis=-1, keepdims=True)
    return ((xf - mu) * lax.rsqrt(var + eps) * g.astype(F32) + b.astype(F32)).astype(x.dtype)

def modulate(x, shift, scale):
    return x * (1 + scale) + shift

def axial_rope_tables(n_tokens, rot_dim, dtype):
    axis_dim = rot_dim // 2
    inv_freq = ROPE_THETA ** (-jnp.arange(0, axis_dim, 2, dtype=F32) / axis_dim)
    t = jnp.arange(n_tokens, dtype=jnp.int32)
    pos = jnp.stack([t // GRID_W, t % GRID_W], axis=-1).astype(F32)
    ang = pos[:, :, None] * inv_freq
    ang = jnp.concatenate([ang, ang], axis=-1).reshape(n_tokens, rot_dim)
    return jnp.cos(ang).astype(dtype), jnp.sin(ang).astype(dtype)

def apply_axial_rope(x, cos, sin):
    rot_dim = x.shape[-1]
    axis_dim = rot_dim // 2
    half = axis_dim // 2
    xs = x.reshape(x.shape[:-1] + (2, axis_dim))
    rot = jnp.concatenate([-xs[..., half:], xs[..., :half]], axis=-1).reshape(x.shape)
    return x * cos[None, :, None, :] + rot * sin[None, :, None, :]

def blocked_attention(q, k, v):
    B, Sq, G, R, Dk = q.shape
    nb = Sq // Q_BLOCK
    scale = Dk ** -0.5
    qb = jnp.moveaxis(q.reshape(B, nb, Q_BLOCK, G, R, Dk), 1, 0)

    def one_block(qblk):
        s = jnp.einsum('bqgrd,bkgd->bgrqk', qblk, k).astype(F32) * scale
        p = jax.nn.softmax(s, axis=-1).astype(v.dtype)
        return jnp.einsum('bgrqk,bkgd->bqgrd', p, v)

    o = lax.map(one_block, qb)
    return jnp.moveaxis(o, 0, 1).reshape(B, Sq, G, R, v.shape[-1])

def neighbourhood_attention(q, k, v, k_ctx, v_ctx, rpb):
    B, S, H, Dh = q.shape
    rows = S // GRID_W
    kh = min(NBR_ROWS, rows)
    kw = NBR_COLS
    r = np.arange(rows)
    row_start = np.clip(r - kh // 2, 0, rows - kh)
    dr_idx = row_start[:, None] + np.arange(kh)[None, :] - r[:, None] + (NBR_ROWS - 1)
    cc = np.arange(GRID_W)
    col_start = np.clip(cc - kw // 2, 0, GRID_W - kw)
    col_idx = col_start[:, None] + np.arange(kw)[None, :]
    dc_idx = col_idx - cc[:, None] + (NBR_COLS - 1)
    rpb_c = rpb[:, :, dc_idx]
    scale = Dh ** -0.5
    q_rows = jnp.moveaxis(q.reshape(B, rows, GRID_W, H, Dh), 1, 0)
    kg = k.reshape(B, rows, GRID_W, H, Dh)
    vg = v.reshape(B, rows, GRID_W, H, Dh)
    n_win = kh * kw

    def one_row(args):
        q_r, r0, dr = args
        kb = lax.dynamic_slice_in_dim(kg, r0, kh, axis=1)
        vb = lax.dynamic_slice_in_dim(vg, r0, kh, axis=1)
        kwin = kb[:, :, col_idx]
        vwin = vb[:, :, col_idx]
        bias = jnp.take(rpb_c, dr, axis=1).transpose(0, 2, 1, 3).astype(F32)
        s_win = jnp.einsum('bchd,bicjhd->bhcij', q_r, kwin).astype(F32) * scale + bias[None]
        s_ctx = jnp.einsum('bchd,bkhd->bhck', q_r, k_ctx).astype(F32) * scale
        s = jnp.concatenate([s_win.reshape(B, H, GRID_W, n_win), s_ctx], axis=-1)
        p = jax.nn.softmax(s, axis=-1).astype(v.dtype)
        p_win = p[..., :n_win].reshape(B, H, GRID_W, kh, kw)
        p_ctx = p[..., n_win:]
        return (jnp.einsum('bhcij,bicjhd->bchd', p_win, vwin)
                + jnp.einsum('bhck,bkhd->bchd', p_ctx, v_ctx))

    o = lax.map(one_row, (q_rows, jnp.asarray(row_start, jnp.int32), jnp.asarray(dr_idx, jnp.int32)))
    return jnp.moveaxis(o, 0, 1).reshape(B, S, H, Dh)

def gla_chunk_scan(q, k, v, log_f, s0, with_outputs):
    B, L, H, E = q.shape
    n = L // HG_CHUNK

    def to_chunks(t):
        return t.reshape(B, n, HG_CHUNK, H, E).transpose(1, 0, 3, 2, 4)

    causal = jnp.tril(jnp.ones((HG_CHUNK, HG_CHUNK), dtype=bool))

    def step(state, blk):
        qc, kc, vc, gc = blk
        b = jnp.cumsum(gc, axis=2)
        b_end = b[:, :, -1, :]
        k_end = kc * jnp.exp(b_end[:, :, None, :] - b)
        new_state = jnp.exp(b_end)[..., None] * state + jnp.einsum('bhse,bhsf->bhef', k_end, vc)
        if not with_outputs:
            return new_state, None
        diff = b[:, :, :, None, :] - b[:, :, None, :, :]
        decay = jnp.exp(jnp.where(causal[:, :, None], diff, -jnp.inf))
        scores = jnp.einsum('bhte,bhtse,bhse->bhts', qc, decay, kc)
        out = (jnp.einsum('bhts,bhsf->bhtf', scores, vc)
               + jnp.einsum('bhte,bhef->bhtf', qc * jnp.exp(b), state))
        return new_state, out

    final, outs = lax.scan(step, s0, (to_chunks(q), to_chunks(k), to_chunks(v), to_chunks(log_f)))
    if not with_outputs:
        return final, None
    return final, outs.transpose(1, 0, 3, 2, 4).reshape(B, L, H, E)

def hgrn_forget(z, lb):
    zf = z.astype(F32)
    lb = lb.reshape(HG_HEADS, HG_EXPAND)
    f = lb + (1.0 - lb) * jax.nn.sigmoid(zf)
    return (1.0 - lb) * jax.nn.sigmoid(-zf), jnp.log(f)

def hgrn2_bidirectional(lat, ctx, need_ctx):
    ql, vl, kfl, gfl, kbl, gbl = lat
    qc, vc, kfc, gfc, kbc, gbc = ctx
    B = ql.shape[0]
    s0 = jnp.zeros((B, HG_HEADS, HG_EXPAND, HG_EXPAND), F32)
    flip = lambda t: jnp.flip(t, axis=1)
    s_cf, o_cf = gla_chunk_scan(qc, kfc, vc, gfc, s0, need_ctx)
    _, o_lf = gla_chunk_scan(ql, kfl, vl, gfl, s_cf, True)
    s_cb, o_cb = gla_chunk_scan(flip(qc), flip(kbc), flip(vc), flip(gbc), s0, need_ctx)
    _, o_lb = gla_chunk_scan(flip(ql), flip(kbl), flip(vl), flip(gbl), s_cb, True)
    o_l = o_lf + flip(o_lb)
    o_c = (o_cf + flip(o_cb)) if need_ctx else None
    return o_l, o_c

def hgrn_readout(o, g, onorm_g):
    B, L = g.shape[:2]
    y = rms_norm(o, onorm_g) * jax.nn.silu(g.astype(F32))
    return y.astype(g.dtype).reshape(B, L, HG_WIDTH)

def attn_mla_mixer(hl, hc, w_in, qn_g, kn_g, cq_g, ckv_g, w_uq, w_ukv, w_out, rope_a, rope_b, need_ctx):
    def project(h, with_rope):
        B, L, _ = h.shape
        qa, ka, va, cq, ckv, kr = split_cols(h @ w_in, EV_SIZES)
        qa = rms_norm(qa.reshape(B, L, A_HEADS, HEAD_DIM), qn_g)
        ka = rms_norm(ka.reshape(B, L, A_KV_HEADS, HEAD_DIM), kn_g)
        va = va.reshape(B, L, A_KV_HEADS, HEAD_DIM)
        qb = (rms_norm(cq, cq_g) @ w_uq).reshape(B, L, MLA_HEADS, MLA_NOPE + MLA_ROPE)
        kvb = (rms_norm(ckv, ckv_g) @ w_ukv).reshape(B, L, MLA_HEADS, MLA_NOPE + MLA_V)
        q_rope = qb[..., MLA_NOPE:]
        k_rope = kr.reshape(B, L, 1, MLA_ROPE)
        if with_rope:
            qa = apply_axial_rope(qa, *rope_a)
            ka = apply_axial_rope(ka, *rope_a)
            q_rope = apply_axial_rope(q_rope, *rope_b)
            k_rope = apply_axial_rope(k_rope, *rope_b)
        qb = jnp.concatenate([qb[..., :MLA_NOPE], q_rope], axis=-1)
        kb = jnp.concatenate([kvb[..., :MLA_NOPE], jnp.broadcast_to(k_rope, (B, L, MLA_HEADS, MLA_ROPE))], axis=-1)
        vb = kvb[..., MLA_NOPE:]
        qa = qa.reshape(B, L, A_KV_HEADS, A_HEADS // A_KV_HEADS, HEAD_DIM)
        return qa, ka, va, qb[:, :, :, None, :], kb, vb

    B, S, _ = hl.shape
    qa_l, ka_l, va_l, qb_l, kb_l, vb_l = project(hl, True)
    qa_c, ka_c, va_c, qb_c, kb_c, vb_c = project(hc, False)
    oa_l = blocked_attention(qa_l, jnp.concatenate([ka_l, ka_c], axis=1), jnp.concatenate([va_l, va_c], axis=1))
    ob_l = blocked_attention(qb_l, jnp.concatenate([kb_l, kb_c], axis=1), jnp.concatenate([vb_l, vb_c], axis=1))
    yl = jnp.concatenate([oa_l.reshape(B, S, A_HEADS * HEAD_DIM), ob_l.reshape(B, S, MLA_HEADS * MLA_V)], axis=-1) @ w_out
    if not need_ctx:
        return yl, None
    Lc = hc.shape[1]
    oa_c = blocked_attention(qa_c, ka_c, va_c)
    ob_c = blocked_attention(qb_c, kb_c, vb_c)
    yc = jnp.concatenate([oa_c.reshape(B, Lc, A_HEADS * HEAD_DIM), ob_c.reshape(B, Lc, MLA_HEADS * MLA_V)], axis=-1) @ w_out
    return yl, yc

def na_hgrn_mixer(hl, hc, w_in, rpb, lb_fwd, lb_bwd, onorm_g, w_out, need_ctx):
    def project(h):
        B, L, _ = h.shape
        parts = split_cols(h @ w_in, OD_SIZES)
        qn, kn, vn = [p.reshape(B, L, NA_HEADS, HEAD_DIM) for p in parts[:3]]
        qd, vd, zf, zb, gd = [p.reshape(B, L, HG_HEADS, HG_EXPAND) for p in parts[3:]]
        k_f, logf_f = hgrn_forget(zf, lb_fwd)
        k_b, logf_b = hgrn_forget(zb, lb_bwd)
        hg = (jax.nn.silu(qd).astype(F32), vd.astype(F32), k_f, logf_f, k_b, logf_b)
        return (qn, kn, vn), hg, gd

    B, S, _ = hl.shape
    (qn_l, kn_l, vn_l), hg_l, g_l = project(hl)
    (qn_c, kn_c, vn_c), hg_c, g_c = project(hc)
    on_l = neighbourhood_attention(qn_l, kn_l, vn_l, kn_c, vn_c, rpb)
    od_l, od_c = hgrn2_bidirectional(hg_l, hg_c, need_ctx)
    yl = jnp.concatenate([on_l.reshape(B, S, NA_HEADS * HEAD_DIM), hgrn_readout(od_l, g_l, onorm_g)], axis=-1) @ w_out
    if not need_ctx:
        return yl, None
    Lc = hc.shape[1]
    on_c = blocked_attention(qn_c[:, :, :, None, :], kn_c, vn_c)
    yc = jnp.concatenate([on_c.reshape(B, Lc, NA_HEADS * HEAD_DIM), hgrn_readout(od_c, g_c, onorm_g)], axis=-1) @ w_out
    return yl, yc

def swiglu(h, wg, wu, wd):
    return (jax.nn.silu(h @ wg) * (h @ wu)) @ wd

def moe_ffn(h, router, wg, wu, wd):
    logits = (h @ router).astype(F32)
    top_v, top_i = lax.top_k(logits, TOP_K)
    w = jax.nn.softmax(top_v, axis=-1)
    gates = jnp.sum(jax.nn.one_hot(top_i, N_EXPERTS, dtype=F32) * w[..., None], axis=-2).astype(h.dtype)
    y = jnp.zeros_like(h)
    for e in range(N_EXPERTS):
        y = y + gates[..., e:e + 1] * swiglu(h, wg[e], wu[e], wd[e])
    return y

def setup_inputs(seed: int = 0) -> dict:
    key = jax.random.key(seed)
    ks = iter(jax.random.split(key, 40))
    D = D_MODEL

    def nrm(shape, scale):
        return jax.random.normal(next(ks), shape, F32) * scale

    def gain(shape):
        return 1.0 + nrm(shape, 0.02)

    return {
        'x': nrm((BATCH, SEQ, D), 1.0),
        'c': nrm((BATCH, D), 1.0),
        'ctx': nrm((BATCH, CTX_LEN, D), 1.0),
        'c_ctx': nrm((D,), 1.0),
        'ada_w': nrm((DEPTH, D, 6 * D), 0.5 * D ** -0.5),
        'ada_b': nrm((DEPTH, 6 * D), 0.02),
        'ln1_g': gain((DEPTH, D)),
        'ln1_b': nrm((DEPTH, D), 0.02),
        'ln2_g': gain((DEPTH, D)),
        'ln2_b': nrm((DEPTH, D), 0.02),
        'ev_w_in': nrm((N_EVEN, D, EV_IN), D ** -0.5),
        'ev_qn_g': gain((N_EVEN, HEAD_DIM)),
        'ev_kn_g': gain((N_EVEN, HEAD_DIM)),
        'ev_cq_g': gain((N_EVEN, MLA_Q_RANK)),
        'ev_ckv_g': gain((N_EVEN, MLA_KV_RANK)),
        'ev_w_uq': nrm((N_EVEN, MLA_Q_RANK, MLA_HEADS * (MLA_NOPE + MLA_ROPE)), MLA_Q_RANK ** -0.5),
        'ev_w_ukv': nrm((N_EVEN, MLA_KV_RANK, MLA_HEADS * (MLA_NOPE + MLA_V)), MLA_KV_RANK ** -0.5),
        'ev_w_out': nrm((N_EVEN, EV_OUT, D), BETA * EV_OUT ** -0.5),
        'ff_w_gate': nrm((N_EVEN, D, D_FF), D ** -0.5),
        'ff_w_up': nrm((N_EVEN, D, D_FF), D ** -0.5),
        'ff_w_down': nrm((N_EVEN, D_FF, D), BETA * D_FF ** -0.5),
        'od_w_in': nrm((N_ODD, D, OD_IN), D ** -0.5),
        'od_rpb': nrm((N_ODD, NA_HEADS, 2 * NBR_ROWS - 1, 2 * NBR_COLS - 1), 0.02),
        'od_lb_logits': nrm((2, N_ODD, HG_WIDTH), 0.1),
        'od_onorm_g': gain((N_ODD, HG_EXPAND)),
        'od_w_out': nrm((N_ODD, OD_OUT, D), BETA * OD_OUT ** -0.5),
        'moe_router': nrm((N_ODD, D, N_EXPERTS), D ** -0.5),
        'moe_w_gate': nrm((N_ODD, N_EXPERTS, D, D_FF_EXPERT), D ** -0.5),
        'moe_w_up': nrm((N_ODD, N_EXPERTS, D, D_FF_EXPERT), D ** -0.5),
        'moe_w_down': nrm((N_ODD, N_EXPERTS, D_FF_EXPERT, D), BETA * D_FF_EXPERT ** -0.5),
    }

def reference(x, c, ctx, c_ctx, ada_w, ada_b, ln1_g, ln1_b, ln2_g, ln2_b,
              ev_w_in, ev_qn_g, ev_kn_g, ev_cq_g, ev_ckv_g, ev_w_uq, ev_w_ukv, ev_w_out,
              ff_w_gate, ff_w_up, ff_w_down,
              od_w_in, od_rpb, od_lb_logits, od_onorm_g, od_w_out,
              moe_router, moe_w_gate, moe_w_up, moe_w_down):
    B, S, _ = x.shape
    rope_a = axial_rope_tables(S, HEAD_DIM, x.dtype)
    rope_b = axial_rope_tables(S, MLA_ROPE, x.dtype)
    lb_p = jax.nn.softmax(od_lb_logits.astype(F32), axis=1)
    lb_tab = jnp.cumsum(lb_p, axis=1) - lb_p[:, :1]
    s_lat = jax.nn.silu(c)
    s_ctx = jax.nn.silu(c_ctx)
    xl, xc = x, ctx

    for layer in range(DEPTH):
        need_ctx = layer < DEPTH - 1
        j = layer // 2
        mod_l = jnp.split((s_lat @ ada_w[layer] + ada_b[layer])[:, None, :], 6, axis=-1)
        mod_c = jnp.split((s_ctx @ ada_w[layer] + ada_b[layer])[None, None, :], 6, axis=-1)
        hl = modulate(xl, mod_l[0], mod_l[1])
        hc = modulate(xc, mod_c[0], mod_c[1])
        if layer % 2 == 0:
            yl, yc = attn_mla_mixer(hl, hc, ev_w_in[j], ev_qn_g[j], ev_kn_g[j], ev_cq_g[j], ev_ckv_g[j],
                                    ev_w_uq[j], ev_w_ukv[j], ev_w_out[j], rope_a, rope_b, need_ctx)
        else:
            yl, yc = na_hgrn_mixer(hl, hc, od_w_in[j], od_rpb[j], lb_tab[0, j], lb_tab[1, j],
                                   od_onorm_g[j], od_w_out[j], need_ctx)

        def channel_mixer(h):
            if layer % 2 == 0:
                return swiglu(h, ff_w_gate[j], ff_w_up[j], ff_w_down[j])
            return moe_ffn(h, moe_router[j], moe_w_gate[j], moe_w_up[j], moe_w_down[j])

        xl = layer_norm(ALPHA * xl + mod_l[2] * yl, ln1_g[layer], ln1_b[layer])
        xl = layer_norm(ALPHA * xl + mod_l[5] * channel_mixer(modulate(xl, mod_l[3], mod_l[4])),
                        ln2_g[layer], ln2_b[layer])
        if need_ctx:
            xc = layer_norm(ALPHA * xc + mod_c[2] * yc, ln1_g[layer], ln1_b[layer])
            xc = layer_norm(ALPHA * xc + mod_c[5] * channel_mixer(modulate(xc, mod_c[3], mod_c[4])),
                            ln2_g[layer], ln2_b[layer])
    return xl


_drawn_inputs = setup_inputs


def setup_inputs(seed=0):
    import zlib

    import numpy as np

    out = dict(_drawn_inputs(seed))
    spreads = {}
    factors = {'ctx': 5.333,
     'ada_b': 5.23,
     'ev_qn_g': 8.0,
     'ev_kn_g': 22.74,
     'ev_cq_g': 8.0,
     'ev_ckv_g': 8.0,
     'ev_w_uq': 7.012,
     'ev_w_ukv': 3.087,
     'od_rpb': 64.0,
     'od_onorm_g': 55.322}
    for name, (base, spread) in spreads.items():
        noise = np.random.default_rng([zlib.crc32(name.encode()), seed]).standard_normal(out[name].shape)
        drawn = base * np.exp(spread * noise) if base else spread * noise
        out[name] = jnp.asarray(drawn.astype(out[name].dtype))
    for name, factor in factors.items():
        out[name] = (out[name] * factor).astype(out[name].dtype)
    return out
```

```python
from contextlib import ExitStack

import numpy as np

import concourse.bass as bass
from concourse import mybir

F32 = mybir.dt.float32
F32R = mybir.dt.float32r
I32 = mybir.dt.int32
ALU = mybir.AluOpType
ACT = mybir.ActivationFunctionType
AX = mybir.AxisListType

P = 128
D = 1024
DK = D // P
SEQ = 256
CTX = 256
TOK = SEQ + CTX
NT = TOK // P
NL = SEQ // P
GRID_W = 64
ROWS = SEQ // GRID_W
DEPTH = 2
ALPHA = (2 * DEPTH) ** 0.25
HEADS = 8
HD = 64
KVH = 2
QR = 384
KVR = 256
NOPE = 64
ROPE = 32
QKB = NOPE + ROPE
EV_IN = 1440
DFF = 2816
FK = DFF // P
OD_IN = 4096
NE = 8
DFE = 3584
EK = DFE // P
HGH = 4
NBR_ROWS = 8
NBR_COLS = 16
RPB_W = 2 * NBR_COLS - 1
RPB_PAD = GRID_W - NBR_COLS
RPB_PW = RPB_W + 2 * RPB_PAD
SLOT = 4096
RING = 7
RING0 = 4
CAP = P
EXTRA = (2 * SEQ) // (CAP + 1)
ROUNDS = NE + EXTRA
UNIT = SLOT // 4
POOLQ = 1
HBUF = 4
UNITS = 84
LEVELS = [64, 32, 16, 8, 4, 2, 1]
F_MIN = 2.0 ** -63
NEG = -1e30


def constants():
    ident = np.eye(P, dtype=np.float32)
    iota = np.tile(np.arange(P, dtype=np.float32), (P, 1))
    upper = np.triu(np.ones((P, P), np.float32), 1)
    ones = np.ones((P, P), np.float32)
    flip = np.kron(np.eye(P // GRID_W), np.eye(GRID_W)[::-1]).astype(np.float32)
    base = np.concatenate([ident, iota, upper, ones, flip], 1)
    tabs = []
    t = np.arange(SEQ)
    pos = np.stack([t // GRID_W, t % GRID_W], -1).astype(np.float32)
    for rot in (HD, ROPE):
        ad = rot // 2
        inv = (np.float32(10000.0) ** (-np.arange(0, ad, 2, dtype=np.float32) / ad)).astype(np.float32)
        ang = pos[:, :, None] * inv
        ang = np.concatenate([ang, ang], -1).reshape(SEQ, rot)
        sin = np.sin(ang).reshape(SEQ, 2, 2, ad // 2)
        sin = sin * np.array([-1.0, 1.0], np.float32)[None, None, :, None]
        tabs += [np.cos(ang), sin.reshape(SEQ, rot)]
    rope = np.concatenate(tabs, 1).astype(np.float32)
    cc = np.arange(GRID_W)
    start = np.clip(cc - NBR_COLS // 2, 0, GRID_W - NBR_COLS)
    inside = (cc[None, :] >= start[:, None]) & (cc[None, :] < start[:, None] + NBR_COLS)
    window = np.tile(np.where(inside, 0.0, NEG).astype(np.float32)[::-1], (2, 1))
    s, tt = np.meshgrid(np.arange(P), np.arange(P), indexing="ij")
    masks = []
    for m in LEVELS:
        same = (s // (2 * m)) == (tt // (2 * m))
        fwd = same & (s % (2 * m) < m) & (tt % (2 * m) >= m)
        masks += [fwd, fwd.T]
    masks.append(s == tt)
    hg = np.concatenate([window] + [m.astype(np.float32) for m in masks], 1)
    return base, rope, np.ascontiguousarray(hg)


def bass_hybrid_dit(nc, A, out, stop=None, taps=None):
    es = ExitStack()
    with es:
        NMEM = 53200
        start = -(-nc.sbuf_base // 32) * 32
        AREAS = [0, SLOT, 2 * SLOT, 3 * SLOT, 4 * SLOT, 7 * SLOT, 8 * SLOT, 9 * SLOT, 10 * SLOT, 10 * SLOT + 1704, NMEM]
        areas = {}
        pb = [es.enter_context(nc.psum_tensor(f"bank{i}", [P, 512], F32)) for i in range(8)]
        sems = {}

        def S(name):
            if name not in sems:
                sems[name] = es.enter_context(nc.semaphore(name))
            return sems[name]

        def at(a, *dims, parts=P, kind=F32):
            n = int(np.prod(dims))
            i = max(i for i, first in enumerate(AREAS) if first <= a)
            first, end = AREAS[i], AREAS[i + 1]
            assert a + n <= end
            if (i, kind) not in areas:
                name = f"area{i}" if kind == F32 else f"parts{i}"
                areas[i, kind] = nc.alloc_sbuf_tensor_at(name, [P, end - first], kind, offset=start + 4 * first)
            v = areas[i, kind][0:parts, a - first:a - first + n]
            if len(dims) == 2:
                v = v.rearrange("p (a b) -> p a b", a=dims[0])
            if len(dims) == 3:
                v = v.rearrange("p (a b c) -> p a b c", a=dims[0], b=dims[1])
            return v

        def part(a, *dims):
            return at(a, *dims, kind=F32R)

        def bc(ap, *shape):
            return ap.broadcast_to(list(shape))

        slot = [i * SLOT for i in range(RING)]
        ARENA = RING0 * SLOT
        X = RING * SLOT
        HT = X + 4096
        G = HT + 4096
        base_c = G + 4096
        ident = at(base_c, P)
        iota = at(base_c + 128, P)
        upper = at(base_c + 256, P)
        ones = at(base_c + 384, P)
        flip = at(base_c + 512, P)
        c0 = base_c + 640
        vcol = at(c0, 88)
        adab = at(c0 + 88, 96)
        modT = at(c0 + 184, 2, 48, 2)
        AB = at(c0 + 376, 3, 2, 16)
        sT = at(c0 + 472, 16)
        lnst = at(c0 + 488, NT, 16)
        eps_c = at(c0 + 88 + 96 + 192 + 96 + 15 + 1 + 64, 1)
        small = c0 + 560
        BB = small + 504
        xr = at(X, NT, D)
        hT = at(HT, DK, TOK)
        gb = at(G, 2, D)
        lnrow = at(G + 2048, 2, D)

        qTa = at(ARENA, 4, TOK)
        kTa = at(ARENA + 2048, KVH, TOK)
        va = at(ARENA + 3072, NT, P)
        qTb = at(ARENA + 3584, HEADS, TOK)
        kTb = at(ARENA + 7680, HEADS, TOK)
        ropt = at(HT, 640)
        vb = at(BB, NT, 512)
        PJ = BB + 2048
        proj = at(PJ, NT, EV_IN)
        rope_c = at(PJ + 5760, NL, 192)
        gains = at(PJ + 6144, 10, HD)
        cqg = at(PJ + 6784, QR)
        ckvg = at(PJ + 7168, KVR)
        ssq = at(PJ + 7424, NT, 16)
        sqj = at(PJ + 7488, 640)
        qbt = at(G, 2, HEADS, QKB)
        kbt = at(G + 1536, 2, HEADS, QKB)
        latT = at(G + 3072, 5, P)
        kdup = at(G + 3712, KVH, 2, HD)
        oA = at(PJ, NT, D)
        p_sb = at(PJ + 4096, 2, 512)
        pT_sb = at(PJ + 6144, 2, 512)
        oT = hT
        mx = at(small, 4, 4)
        rowbuf = at(PJ + 7424, 2, 512)
        vr1 = at(PJ, P)
        vr2 = at(PJ + 128, P)
        aT0 = at(ARENA, FK, TOK)
        sil = at(BB, 2, 512)
        lt = at(BB + 1024, 2, D)
        diag = at(BB + 1024, 2, 512)

        qnT = at(ARENA, 4, SEQ)
        knT = at(ARENA + 1024, 4, TOK)
        vn = at(ARENA + 3072, NT, 512)
        oT1 = at(ARENA + 3072, DK, SEQ)
        qd = at(ARENA + 5120, HGH, SEQ)
        vd = at(ARENA + 6144, NT, 512)
        gd = at(ARENA + 8192, NL, 512)
        kf = at(ARENA + 9216, HGH, TOK)
        qxf = at(ARENA + 11264, HGH, SEQ)
        kb = at(BB, HGH, TOK)
        CW = SEQ + 1
        cum = [at(BB + 2048 + i * 2 * HGH * CW, 2, HGH, CW) for i in range(2)]
        BI = BB + 2048 + 4 * HGH * CW
        bias = at(BI, 2 * HEADS, SEQ)
        AT = at(BI, NL, HGH, SEQ)
        kendT = at(BI + 2048, NL, HGH, P)
        state = at(BI + 3072, 2, HGH, P)
        onorm = at(BI + 4096, P)
        rms1 = at(BI + 4224, NL, HGH)
        forget = at(X + 2048, HGH, TOK)
        p1 = at(HT, 2, 512)
        pT1 = at(HT + 1024, 2, 512)
        qxb = at(HT, HGH, SEQ)
        ksum = at(HT + 1024, HGH, SEQ)
        W = [at(HT + 2048 + 1024 * i, HGH, SEQ) for i in range(2)]
        window = at(G, GRID_W)
        masks = at(G + GRID_W, 2 * len(LEVELS) + 1, P)
        o1 = at(G + 1984, NL, D)
        lbs = at(small + 16, 6, 2 * HGH)
        hsH, hsL = part(BB, DK, P), part(BB + 1024, DK, P)
        yacc = at(BB + 2048, NL, D)
        aH, aL = part(BB + 4096, EK, P), part(G, EK, P)
        s_e = at(BB + 7680, 2, 512)
        sel = at(BB + 8704, NL, P)
        selG = at(BB + 8960, NL, P)
        selGT = at(BB + 9216, SEQ)
        hsN = at(BB + 9472, DK, P)
        y_e = at(BB + 9472, D)
        wH = [part(HT + UNIT * i, UNIT) for i in range(HBUF)]
        router = at(small + 80, DK, NE)
        RT = small + 144
        NR = ROUNDS + 1
        posT = at(RT, NL, NR)
        gateT = at(RT + 24, NL, NR)
        ids = at(RT + 48, NR).bitcast(I32)
        nover = at(RT + 60, 1).bitcast(I32)
        rt = [at(RT + 64 + 16 * i, NL, NE) for i in range(10)]
        r1 = at(RT + 230, 8, NL)

        def rows(ap, pat, **k):
            return ap.rearrange(pat, **k)

        def cols_slot(w, a, b):
            return w.rearrange("(k p) n -> p k n", p=P)[:, :, a:b]

        def rows_slot(w, k0, k1):
            return w.rearrange("(k p) n -> p k n", p=P)[:, k0:k1, :]

        loads = []

        def add(name, src, a, b, *read):
            loads.append((name, src, a, b, read))

        def ada_loads(L):
            for j in range(12):
                add(("ada", L, j), cols_slot(A["ada_w"][L], 512 * j, 512 * j + 512), DK, 512,
                    "mod_mm", 12 * L + j + 1)
        ada_loads(0)
        EVC = [(0, 512), (512, 1024), (1024, EV_IN)]
        for i, (a, b) in enumerate(EVC):
            add(("evin", a), cols_slot(A["ev_w_in"][0], a, b), DK, b - a, "proj_mm", NT * (i + 1))
        add(("uq",), rows_slot(A["ev_w_uq"][0], 0, 3), 3, 768, "up_mm", 2 * NT)
        add(("ukv",), rows_slot(A["ev_w_ukv"][0], 0, 2), 2, 1024, "up_mm", 2 * NT)
        for c in range(2):
            add(("evout", c), cols_slot(A["ev_w_out"][0], 512 * c, 512 * c + 512), DK, 512, "y_mm", NT)
        ada_loads(1)
        FC = [(a, min(a + 512, DFF)) for a in range(0, DFF, 512)]
        for a, b in FC:
            add(("fg", a), cols_slot(A["ff_w_gate"][0], a, b), DK, b - a, "ff_mm", b // P)
            add(("fu", a), cols_slot(A["ff_w_up"][0], a, b), DK, b - a, "ff_mm", b // P)
        FD = [(a, min(a + 4, FK)) for a in range(0, FK, 4)]
        for i, (a, b) in enumerate(FD):
            add(("fd", a), rows_slot(A["ff_w_down"][0], a, b), b - a, D,
                *(("fd_mm", i + 1) if b < FK else ("y_mm", 2 * NT)))
        ORDER1 = [5, 6, 3, 0, 1, 2, 4, 7]
        in1 = [(c, i) for c in ORDER1 for i in range(NL if c == 7 else 4)]
        for c in ORDER1:
            add(("odin", c), cols_slot(A["od_w_in"][0], 512 * c, 512 * c + 512), DK, 512,
                "in1_mm", max(i for i, u in enumerate(in1) if u[0] == c) + 1)
        for c in range(2):
            add(("odout", c), cols_slot(A["od_w_out"][0], 512 * c, 512 * c + 512), DK, 512, "y_mm", 2 * NT + NL)
        index = {name: n for n, (name, *_) in enumerate(loads)}
        NPRE = len(loads)
        base_n = [len(range(s, NPRE, RING0)) if s < RING0 else 0 for s in range(RING)]

        def landed(eng, *name):
            n = index[name]
            eng.wait_ge(S(f"w_landed{n % RING0}"), 16 * (n // RING0 + 1))
            return at(slot[n % RING0], loads[n][2], loads[n][3])

        def chain(eng, name):
            count = [0]

            def link(ins):
                count[0] += 1
                ins.then_inc(S(name), 1)
                eng.wait_ge(S(name), count[0])
            return link

        STOP = {None: 99, "mod": 1, "hT": 2, "proj": 3, "attn": 4, "ln1": 5, "ffn": 6, "mod1": 7, "proj1": 8,
                "na": 9, "hgrn": 10, "ln3": 11, "route": 12}[stop]

        TMB = [0, 2 * NT, 4 * NT, 6 * NT, 6 * NT + 2 * NL]

        ADA1 = [(12, 12), (12, 16), (16, 20), (20, 24)]
        TBANK = [4, 4, 0, 4]

        units = [(kind, h, t, 0 if t < NL else SEQ, TOK if t < NL else CTX)
                 for kind in "ab" for h in range(HEADS) for t in range(NT)]
        scale_of = {"a": HD ** -0.5, "b": QKB ** -0.5}
        NU = len(units)
        units1 = [("n", h, t, 0, TOK) for h in range(HEADS) for t in range(NL)]
        scale_of["n"] = 1.0
        NU1 = len(units1)
        levels = [(m, d) for m in [P] + LEVELS for d in range(2)]
        OPEN = 1

        def debug_taps():
            m = {"mod": [("mod", modT)], "hT": [("hT", hT)], "proj": [("qTa", qTa), ("kTa", kTa), ("qTb", at(ARENA + 3584, HEADS, TOK, parts=QKB)), ("kTb", at(ARENA + 7680, HEADS, TOK, parts=QKB)), ("vb", vb), ("va", va)],
                 "attn": [("o", oA)], "ln1": [("x", xr), ("hT", hT)], "ffn": [("x", xr), ("hT", hT)], "na": [("o", o1)], "hgrn": [("o", o1)],
                 "ln3": [("x", xr[:, NL:NT]), ("hT", hT[:, :, 0:SEQ])], "route": [("tab", at(RT, NL, NR)), ("tabg", at(RT + 24, NL, NR))]}
            return [(taps[n], v) for n, v in m[stop]]

        def ln_rows(sp, which):
            g, b = [(A["ln1_g"][0:1], A["ln1_b"][0:1]), (A["ln2_g"][0:1], A["ln2_b"][0:1]),
                    (A["ln1_g"][1:2], A["ln1_b"][1:2]), (A["ln2_g"][1:2], A["ln2_b"][1:2])][which]
            if which == 0:
                sp.wait_ge(S("tp_b"), 2 * HEADS)
            else:
                sp.wait_ge(S("x_ln"), (0, NT, NT + NL, NT + 2 * NL)[which])
            if which == 3:
                sp.wait_ge(S("gb_mm"), 12)
            if which == 2:
                sp.wait_ge(S("oT_t"), 2 * NT + 2 * NL)
            sp.dma_start(lnrow[:, 0, :], bc(g, P, D)).then_inc(S("lnrow_in"), 16)
            sp.dma_start(lnrow[:, 1, :], bc(b, P, D)).then_inc(S("lnrow_in"), 16)

        def layer1_loads(sp):
            sp.wait_ge(S("x_ln"), NT + NL)
            sp.dma_start(at(G, 1984), A["c_hg"]).then_inc(S("c1_in"), 16)
            sp.dma_start(onorm, bc(A["od_onorm_g"], P, P)).then_inc(S("c1_in"), 16)
            sp.dma_start(router, A["moe_router"][0].rearrange("(k p) e -> p k e", p=P)).then_inc(S("c1_in"), 16)

        def bias_loads(sp):
            sp.wait_ge(S("mod_t"), 24)
            table = A["rpb"]
            for h in range(HEADS):
                for r in range(ROWS):
                    t, rl = r // 2, r % 2
                    src = bass.AP(table.tensor, (h * (2 * NBR_ROWS - 1) + NBR_ROWS - 1 - r) * RPB_PW,
                                  [[1, GRID_W], [RPB_PW, ROWS], [1, GRID_W]])
                    dst = bias[rl * GRID_W:(rl + 1) * GRID_W, 2 * h + t, :].rearrange("p (i c) -> p i c", i=ROWS)
                    sp.dma_start(dst, src).then_inc(S("bias_in"), 16)

        def expert_load(sp, r, e, j, first=False):
            s = j % RING
            if not first:
                i = j - RING if j >= RING else j + 2 * RING
                rr = r if j >= RING else r - 1
                sp.wait_ge(S("unit_mm"), rr * UNITS + 4 * (i + 1) + HBUF)
            if j < 14:
                w = A[("moe_w_gate", "moe_w_up")[j % 2]][0]
                a = 512 * (j // 2)
                src = w[bass.ds(e, 1), :, a:a + 512].rearrange("o (k p) n -> p (o k) n", p=P)
                dst = at(slot[s], DK, 512)
            else:
                k = 4 * (j - 14)
                src = A["moe_w_down"][0][bass.ds(e, 1), k * P:(k + 4) * P, :].rearrange("o (k p) n -> p (o k) n", p=P)
                dst = at(slot[s], 4, D)
            sp.dma_start(dst, src).then_inc(S(f"w_landed{s}"), 16)

        def experts_loads(sp):
            last = {n % RING0: n for n in range(NPRE)}
            for j in range(21):
                if j < RING:
                    if j < RING0:
                        sp.wait_ge(S(loads[last[j]][4][0]), loads[last[j]][4][1])
                    else:
                        sp.wait_ge(S("y_mm"), 2 * NT + NL)
                    expert_load(sp, 0, 0, j, first=True)
                else:
                    expert_load(sp, 0, 0, j)
            with sp.Fori(1, NE) as r:
                for j in range(21):
                    expert_load(sp, r, r, j)
            sp.wait_ge(S("routed"), 1)
            many = sp.value_load(nover[0:1, :], min_val=0, max_val=EXTRA)
            with sp.If(many > 0):
                with sp.Fori(NE, ROUNDS) as r:
                    e = sp.value_load(ids[0:1, bass.ds(r, 1)], min_val=0, max_val=NE - 1)
                    for j in range(21):
                        expert_load(sp, r, e, j)

        block = es.enter_context(nc.Block())

        @block.sync
        def _(sp):
            def small_loads():
                sp.dma_start(at(base_c, 640), A["c_base"]).then_inc(S("c_in"), 16)
                for d, s in ((vr1[0:96, :], A["vr1"]), (vr2[0:88, :], A["vr2"])):
                    sp.dma_start(d, s).then_inc(S("c_in"), 16)
                sp.dma_start(xr[:, 0:NL, :], A["x"][0].rearrange("(t p) d -> p t d", p=P)).then_inc(S("x_in"), 16)
                sp.dma_start(xr[:, NL:NT, :], A["ctx"][0].rearrange("(t p) d -> p t d", p=P)).then_inc(S("x_in"), 16)
                sp.dma_start(rope_c, A["c_rope"].rearrange("(t p) d -> p t d", p=P)).then_inc(S("g_in"), 16)
                sp.dma_start(gains[:, 0:8, :], bc(A["ev_qn_g"].unsqueeze(1), P, 8, HD)).then_inc(S("g_in"), 16)
                sp.dma_start(gains[:, 8:10, :], bc(A["ev_kn_g"].unsqueeze(1), P, 2, HD)).then_inc(S("g_in"), 16)
                sp.dma_start(cqg, bc(A["ev_cq_g"], P, QR)).then_inc(S("g_in"), 16)
                sp.dma_start(ckvg, bc(A["ev_ckv_g"], P, KVR)).then_inc(S("g_in"), 16)
            small_loads()

            def load(n):
                if n >= RING0:
                    sem, value = loads[n - RING0][4]
                    sp.wait_ge(S(sem), value)
                _, src, a, b, _ = loads[n]
                sp.dma_start(at(slot[n % RING0], a, b), src).then_inc(S(f"w_landed{n % RING0}"), 16)
            last = {1: ("ada", 0, 11), 2: ("ada", 0, 11), 3: ("ukv",), 4: ("ukv",), 5: ("evout", 1), 6: ("fd", 20),
                    7: ("fd", 20), 8: ("odin", 7), 9: ("odin", 7), 10: ("odin", 7)}.get(STOP)
            NLOAD = NPRE if last is None else index[last] + 1
            for n in range(NLOAD):
                load(n)
                if loads[n][0] == ("evout", 1):
                    ln_rows(sp, 0)
                if loads[n][0] == ("fd", 20):
                    ln_rows(sp, 1)
                    if STOP >= 8:
                        bias_loads(sp)
                        layer1_loads(sp)
            if STOP >= 11:
                ln_rows(sp, 2)
            if STOP >= 99:
                experts_loads(sp)
                ln_rows(sp, 3)
                for t in range(NL):
                    sp.wait_ge(S("x_ln"), NT + 2 * NL + t + 1)
                    sp.dma_start(out[0, t * P:t * P + P, :], xr[:, NL + t, :]).then_inc(S("out_done"), 16)
                sp.wait_ge(S("out_done"), 16 * NL)
            if STOP < 99:
                dve_end = S("dbg_go")
                sp.wait_ge(dve_end, 3)
                for i, (dst, view) in enumerate(debug_taps()):
                    sp.dma_start(dst, view).then_inc(S("dbg_out"), 16)
                sp.wait_ge(S("dbg_out"), 16 * len(debug_taps()))

        @block.tensor
        def _(pe):
            mm = nc.tensor.matmul
            tp = nc.tensor.transpose

            def setup():
                pe.wait_ge(S("c_in"), 48)
                tp(pb[4][:, 0:96], vr1[0:96, :], ident[0:96, 0:96])
                tp(pb[5][:, 0:88], vr2[0:88, :], ident[0:88, 0:88]).then_inc(S("vec_t"), 1)
                pe.wait_ge(S("silu_c"), 1)

            def ada(L):
                sv = sT.rearrange("p (s k) -> p s k", s=2)
                B = 4 * L
                if L == 1:
                    pe.wait_ge(S("gb_c"), 4)
                for i in range(12 * L, 12 * L + 13):
                    if i < 12 * L + 12:
                        w = landed(pe, "ada", L, i - 12 * L)
                        if i >= 2:
                            pe.wait_ge(S("mod_row"), i - 1)
                        for k in range(DK):
                            ins = mm(pb[B + i % 2][0:2, :], sv[:, :, k], w[:, k, :], start=(k == 0), stop=(k == DK - 1))
                        ins.then_inc(S("mod_mm"), 1)
                    i -= 1
                    if i >= 12 * L:
                        pe.wait_ge(S("mod_row"), i + 1)
                        if i >= 2:
                            pe.wait_ge(S("mod_col"), i - 1)
                        for q in range(4):
                            ins = tp(pb[B + 2 + i % 2][:, 2 * q:2 * q + 2], rowbuf[0:2, i % 2, q * P:q * P + P],
                                     ident[0:2, 0:2])
                        ins.then_inc(S("mod_t"), 1)

            def transpose_in(n, tiles):
                for t in range(tiles):
                    if n > 0:
                        pe.wait_ge(S("x_hat"), (0, 0, NT, 2 * NT)[n] + t + 1)
                    for half in range(2):
                        g = TMB[n] + 2 * t + half
                        b = TBANK[n] + g % 2
                        if g >= 2:
                            pe.wait_ge(S("hT_half"), g - 1)
                        if n == 0 and g < 2:
                            pe.wait_ge(S("vec_c"), 2)
                        for q in range(4):
                            k = 4 * half + q
                            ins = tp(pb[b][:, q * P:q * P + P], xr[:, t, k * P:k * P + P], ident)
                        ins.then_inc(S("tm_t"), 1)

            def proj0():
                pe.wait_ge(S("hT_half"), TMB[1])
                g = 0
                for a, b in EVC:
                    w = landed(pe, "evin", a)
                    for t in range(NT):
                        if g >= 2:
                            pe.wait_ge(S("proj_c"), g - 1)
                        for k in range(DK):
                            ins = mm(pb[g % 2][:, 0:b - a], hT[:, k, t * P:t * P + P], w[:, k, :],
                                     start=(k == 0), stop=(k == DK - 1))
                        ins.then_inc(S("proj_mm"), 1)
                        g += 1
                    

            def heads0():
                pe.wait_ge(S("proj_c"), 3 * NT)
                wq = landed(pe, "uq")
                wkv = landed(pe, "ukv")
                for t in range(NT):
                    pe.wait_ge(S("qk_n"), t + 1)
                    if t:
                        pe.wait_ge(S("heads_c"), 5 * t)
                    for h in range(4):
                        ins = tp(pb[2][:, h * P:h * P + P], proj[:, t, h * P:h * P + P], ident)
                    ins.then_inc(S("tp_a"), 1)
                    for i in range(2):
                        tp(pb[3][:, i * P:i * P + P], kdup[:, i].rearrange("p a e -> p (a e)"), ident)
                    for i in range(2):
                        tp(pb[3][:, (2 + i) * P:(3 + i) * P], proj[:, t, 768 + i * P:768 + i * P + P], ident)
                    for i in range(3):
                        ins = tp(pb[4][:, i * P:i * P + P], proj[:, t, 1024 + i * P:1024 + i * P + P], ident)
                    ins.then_inc(S("tp_a"), 1)
                    pe.wait_ge(S("lat_c"), 3 * (t + 1))
                    for c in range(2):
                        for k in range(3):
                            ins = mm(pb[5 + c][:, 0:384], latT[:, k, :], wq[:, k, c * 384:c * 384 + 384],
                                     start=(k == 0), stop=(k == 2))
                    ins.then_inc(S("up_mm"), 1)
                    for c in range(2):
                        for k in range(2):
                            ins = mm(pb[(7, 0)[c]][:, :], latT[:, 3 + k, :], wkv[:, k, c * 512:c * 512 + 512],
                                     start=(k == 0), stop=(k == 1))
                    ins.then_inc(S("up_mm"), 1)
                    pe.wait_ge(S("heads_c"), 5 * t + 1)
                    pe.wait_ge(S("qb_r"), t + 1)
                    for h in range(HEADS):
                        ins = tp(pb[2 + h // 4][0:QKB, (h % 4) * P:(h % 4) * P + P], qbt[:, t % 2, h, :], ident)
                        if h % 4 == 3:
                            ins.then_inc(S("tp_b"), 1)
                    pe.wait_ge(S("kb_r"), t + 1)
                    for h in range(HEADS):
                        ins = tp(pb[(4, 1)[h // 4]][0:QKB, (h % 4) * P:(h % 4) * P + P], kbt[:, t % 2, h, :], ident)
                        if h % 4 == 3:
                            ins.then_inc(S("tp_b"), 1)

            def attention(units, base, p_sb, pT_sb):
                n = len(units)
                for u in range(base, base + n + 2):
                    if u < base + n:
                        kind, h, t, k0, nk = units[u - base]
                        if u >= 2:
                            pe.wait_ge(S("p_exp"), u - 1)
                        if kind == "a":
                            o = HD * (h % 2)
                            q, k = qTa[o:o + HD, h // 2, t * P:t * P + P], kTa[o:o + HD, h // 4, k0:k0 + nk]
                        elif kind == "b":
                            q, k = qTb[0:QKB, h, t * P:t * P + P], kTb[0:QKB, h, k0:k0 + nk]
                        else:
                            o = HD * (h % 2)
                            q, k = qnT[o:o + HD, h // 2, t * P:t * P + P], knT[o:o + HD, h // 2, :]
                        ins = mm(pb[u % 2][:, 0:nk], q, k, start=True, stop=(kind != "n"))
                        if kind == "n":
                            ins = mm(pb[u % 2][:, 0:SEQ], flip, bias[:, 2 * h + t, :], start=False, stop=True)
                        ins.then_inc(S("s_mm"), 1)
                    if base + 1 <= u <= base + n:
                        v = u - 1
                        _, h, t, k0, nk = units[v - base]
                        pe.wait_ge(S("p_exp"), v + 1)
                        if v >= 2:
                            pe.wait_ge(S("pT_c"), v - 1)
                        for i in range(nk // P):
                            ins = tp(pb[2 + v % 2][:, i * P:i * P + P], p_sb[:, v % 2, i * P:i * P + P], ident)
                        ins.then_inc(S("p_t"), 1)
                    if u >= base + 2:
                        v = u - 2
                        kind, h, t, k0, nk = units[v - base]
                        pe.wait_ge(S("pT_c"), v + 1)
                        if v >= 2:
                            pe.wait_ge(S("o_c"), v - 1)
                        for i in range(nk // P):
                            kt = k0 // P + i
                            o = HD * (h // 4)
                            val = va[:, kt, o:o + HD] if kind == "a" else (vb if kind == "b" else vn)[:, kt, h * HD:h * HD + HD]
                            ins = mm(pb[4 + v % 2][:, 0:HD], pT_sb[:, v % 2, i * P:i * P + P], val,
                                     start=(i == 0), stop=(i == nk // P - 1))
                        ins.then_inc(S("o_mm"), 1)

            def out_t(tiles, src, dst_sem, done, base):
                pe.wait_ge(S(done[0]), done[1])
                for t in range(tiles):
                    for half in range(2):
                        g = base + 2 * t + half
                        if g >= 2:
                            pe.wait_ge(S("oT_c"), g - 1)
                        for q in range(4):
                            k = 4 * half + q
                            ins = tp(pb[6 + g % 2][:, q * P:q * P + P], src[:, t, k * P:k * P + P], ident)
                        ins.then_inc(S("oT_t"), 1)

            def gates(L, which, streams, n):
                for s in range(streams):
                    for half in range(2):
                        g = n + 2 * s + half
                        pe.wait_ge(S("dg"), g + 1)
                        if g >= 2:
                            pe.wait_ge(S("gb_c"), g - 1)
                        mm(pb[6 + g % 2][:, :], ones, diag[:, g % 2, :], start=True, stop=True).then_inc(S("gb_mm"), 1)

            def out_proj(name, tiles, src, base, ready):
                w = [landed(pe, name, c) for c in range(2)]
                pe.wait_ge(S(ready[0]), ready[1])
                for t in range(tiles):
                    if t >= 2:
                        pe.wait_ge(S("y_c"), base + t - 1)
                    for c in range(2):
                        for k in range(DK):
                            ins = mm(pb[2 * (t % 2) + c][:, :], src[:, k, t * P:t * P + P], w[c][:, k, :],
                                     start=(k == 0), stop=(k == DK - 1))
                    ins.then_inc(S("y_mm"), 1)

            def ffn0():
                pe.wait_ge(S("hT_half"), TMB[2])
                g = 0
                for a, b in FC:
                    wg, wu = landed(pe, "fg", a), landed(pe, "fu", a)
                    for f in range((b - a) // P):
                        if g >= 2:
                            pe.wait_ge(S("ff_a"), g - 1)
                        for w, o in ((wg, 0), (wu, 2)):
                            for k in range(DK):
                                ins = mm(pb[o + g % 2][:, :], w[:, k, f * P:f * P + P], hT[:, k, :],
                                         start=(k == 0), stop=(k == DK - 1))
                        ins.then_inc(S("ff_mm"), 1)
                        g += 1
                for a, b in FD:
                    w = landed(pe, "fd", a)
                    if a == 0:
                        pe.wait_ge(S("ff_a"), FK)
                        pe.wait_ge(S("gb_c"), 8)
                    for k in range(a, b):
                        for t in range(NT):
                            for c in range(2):
                                ins = mm(pb[2 * t + c][:, :], aT0[:, k, t * P:t * P + P],
                                         w[:, k - a, c * 512:c * 512 + 512], start=(k == 0), stop=(k == FK - 1))
                                if k == FK - 1 and c == 1:
                                    ins.then_inc(S("y_mm"), 1)
                                elif k == b - 1 and t == NT - 1 and c == 1:
                                    ins.then_inc(S("fd_mm"), 1)

            def proj1():
                pe.wait_ge(S("hT_half"), TMB[3])
                for g, (c, i) in enumerate(in1):
                    if g >= 4:
                        pe.wait_ge(S("in1_c"), g - 3)
                    w = landed(pe, "odin", c)
                    for k in range(DK):
                        if c in (2, 4, 7):
                            a, b, n = hT[:, k, i * P:i * P + P], w[:, k, :], 512
                        else:
                            n = SEQ if c in (0, 3) else TOK
                            a, b = w[:, k, i * P:i * P + P], hT[:, k, 0:n]
                        ins = mm(pb[g % 4][:, 0:n], a, b, start=(k == 0), stop=(k == DK - 1))
                    ins.then_inc(S("in1_mm"), 1)

            def hgrn():
                for d in range(2):
                    pe.wait_ge(S("kend"), d + 1)
                    pe.wait_ge(S("o_c"), NU + NU1)
                    if d:
                        pe.wait_ge(S("kend_c"), 2)
                        pe.wait_ge(S("state_c"), 1)
                    for i in range(2):
                        for h in range(HGH):
                            ins = tp(pb[i][:, h * P:h * P + P], W[d][:, h, i * P:i * P + P], ident)
                        ins.then_inc(S("kend_t"), 1)
                    pe.wait_ge(S("kend_c"), 2 * d + 2)
                    for h in range(HGH):
                        for i in range(2):
                            ins = mm(pb[2][:, h * P:h * P + P], kendT[:, i, h, :], vd[:, NL + i, h * P:h * P + P],
                                     start=(i == 0), stop=(i == 1))
                    ins.then_inc(S("state_mm"), 1)
                pe.wait_ge(S("ksum"), 1)
                for i in range(NL):
                    for h in range(HGH):
                        c = slice(i * P, i * P + P)
                        ins = mm(pb[4 + i][:, h * P:h * P + P], ksum[:, h, c], qd[:, h, c], start=True, stop=True)
                ins.then_inc(S("same_mm"), 1)
                pe.wait_ge(S("state_c"), 2)
                for n, (m, d) in enumerate(levels):
                    pe.wait_ge(S("hg_w"), n + 1)
                    if n >= 2:
                        pe.wait_ge(S("hg_at"), n - 1)
                    for i in range(1 if m == P else NL):
                        for h in range(HGH):
                            w = W[n % 2][:, h]
                            if m == P:
                                a, b = (w[:, 0:P], w[:, P:SEQ]) if d == 0 else (w[:, P:SEQ], w[:, 0:P])
                            else:
                                a = b = w[:, i * P:i * P + P]
                            ins = mm(pb[2 * (n % 2) + i][:, h * P:h * P + P], a, b, start=True, stop=True)
                    ins.then_inc(S("hg_mm"), 1)
                pe.wait_ge(S("hg_at"), len(levels))
                pe.wait_ge(S("qx"), 2)
                for t in range(NL):
                    c = slice(t * P, t * P + P)
                    for h in range(HGH):
                        f = slice(h * P, h * P + P)
                        terms = [(AT[:, i, h, c], vd[:, i, f]) for i in range(NL)]
                        terms += [(qxf[:, h, c], state[:, 0, h, :]), (qxb[:, h, c], state[:, 1, h, :])]
                        for i, (a, b) in enumerate(terms):
                            ins = mm(pb[6 + t][:, f], a, b, start=(i == 0), stop=(i == 3))
                    ins.then_inc(S("hg_o"), 1)

            def route():
                pe.wait_ge(S("hT_half"), TMB[4])
                pe.wait_ge(S("c1_in"), 48)
                pe.wait_ge(S("gb_c"), 10)
                for t in range(NL):
                    for k in range(DK):
                        ins = mm(pb[6][:, t * NE:t * NE + NE], hT[:, k, t * P:t * P + P], router[:, k, :],
                                 start=(k == 0), stop=(k == DK - 1))
                ins.then_inc(S("logit_mm"), 1)
                pe.wait_ge(S("mask_r"), 1)
                m = rt[5]
                mm(pb[7][:, 0:8], upper, m[:, 0, :], start=True, stop=True)
                mm(pb[7][:, 8:16], upper, m[:, 1, :], start=True, stop=False)
                mm(pb[7][:, 8:16], ones, m[:, 0, :], start=False, stop=True)
                mm(pb[7][:, 16:24], ones, m[:, 0, :], start=True, stop=False)
                mm(pb[7][:, 16:24], ones, m[:, 1, :], start=False, stop=True).then_inc(S("pos_mm"), 1)

            def gather_half(r, half):
                pe.wait_ge(S("sel_r"), r + 1)
                if not (isinstance(r, int) and r == 0 and half == 0):
                    pe.wait_ge(S("bank7"), r * 3 + half)
                for q in range(4):
                    k = 4 * half + q
                    for t in range(NL):
                        ins = mm(pb[7][:, q * P:q * P + P], xr[:, t, k * P:k * P + P], sel[:, t, :],
                                 start=(t == 0), stop=(t == NL - 1))
                ins.then_inc(S("g_mm"), 1)

            def scatter(r, n, t):
                pe.wait_ge(S("y_s"), 2 * n + 2)
                pe.wait_ge(S("bank7"), r * 3 + 2)
                if t:
                    pe.wait_ge(S("sc_a"), 4 * n + 2)
                for c in range(2):
                    mm(pb[4 + c][:, :], selGT[:, t * P:t * P + P], y_e[:, 512 * c:512 * c + 512],
                       start=True, stop=True).then_inc(S("sc_mm"), 1)

            def expert(r, n):
                def split_mm(bank, hs, w, lo, first, last):
                    mm(bank, hs[0], w, start=first, stop=False)
                    mm(bank, hs[0], lo, start=False, stop=False)
                    return mm(bank, hs[1], w, start=False, stop=last)

                def unit(j, q):
                    u = 4 * j + q
                    if q == POOLQ:
                        pe.wait_ge(S("w_lo_g"), r * 21 + j + 1)
                    else:
                        pe.wait_ge(S("w_lo"), r * 63 + 3 * j + q - (q > POOLQ) + 1)
                    return wH[u % HBUF], part(slot[j % RING] + UNIT * q, UNIT)

                def transposed(c):
                    pe.wait_ge(S("e_a"), r * 7 + c + 1 + OPEN)
                    pe.wait_ge(S("e_aT"), r * 7 + c + OPEN)
                    for q in range(4):
                        ins = tp(pb[6][:, q * P:q * P + P], s_e[:, c % 2, q * P:q * P + P], ident)
                    ins.then_inc(S("e_t"), 1)

                pe.wait_ge(S("hs_r"), r + 1)
                for c in range(7):
                    pe.wait_ge(S("e_a"), r * 7 + max(c - 1, 0) + OPEN)
                    for i in range(2):
                        for q in range(4):
                            h, l = unit(2 * c + i, q)
                            for k in range(2):
                                f = slice(512 * k, 512 * k + 512)
                                kk = 2 * q + k
                                ins = split_mm(pb[2 * i + c % 2][:, :], (hsH[:, kk, :], hsL[:, kk, :]), h[:, f], l[:, f],
                                               kk == 0, kk == DK - 1)
                            ins.then_inc(S("unit_mm"), 1)
                    if c < 2:
                        scatter(r, n, c)
                    if c >= 1:
                        transposed(c - 1)
                    if c == 2:
                        pe.wait_ge(S("selg"), r + 1)
                        pe.wait_ge(S("bank7"), r * 3 + 2)
                        for t in range(NL):
                            ins = tp(pb[7][:, t * P:t * P + P], selG[:, t, :], ident)
                        ins.then_inc(S("sg_t"), 1)
                    if c == 3:
                        gather_half(r + 1, 0)
                    if c == 4:
                        gather_half(r + 1, 1)
                pe.wait_ge(S("sc_a"), 4 * n + 4)
                for d in range(7):
                    pe.wait_ge(S("e_aT"), r * 7 + d + 1 + OPEN)
                    for q in range(4):
                        h, l = unit(14 + d, q)
                        for c in range(2):
                            f = slice(512 * c, 512 * c + 512)
                            k = 4 * d + q
                            ins = split_mm(pb[4 + c][:, :], (aH[:, k, :], aL[:, k, :]), h[:, f], l[:, f],
                                           k == 0, k == EK - 1)
                        ins.then_inc(S("unit_mm"), 1)
                    if d == 1:
                        transposed(6)

            setup()
            ada(0)
            if STOP >= 2:
                transpose_in(0, NT)
            if STOP >= 3:
                proj0()
                heads0()
            if STOP >= 4:
                pe.wait_ge(S("heads_c"), 5 * NT)
                attention(units, 0, p_sb, pT_sb)
            if STOP >= 5:
                out_t(NT, oA, None, ("o_c", NU), 0)
                pe.wait_ge(S("oT_c"), 2 * NT)
                gates(0, 0, 2, 0)
                out_proj("evout", NT, oT, 0, ("oT_c", 2 * NT))
                ada(1)
                pe.wait_ge(S("mod_row"), 24)
                transpose_in(1, NT)
            if STOP >= 6:
                gates(0, 1, 2, 4)
                ffn0()
                transpose_in(2, NT)
            if STOP >= 8:
                proj1()
            if STOP >= 9:
                pe.wait_ge(S("in1_c"), len(in1))
                pe.wait_ge(S("bias_r"), 1)
                attention(units1, NU, p1, pT1)
            if STOP >= 10:
                hgrn()
            if STOP >= 11:
                out_t(NL, o1, None, ("y_hg", NL), 2 * NT)
                pe.wait_ge(S("oT_c"), 2 * NT + 2 * NL)
                gates(1, 2, 1, 8)
                out_proj("odout", NL, oT1, 2 * NT, ("oT_c", 2 * NT + 2 * NL))
                transpose_in(3, NL)
            if STOP >= 12:
                route()
            if STOP >= 99:
                pe.wait_ge(S("mask_r"), 1)
                pe.wait_ge(S("routed"), 1)
                gather_half(0, 0)
                gather_half(0, 1)
                for name in ("sg_t", "e_t"):
                    pe.sem_inc(S(name), OPEN)
                pe.sem_inc(S("unit_mm"), HBUF)
                with pe.Fori(0, NE) as r:
                    expert(r, r)
                for t in range(NL):
                    scatter(NE, NE, t)
                pe.wait_ge(S("routed"), 1)
                many = pe.value_load(nover[0:1, :], min_val=0, max_val=EXTRA)
                with pe.If(many > 0):
                    with pe.Fori(NE, ROUNDS) as r:
                        expert(r, r + 1)
                    for t in range(NL):
                        scatter(ROUNDS, ROUNDS + 1, t)
                gates(1, 5, 1, 10)

        @block.scalar
        def _(act):
            link = chain(act, "act_done")
            fn = nc.scalar.activation

            def copy(out_, in_):
                return fn(out_, in_, ACT.Copy)

            def setup():
                act.wait_ge(S("vec_c"), 1)
                fn(sT, vcol[:, 64:80], ACT.Silu).then_inc(S("silu_c"), 1)

            def ada(first, last):
                for i in range(first, last):
                    act.wait_ge(S("mod_mm"), i + 1)
                    if i >= 2:
                        act.wait_ge(S("mod_t"), i - 1)
                    copy(rowbuf[0:2, i % 2, :], pb[4 * (i // 12) + i % 2][0:2, :]).then_inc(S("mod_row"), 1)

            def modulate(n, tiles):
                for t in range(tiles):
                    s = t // NL
                    for half in range(2):
                        g = TMB[n] + 2 * t + half
                        act.wait_ge(S("tm_t"), g + 1)
                        if n == 0:
                            act.wait_ge(S("mod_col"), 4)
                        else:
                            act.wait_ge(S("ab_r"), n)
                        for q in range(4):
                            k = 4 * half + q
                            if n == 0:
                                a, b = modT[:, 0, 8 + k, s:s + 1], modT[:, 0, k, s:s + 1]
                            else:
                                a, b = (AB[:, n - 1, i, 2 * k + s:2 * k + s + 1] for i in range(2))
                            ins = fn(hT[:, k, t * P:t * P + P], pb[TBANK[n] + g % 2][:, q * P:q * P + P], ACT.Identity,
                                     bias=b, scale=a)
                        ins.then_inc(S("hT_half"), 1)

            def proj0():
                g = 0
                for a, b in EVC:
                    for t in range(NT):
                        act.wait_ge(S("proj_mm"), g + 1)
                        copy(proj[:, t, a:b], pb[g % 2][:, 0:b - a]).then_inc(S("proj_c"), 1)
                        g += 1
                act.wait_ge(S("proj_c"), 3 * NT)
                for t in range(NT):
                    copy(va[:, t, :], proj[:, t, 640:768]).then_inc(S("va_c"), 1)

            def heads0():
                for t in range(NT):
                    act.wait_ge(S("ssq"), t + 1)
                    fn(ssq[:, t, 0:12], ssq[:, t, 0:12], ACT.Sqrt).then_inc(S("rms"), 1)
                for t in range(NT):
                    tile = slice(t * P, t * P + P)
                    act.wait_ge(S("tp_a"), 2 * t + 1)
                    copy(qTa[:, :, tile], pb[2].rearrange("p (h c) -> p h c", h=4)).then_inc(S("heads_c"), 1)
                    act.wait_ge(S("up_mm"), 2 * t + 1)
                    for c in range(2):
                        copy(qbt[:, t % 2, 4 * c:4 * c + 4, :], pb[5 + c][:, 0:384].rearrange("p (h c) -> p h c", h=4))\
                            .then_inc(S("qb_c"), 1)
                    act.wait_ge(S("up_mm"), 2 * t + 2)
                    for c in range(2):
                        bank = pb[(7, 0)[c]].rearrange("p (h c) -> p h c", h=4)
                        copy(kbt[:, t % 2, 4 * c:4 * c + 4, 0:NOPE], bank[:, :, 0:NOPE]).then_inc(S("kb_c"), 1)
                        copy(vb[:, t, 256 * c:256 * c + 256].rearrange("p (h c) -> p h c", h=4), bank[:, :, NOPE:])\
                            .then_inc(S("kb_c"), 1)
                    for c, (b, dst) in enumerate(((2, qTb), (3, qTb), (4, kTb), (1, kTb))):
                        act.wait_ge(S("tp_b"), 4 * t + c + 1)
                        h = 4 * (c % 2)
                        copy(dst[0:QKB, h:h + 4, tile], pb[b][0:QKB, :].rearrange("p (h c) -> p h c", h=4))\
                            .then_inc(S("heads_c"), 1)

            def attention(units, base, p_sb, pT_sb):
                n = len(units)
                for u in range(n + 1):
                    g = base + u
                    if u < n:
                        act.wait_ge(S("mx_r"), g + 1)
                        if u >= 2:
                            act.wait_ge(S("p_t"), g - 1)
                        nk = units[u][4]
                        fn(p_sb[:, g % 2, 0:nk], pb[g % 2][:, 0:nk], ACT.Exp, bias=mx[:, g % 4, 1:2],
                           scale=scale_of[units[u][0]], accum_out=mx[:, g % 4, 2:3]).then_inc(S("p_exp"), 1)
                    if u >= 1:
                        v = g - 1
                        act.wait_ge(S("p_t"), v + 1)
                        if u >= 3:
                            act.wait_ge(S("o_mm"), v - 1)
                        nk = units[u - 1][4]
                        copy(pT_sb[:, v % 2, 0:nk], pb[2 + v % 2][:, 0:nk]).then_inc(S("pT_c"), 1)

            def out_t(tiles, dst, base):
                for t in range(tiles):
                    for half in range(2):
                        g = base + 2 * t + half
                        act.wait_ge(S("oT_t"), g + 1)
                        copy(dst[:, 4 * half:4 * half + 4, t * P:t * P + P],
                             pb[6 + g % 2].rearrange("p (k c) -> p k c", k=4)).then_inc(S("oT_c"), 1)

            def gates(streams, n, y_read):
                if y_read:
                    act.wait_ge(S("y_c"), y_read)
                for g in range(n, n + 2 * streams):
                    s, half = (g - n) // 2, g % 2
                    act.wait_ge(S("gb_mm"), g + 1)
                    copy(gb[:, s, 512 * half:512 * half + 512], pb[6 + g % 2][:, :]).then_inc(S("gb_c"), 1)

            def root(base, t):
                act.wait_ge(S("var_r"), base + t + 1)
                fn(lnst[:, t, 14:15], lnst[:, t, 13:14], ACT.Sqrt, bias=eps_c).then_inc(S("std_r"), 1)

            def ffn0():
                for g in range(FK):
                    act.wait_ge(S("ff_mm"), g + 1)
                    if g >= 2:
                        act.wait_ge(S("ff_a"), g - 1)
                    fn(sil[:, g % 2, :], pb[g % 2][:, :], ACT.Silu).then_inc(S("ff_s"), 1)

            def lower_bound():
                act.wait_ge(S("lb_s"), 1)
                fn(lbs[:, 0], lbs[:, 0], ACT.Exp).then_inc(S("lb_e"), 1)

            def proj1():
                for g, (c, i) in enumerate(in1):
                    act.wait_ge(S("in1_mm"), g + 1)
                    b = pb[g % 4]
                    if c == 0:
                        ins = fn(qnT[:, i, :], b[:, 0:SEQ], ACT.Copy, scale=HD ** -0.5)
                    elif c == 1:
                        ins = copy(knT[:, i, :], b[:, :])
                    elif c == 2:
                        ins = copy(vn[:, i, :], b[:, :])
                    elif c == 3:
                        ins = fn(qd[:, i, :], b[:, 0:SEQ], ACT.Silu)
                    elif c == 4:
                        ins = copy(vd[:, i, :], b[:, :])
                    elif c == 7:
                        ins = fn(gd[:, i, :], b[:, :], ACT.Silu)
                    else:
                        d = c - 5
                        if d == 1 and i == 0:
                            act.wait_ge(S("cum_r"), 1)
                        fn((kf, kb)[d][:, i, :], b[:, :], ACT.Sigmoid, scale=-1.0).then_inc(S("sig"), 1)
                        fn(forget[:, i, :], b[:, :], ACT.Sigmoid).then_inc(S("sig"), 1)
                        ins = None
                    if ins is None:
                        act.wait_ge(S("sig"), 8 * (c - 5) + 2 * i + 2)
                        act.sem_inc(S("in1_c"), 1)
                        if i == 3:
                            act.wait_ge(S("f_r"), c - 4)
                            fn(forget, forget, ACT.Ln).then_inc(S("ln_f"), 1)
                    else:
                        ins.then_inc(S("in1_c"), 1)

            def hgrn():
                act.wait_ge(S("cum_r"), 2)
                for h in range(HGH):
                    c = cum[0][:, 1, h]
                    ins = fn(W[0][:, h, :], c[:, 1:CW], ACT.Exp, bias=c[:, SEQ:CW], scale=-1.0)
                ins.then_inc(S("kend_e"), 1)
                fn(W[1], cum[1][:, 1, :, 0:SEQ], ACT.Exp).then_inc(S("kend_e"), 1)
                act.wait_ge(S("o_c"), NU + NU1)
                fn(qxf, cum[0][:, 0, :, 1:CW], ACT.Exp).then_inc(S("qx_e"), 1)
                for h in range(HGH):
                    c = cum[1][:, 0, h]
                    ins = fn(qxb[:, h, :], c[:, 0:SEQ], ACT.Exp, bias=c[:, SEQ:CW], scale=-1.0)
                ins.then_inc(S("qx_e"), 1)
                for d in range(2):
                    for i in range(2):
                        act.wait_ge(S("kend_t"), 2 * d + i + 1)
                        if d:
                            act.wait_ge(S("state_mm"), 1)
                        copy(kendT[:, i].rearrange("p h c -> p (h c)"), pb[i][:, :]).then_inc(S("kend_c"), 1)
                    act.wait_ge(S("state_mm"), d + 1)
                    copy(state[:, d].rearrange("p h c -> p (h c)"), pb[2][:, :]).then_inc(S("state_c"), 1)
                for n, (m, d) in enumerate(levels):
                    act.wait_ge(S("hg_sub"), n + 1)
                    w = W[n % 2].rearrange("p h (b m) -> p (h b) m", m=2 * m)
                    for i, o in enumerate((slice(0, m), slice(m, 2 * m))):
                        ins = fn(w[:, :, o], w[:, :, o], ACT.Exp, scale=(-1.0, 1.0)[i])
                    ins.then_inc(S("hg_exp"), 1)
                for t in range(NL):
                    act.wait_ge(S("hg_ss"), t + 1)
                    fn(rms1[:, t, :], rms1[:, t, :], ACT.Sqrt).then_inc(S("hg_rt"), 1)

            def hs_copy(r, half, quarters=(0, 1, 2, 3)):
                if quarters[0] == 0:
                    act.wait_ge(S("g_mm"), r * 2 + half + 1)
                for q in quarters:
                    k = 4 * half + q
                    ins = fn(hsN[:, k, :], pb[7][:, q * P:q * P + P], ACT.Identity,
                             bias=AB[:, 2, 1, 2 * k:2 * k + 1], scale=AB[:, 2, 0, 2 * k:2 * k + 1])
                if quarters[-1] == 3:
                    ins.then_inc(S("bank7"), 1)

            def outputs(r):
                act.wait_ge(S("unit_mm"), r * UNITS + HBUF)
                act.wait_ge(S("hs_r"), r + 1)
                for c in range(2):
                    copy(y_e[:, 512 * c:512 * c + 512], pb[4 + c][:, :]).then_inc(S("y_s"), 1)

            def expert(r):
                for u in range(UNITS):
                    j, q = u // 4, u % 4
                    s = j % RING
                    if q == 0:
                        act.wait_ge(S(f"w_landed{s}"), r * 48 + 16 * (base_n[s] + j // RING + 1))
                    act.wait_ge(S("unit_mm"), r * UNITS + u + 1)
                    copy(wH[u % HBUF], at(slot[s] + UNIT * q, UNIT)).then_inc(S("w_hi"), 1)
                    if u == 3:
                        outputs(r)
                    c, step = (u - 12) // 8, (u - 12) % 8
                    if step == 0 and 0 <= c < 7:
                        act.wait_ge(S("unit_mm"), r * UNITS + 8 * c + 8 + HBUF)
                        act.wait_ge(S("e_t"), r * 7 + max(c - 1, 0) + OPEN)
                        fn(s_e[:, c % 2, :], pb[c % 2][:, :], ACT.Silu).then_inc(S("e_s"), 1)
                    if step == 2 and 1 <= c < 8:
                        act.wait_ge(S("e_t"), r * 7 + c + OPEN)
                        if c == 1:
                            act.wait_ge(S("unit_mm"), r * UNITS + HBUF)
                        copy(aH[:, 4 * c - 4:4 * c, :].rearrange("p k c -> p (k c)"), pb[6][:, :])\
                            .then_inc(S("e_aH"), 1)
                    if step == 1 and c == 2:
                        act.wait_ge(S("sg_t"), r + 1 + OPEN)
                        copy(selGT, pb[7][:, 0:SEQ]).then_inc(S("bank7"), 1)
                    if c in (3, 4) and step in (1, 3):
                        hs_copy(r + 1, c - 3, (0, 1) if step == 1 else (2, 3))
                    if step == 4 and c == 6:
                        act.wait_ge(S("bank7"), r * 3 + 5)
                        copy(hsH, hsN).then_inc(S("hs_h"), 1)

            setup()
            ada(0, 12)
            if STOP >= 2:
                modulate(0, NT)
            if STOP >= 3:
                proj0()
                heads0()
            if STOP >= 4:
                attention(units, 0, p_sb, pT_sb)
            if STOP >= 5:
                out_t(NT, oT, 0)
                gates(2, 0, 0)
                for t in range(NT):
                    root(0, t)
                    ada(*ADA1[t])
                modulate(1, NT)
            if STOP >= 6:
                gates(2, 4, NT)
                ffn0()
                for t in range(NT):
                    root(NT, t)
                modulate(2, NT)
            if STOP >= 8:
                lower_bound()
                proj1()
            if STOP >= 9:
                attention(units1, NU, p1, pT1)
            if STOP >= 10:
                hgrn()
            if STOP >= 11:
                out_t(NL, oT1, 2 * NT)
                gates(1, 8, 0)
                for t in range(NL):
                    root(2 * NT, t)
                modulate(3, NL)
            if STOP >= 12:
                act.wait_ge(S("top_r"), 1)
                fn(r1[:, 2, :], r1[:, 2, :], ACT.Exp).then_inc(S("top_e"), 1)
            if STOP >= 99:
                hs_copy(0, 0)
                hs_copy(0, 1)
                act.wait_ge(S("bank7"), 2)
                act.wait_ge(S("gb_mm"), 10)
                copy(hsH, hsN).then_inc(S("hs_h"), 1)
                act.wait_ge(S("logit_mm"), 1)
                act.wait_ge(S("y_zero"), 2)
                with act.Fori(0, NE) as r:
                    expert(r)
                outputs(NE)
                act.wait_ge(S("routed"), 1)
                many = act.value_load(nover[0:1, :], min_val=0, max_val=EXTRA)
                with act.If(many > 0):
                    act.wait_ge(S("y_zero"), 4)
                    with act.Fori(NE, ROUNDS) as r:
                        expert(r)
                    outputs(ROUNDS)
                gates(1, 10, 2 * NT + NL)
                for t in range(NL):
                    root(2 * NT + NL, t)
            if STOP < 99: fn(at(small + 400, 1), eps_c, ACT.Copy).then_inc(S("dbg_go"), 1)

        @block.vector
        def _(dve):
            link = chain(dve, "dve_done")
            v = nc.vector

            def setup():
                link(v.memset(eps_c, 1e-5 if False else 1e-6))
                dve.wait_ge(S("vec_t"), 1)
                v.tensor_copy(vcol, pb[5][:, 0:88]).then_inc(S("vec_c"), 1)
                link(v.tensor_copy(adab, pb[4][:, 0:96]))
                cols = adab.rearrange("p (l c k) -> p l c k", l=DEPTH, c=6)
                link(v.tensor_scalar(cols[:, :, 1], cols[:, :, 1], 1.0, None, ALU.add))
                v.tensor_scalar(cols[:, :, 4], cols[:, :, 4], 1.0, None, ALU.add).then_inc(S("vec_c"), 1)
                dve.wait_ge(S("vec_c"), 2)

            def ada(first, last):
                for i in range(first, last):
                    L, j = i // 12, i % 12
                    dve.wait_ge(S("mod_t"), i + 1)
                    v.tensor_tensor(modT[:, L, 4 * j:4 * j + 4, :],
                                    pb[4 * L + 2 + i % 2][:, 0:8].rearrange("p (c s) -> p c s", s=2),
                                    bc(adab[:, 48 * L + 4 * j:48 * L + 4 * j + 4].unsqueeze(2), P, 4, 2),
                                    ALU.add).then_inc(S("mod_col"), 1)

            def rope(x, n, rot, cos, sin, t1, t2):
                half = rot // 4
                link(v.tensor_tensor(t1, x, bc(cos.unsqueeze(1), P, n, rot), ALU.mult))
                xs = x.rearrange("p n (a b) -> p n a b", a=2)
                ts = t2.rearrange("p n (a b) -> p n a b", a=2)
                ss = sin.rearrange("p (a b) -> p a b", a=2)
                for i in range(2):
                    o, f = slice(i * half, i * half + half), slice((1 - i) * half, (1 - i) * half + half)
                    link(v.tensor_tensor(ts[:, :, :, o], xs[:, :, :, f], bc(ss[:, :, o].unsqueeze(1), P, n, 2, half),
                                         ALU.mult))
                return v.tensor_tensor(x, t1, t2, ALU.add)

            def heads0():
                dve.wait_ge(S("g_in"), 80)
                for t in range(NT):
                    pt = proj[:, t]
                    dve.wait_ge(S("proj_c"), 2 * NT + t + 1)
                    link(v.tensor_tensor(sqj, pt[:, 0:640], pt[:, 0:640], ALU.mult))
                    link(v.tensor_reduce(ssq[:, t, 0:10], sqj.rearrange("p (h e) -> p h e", e=HD), AX.X, ALU.add))
                    link(v.tensor_scalar(ssq[:, t, 0:10], ssq[:, t, 0:10], 1.0 / HD, 1e-6, ALU.mult, ALU.add))
                    for i, (a, n) in enumerate(((768, QR), (1152, KVR))):
                        c = ssq[:, t, 10 + i:11 + i]
                        link(v.tensor_tensor_reduce(sqj[:, 0:n], pt[:, a:a + n], pt[:, a:a + n], 1.0, 0.0, ALU.mult,
                                                    ALU.add, c))
                        ins = v.tensor_scalar(c, c, 1.0 / n, 1e-6, ALU.mult, ALU.add)
                        if i == 0:
                            link(ins)
                    ins.then_inc(S("ssq"), 1)
                for t in range(NT):
                    pt = proj[:, t]
                    r = ssq[:, t]
                    dve.wait_ge(S("rms"), t + 1)
                    link(v.reciprocal(r[:, 0:12], r[:, 0:12]))
                    qk = pt[:, 0:640].rearrange("p (h e) -> p h e", e=HD)
                    link(v.tensor_tensor(qk, qk, bc(r[:, 0:10].unsqueeze(2), P, 10, HD), ALU.mult))
                    link(v.tensor_tensor(qk, qk, gains, ALU.mult))
                    for i, (a, n, g) in enumerate(((768, QR, cqg), (1152, KVR, ckvg))):
                        link(v.scalar_tensor_tensor(out=pt[:, a:a + n], in0=pt[:, a:a + n],
                                                    scalar=r[:, 10 + i:11 + i], in1=g, op0=ALU.mult, op1=ALU.mult))
                    if t < NL:
                        t1, t2 = (x.rearrange("p (h e) -> p h e", e=HD) for x in (ropt[:, 0:640], sqj))
                        link(rope(qk, 10, HD, rope_c[:, t, 0:64], rope_c[:, t, 64:128], t1, t2))
                        link(rope(pt[:, 1408:1440].unsqueeze(1), 1, ROPE, rope_c[:, t, 128:160], rope_c[:, t, 160:192],
                                  ropt[:, 0:ROPE].unsqueeze(1), sqj[:, 0:ROPE].unsqueeze(1)))
                    v.tensor_copy(kdup, bc(pt[:, 512:640].rearrange("p (g e) -> p g e", g=KVH).unsqueeze(2), P, KVH, 2, HD))\
                        .then_inc(S("qk_n"), 1)
                    dve.wait_ge(S("tp_a"), 2 * t + 2)
                    v.tensor_copy(kTa[:, :, t * P:t * P + P], pb[3][:, 0:256].rearrange("p (k c) -> p k c", k=2))\
                        .then_inc(S("lat_c"), 1)
                    v.tensor_copy(latT[:, 0:2, :], pb[3][:, 256:512].rearrange("p (k c) -> p k c", k=2))\
                        .then_inc(S("lat_c"), 1)
                    v.tensor_copy(latT[:, 2:5, :], pb[4][:, 0:384].rearrange("p (k c) -> p k c", k=3))\
                        .then_inc(S("lat_c"), 1)
                    dve.wait_ge(S("qb_c"), 2 * t + 2)
                    if t < NL:
                        link(rope(qbt[:, t % 2, :, NOPE:], HEADS, ROPE, rope_c[:, t, 128:160], rope_c[:, t, 160:192],
                                  ropt[:, 0:256].rearrange("p (h e) -> p h e", h=HEADS),
                                  sqj[:, 0:256].rearrange("p (h e) -> p h e", h=HEADS)))
                    dve.sem_inc(S("qb_r"), 1)
                    link(v.tensor_copy(kbt[:, t % 2, :, NOPE:], bc(pt[:, 1408:1440].unsqueeze(1), P, HEADS, ROPE)))
                    dve.wait_ge(S("kb_c"), 4 * t + 4)
                    dve.sem_inc(S("kb_r"), 1)

            def attention(units, base, col):
                n = len(units)
                for u in range(n + 2):
                    g = base + u
                    if u < n:
                        nk = units[u][4]
                        dve.wait_ge(S("s_mm"), g + 1)
                        link(v.tensor_reduce(mx[:, g % 4, 0:1], pb[g % 2][:, 0:nk], AX.X, ALU.max))
                        v.tensor_scalar(mx[:, g % 4, 1:2], mx[:, g % 4, 0:1], -scale_of[units[u][0]], None, ALU.mult)\
                            .then_inc(S("mx_r"), 1)
                    if u >= 2:
                        w = g - 2
                        unit = units[u - 2]
                        dve.wait_ge(S("o_mm"), w + 1)
                        dve.wait_ge(S("p_exp"), w + 1)
                        link(v.reciprocal(mx[:, w % 4, 3:4], mx[:, w % 4, 2:3]))
                        v.tensor_scalar(col(unit), pb[4 + w % 2][:, 0:HD], mx[:, w % 4, 3:4], None, ALU.mult)\
                            .then_inc(S("o_c"), 1)

            def gates(L, chunk, streams, n):
                for g in range(n, n + 2 * streams):
                    s, half = (g - n) // 2, g % 2
                    if g - n >= 2:
                        dve.wait_ge(S("gb_mm"), g - 1)
                    col = modT[:, L, 8 * chunk + 4 * half:8 * chunk + 4 * half + 4, s]
                    v.tensor_tensor(diag[:, g % 2, :].rearrange("p (q c) -> p q c", q=4), bc(ident.unsqueeze(1), P, 4, P),
                                    bc(col.unsqueeze(2), P, 4, P), ALU.mult).then_inc(S("dg"), 1)

            def layernorm(i, tiles, base, bank, between=lambda t: None):
                dve.wait_ge(S("gb_mm"), (4, 8, 10, 12)[i])
                dve.wait_ge(S("gb_c"), (4, 8, 10, 12)[i])
                ltb = lt if i < 3 else at(BB + 4096, 2, D)
                for t in range(tiles):
                    s = t // NL
                    if i < 3:
                        dve.wait_ge(S("y_mm"), base + t + 1)
                    for c in range(2):
                        h = slice(512 * c, 512 * c + 512)
                        y = pb[bank(t) + c][:, :] if i < 3 else yacc[:, t, h]
                        ins = v.tensor_tensor(ltb[:, t % 2, h], y, gb[:, s, h], ALU.mult)
                        if c == 0:
                            link(ins)
                    ins.then_inc(S("y_c"), 1)
                    dve.wait_ge(S("y_c"), base + t + 1)
                    if i == 0:
                        dve.wait_ge(S("x_in"), 32)
                        dve.wait_ge(S("tm_t"), 2 * NT)
                    else:
                        dve.wait_ge(S("x_ln"), (0, NT, NT + NL, NT + 2 * NL)[i])
                    x = xr[:, t if i < 3 else NL + t, :]
                    link(v.scalar_tensor_tensor(out=x, in0=x, scalar=ALPHA, in1=ltb[:, t % 2, :], op0=ALU.mult,
                                                op1=ALU.add))
                    for c in range(2):
                        link(v.bn_stats(lnst[:, t, 6 * c:6 * c + 6], x[:, 512 * c:512 * c + 512]))
                    v.bn_aggr(lnst[:, t, 12:14], lnst[:, t, 0:12]).then_inc(S("var_r"), 1)
                    dve.wait_ge(S("std_r"), base + t + 1)
                    link(v.reciprocal(lnst[:, t, 15:16], lnst[:, t, 14:15]))
                    v.tensor_scalar(x, x, lnst[:, t, 12:13], lnst[:, t, 15:16], ALU.subtract, ALU.mult)\
                        .then_inc(S("x_hat"), 1)
                    between(t)

            def affine(n, L, ln, chunk):
                def vc(a):
                    return bc(vcol[:, a:a + 8].unsqueeze(2), P, 8, 2)
                a, b = (AB[:, n - 1, i].rearrange("p (k s) -> p k s", s=2) for i in range(2))
                scale, shift = modT[:, L, 8 * chunk + 8:8 * chunk + 16, :], modT[:, L, 8 * chunk:8 * chunk + 8, :]
                link(v.tensor_tensor(a, vc(32 * (ln[0] - 1) + 8 * ln[1]), scale, ALU.mult))
                link(v.tensor_tensor(b, vc(32 * (ln[0] - 1) + 16 + 8 * ln[1]), scale, ALU.mult))
                v.tensor_tensor(b, b, shift, ALU.add).then_inc(S("ab_r"), 1)

            def proj1():
                lb, oml = lbs[:, 3], lbs[:, 4]
                lo = vcol[:, 80:88]
                link(v.tensor_tensor(lbs[:, 0], lo, lo, ALU.subtract))
                dve.sem_inc(S("lb_s"), 1)
                dve.wait_ge(S("lb_e"), 1)
                link(v.reciprocal(lbs[:, 1], lbs[:, 0]))
                link(v.tensor_tensor(lbs[:, 2], lbs[:, 0], lbs[:, 1], ALU.mult))
                link(v.tensor_tensor(lb, lbs[:, 2], lbs[:, 2], ALU.subtract))
                link(v.tensor_scalar(oml, lb, -1.0, 1.0, ALU.mult, ALU.add))
                for d in range(2):
                    link(v.memset(cum[d][:, :, :, 0:1], 0.0))
                for d in range(2):
                    k = (kf, kb)[d]
                    for h in range(HGH):
                        c = slice(HGH * d + h, HGH * d + h + 1)
                        dve.wait_ge(S("sig"), 8 * d + 2 * h + 2)
                        link(v.tensor_scalar(k[:, h, :], k[:, h, :], oml[:, c], None, ALU.mult))
                        link(v.tensor_scalar(forget[:, h, :], forget[:, h, :], oml[:, c], lb[:, c], ALU.mult, ALU.add))
                        ins = v.tensor_scalar(forget[:, h, :], forget[:, h, :], F_MIN, None, ALU.max)
                        if h < HGH - 1:
                            link(ins)
                    ins.then_inc(S("f_r"), 1)
                    dve.wait_ge(S("ln_f"), d + 1)
                    for h in range(HGH):
                        for seg in range(2):
                            ins = v.tensor_tensor_scan(cum[d][:, seg, h, 1:CW], bc(ones[:, 0:1], P, SEQ),
                                                       forget[:, h, seg * SEQ:seg * SEQ + SEQ], 0.0, ALU.mult, ALU.add)
                            if (h, seg) != (HGH - 1, 1):
                                link(ins)
                    ins.then_inc(S("cum_r"), 1)
                dve.wait_ge(S("cum_r"), 2)
                dve.wait_ge(S("bias_in"), 16 * HEADS * ROWS)
                dve.wait_ge(S("c1_in"), 48)
                b = bias.rearrange("p u (i c) -> p (u i) c", c=GRID_W)
                v.tensor_tensor(b, b, bc(window.unsqueeze(1), P, 2 * HEADS * ROWS, GRID_W), ALU.add)\
                    .then_inc(S("bias_r"), 1)

            def hgrn():
                kl = [kf[:, :, 0:SEQ], kb[:, :, 0:SEQ]]
                for d in range(2):
                    dve.wait_ge(S("kend_e"), d + 1)
                    v.tensor_tensor(W[d], W[d], (kf, kb)[d][:, :, SEQ:TOK], ALU.mult).then_inc(S("kend"), 1)
                for d, q in enumerate((qxf, qxb)):
                    dve.wait_ge(S("qx_e"), d + 1)
                    dve.wait_ge(S("in1_c"), len(in1))
                    v.tensor_tensor(q, q, qd, ALU.mult).then_inc(S("qx"), 1)
                v.tensor_tensor(ksum, kl[0], kl[1], ALU.add).then_inc(S("ksum"), 1)
                dve.wait_ge(S("same_mm"), 1)
                dve.wait_ge(S("s_mm"), NU + NU1)
                for i in range(NL):
                    link(v.tensor_copy(AT[:, i, :, i * P:i * P + P], pb[4 + i].rearrange("p (h c) -> p h c", h=HGH)))
                N = len(levels)
                for n in range(N + 2):
                    if n < N:
                        m, d = levels[n]
                        c = cum[d][:, 0]
                        if n < 2:
                            dve.wait_ge(S("kend_t"), 2 * n + 2)
                        else:
                            dve.wait_ge(S("hg_mm"), n - 1)
                        nb = SEQ // (2 * m)
                        for h in ([None] if nb == 1 else range(HGH)):
                            if h is None:
                                ins = v.tensor_tensor(W[n % 2], c[:, :, 1 - d:1 - d + SEQ],
                                                      bc(c[:, :, m:m + 1], P, HGH, SEQ), ALU.subtract)
                            else:
                                ins = v.tensor_tensor(W[n % 2][:, h].rearrange("p (b m) -> p b m", b=nb),
                                                      c[:, h, 1 - d:1 - d + SEQ].rearrange("p (b m) -> p b m", b=nb),
                                                      bc(c[:, h, m:SEQ:2 * m].unsqueeze(2), P, nb, 2 * m), ALU.subtract)
                        ins.then_inc(S("hg_sub"), 1)
                    if 1 <= n <= N:
                        m, d = levels[n - 1]
                        dve.wait_ge(S("hg_exp"), n)
                        for i in range(2):
                            o = slice(i * m, i * m + m)
                            x = qd if i != d else kl[d]
                            w = W[(n - 1) % 2].rearrange("p h (b m) -> p h b m", m=2 * m)[:, :, :, o]
                            ins = v.tensor_tensor(w, w, x.rearrange("p h (b m) -> p h b m", m=2 * m)[:, :, :, o], ALU.mult)
                        ins.then_inc(S("hg_w"), 1)
                    if n >= 2:
                        m, d = levels[n - 2]
                        dve.wait_ge(S("hg_mm"), n - 1)
                        if n >= 3:
                            dve.wait_ge(S("hg_at"), n - 2)
                        for i in range(1 if m == P else NL):
                            b = pb[2 * (n % 2) + i].rearrange("p (h c) -> p h c", h=HGH)
                            if m == P:
                                dst = AT[:, 0, :, P:SEQ] if d == 0 else AT[:, 1, :, 0:P]
                                ins = v.tensor_copy(dst, b)
                            else:
                                k = masks[:, 2 * LEVELS.index(m) + d, :].bitcast(I32).unsqueeze(1)
                                ins = v.copy_predicated(AT[:, i, :, i * P:i * P + P], bc(k, P, HGH, P), b)
                        ins.then_inc(S("hg_at"), 1)
                for t in range(NL):
                    y = o1[:, t, 512:D]
                    yh = y.rearrange("p (h e) -> p h e", h=HGH)
                    sq = W[t].rearrange("p h c -> p (h c)")[:, 0:512]
                    dve.wait_ge(S("hg_o"), t + 1)
                    link(v.tensor_copy(y, pb[6 + t][:, :]))
                    link(v.tensor_tensor(sq, y, y, ALU.mult))
                    link(v.tensor_reduce(rms1[:, t, :], sq.rearrange("p (h e) -> p h e", h=HGH), AX.X, ALU.add))
                    v.tensor_scalar(rms1[:, t, :], rms1[:, t, :], 1.0 / P, 1e-6, ALU.mult, ALU.add)\
                        .then_inc(S("hg_ss"), 1)
                for t in range(NL):
                    y = o1[:, t, 512:D]
                    yh = y.rearrange("p (h e) -> p h e", h=HGH)
                    dve.wait_ge(S("hg_rt"), t + 1)
                    link(v.reciprocal(rms1[:, t, :], rms1[:, t, :]))
                    link(v.tensor_tensor(yh, yh, bc(rms1[:, t, :].unsqueeze(2), P, HGH, P), ALU.mult))
                    link(v.tensor_tensor(yh, yh, bc(onorm.unsqueeze(1), P, HGH, P), ALU.mult))
                    v.tensor_tensor(y, y, gd[:, t, :], ALU.mult).then_inc(S("y_hg"), 1)

            def route():
                L, oh = rt[0], (rt[1], rt[2])
                key, gate, mask, pos = rt[3], rt[4], rt[5], rt[6]
                cnt, over, rank, tmp = (rt[7 + i // 2][:, i % 2] for i in range(4))
                rk = r1[:, 6, :]
                rk = at(RT + 246, NE)
                top, first, e2 = r1[:, 0:2], r1[:, 3:5], r1[:, 2]

                def cols(x):
                    return bc(x.unsqueeze(2), P, NL, NE)
                dve.wait_ge(S("logit_mm"), 1)
                link(v.tensor_copy(L, pb[6][:, 0:NL * NE].rearrange("p (t e) -> p t e", t=NL)))
                link(v.tensor_scalar(rk, iota[:, 0:NE], -1.0, float(NE), ALU.mult, ALU.add))
                for j in range(2):
                    link(v.tensor_reduce(top[:, j], L, AX.X, ALU.max))
                    link(v.tensor_tensor(key, L, cols(top[:, j]), ALU.is_equal))
                    link(v.tensor_tensor(key, key, bc(rk.unsqueeze(1), P, NL, NE), ALU.mult))
                    link(v.tensor_reduce(first[:, j], key, AX.X, ALU.max))
                    link(v.tensor_tensor(oh[j], key, cols(first[:, j]), ALU.is_equal))
                    if j == 0:
                        link(v.scalar_tensor_tensor(out=L, in0=oh[0], scalar=NEG, in1=L, op0=ALU.mult, op1=ALU.add))
                v.tensor_tensor(mask, oh[0], oh[1], ALU.add).then_inc(S("mask_r"), 1)
                v.tensor_tensor(e2, top[:, 1], top[:, 0], ALU.subtract).then_inc(S("top_r"), 1)
                dve.wait_ge(S("top_e"), 1)
                w0, w1 = r1[:, 5], r1[:, 6]
                link(v.tensor_scalar(w0, e2, 1.0, None, ALU.add))
                link(v.reciprocal(w0, w0))
                link(v.tensor_tensor(w1, e2, w0, ALU.mult))
                link(v.tensor_tensor(gate, oh[0], cols(w0), ALU.mult))
                link(v.tensor_tensor(key, oh[1], cols(w1), ALU.mult))
                link(v.tensor_tensor(gateT[:, :, 0:NE], gate, key, ALU.add))
                dve.wait_ge(S("pos_mm"), 1)
                link(v.tensor_copy(pos, pb[7][:, 0:16].rearrange("p (t e) -> p t e", t=NL)))
                link(v.tensor_copy(cnt, pb[7][:, 16:24]))
                link(v.scalar_tensor_tensor(out=pos, in0=pos, scalar=1.0, in1=mask, op0=ALU.add, op1=ALU.mult))
                link(v.tensor_scalar(posT[:, :, 0:NE], pos, -1.0, None, ALU.add))
                link(v.tensor_scalar(over, cnt, float(CAP), None, ALU.is_gt))
                link(v.tensor_tensor_scan(rank, bc(ones[:, 0:1], P, NE), over, 0.0, ALU.mult, ALU.add))
                link(v.tensor_copy(nover, rank[:, NE - 1:NE]))
                link(v.tensor_copy(ids[:, 0:NE], iota[:, 0:NE]))
                link(v.memset(posT[:, :, NR - 1:NR], -1.0))
                link(v.memset(gateT[:, :, NR - 1:NR], 0.0))
                link(v.memset(at(RT + 48 + NR - 1, 1), 0.0))
                for x in range(EXTRA):
                    link(v.tensor_scalar(tmp, rank, float(x + 1), None, ALU.is_equal))
                    link(v.tensor_tensor(tmp, tmp, over, ALU.mult))
                    tb = bc(tmp.unsqueeze(1), P, NL, NE)
                    link(v.scalar_tensor_tensor(out=key, in0=pos, scalar=float(-CAP), in1=tb, op0=ALU.add, op1=ALU.mult))
                    link(v.tensor_reduce(first[:, 0], key, AX.X, ALU.add))
                    link(v.tensor_scalar(posT[:, :, NE + x], first[:, 0], -1.0, None, ALU.add))
                    link(v.tensor_tensor(key, gateT[:, :, 0:NE], tb, ALU.mult))
                    link(v.tensor_reduce(gateT[:, :, NE + x], key, AX.X, ALU.add))
                    link(v.tensor_tensor(tmp, tmp, iota[:, 0:NE], ALU.mult))
                    link(v.tensor_reduce(first[:, 1, 0:1], tmp, AX.X, ALU.add))
                    link(v.tensor_copy(ids[:, NE + x:NE + x + 1], first[:, 1, 0:1]))
                dve.sem_inc(S("routed"), 1)

            def select(r):
                for t in range(NL):
                    ins = v.tensor_scalar(sel[:, t, :], iota, posT[:, t, bass.ds(r, 1)], None, ALU.is_equal)
                ins.then_inc(S("sel_r"), 1)

            def accumulate(n, t):
                for c in range(2):
                    dve.wait_ge(S("sc_mm"), 4 * n + 2 * t + c + 1)
                    y = yacc[:, t, 512 * c:512 * c + 512]
                    v.tensor_tensor(y, y, pb[4 + c][:, :], ALU.add).then_inc(S("sc_a"), 1)

            def zero_outputs():
                for c in range(2):
                    v.memset(pb[4 + c][:, :], 0.0).then_inc(S("y_zero"), 1)

            def expert(r, n):
                for u in range(UNITS):
                    j, q = u // 4, u % 4
                    o = slot[j % RING] + UNIT * q
                    if q != POOLQ:
                        dve.wait_ge(S("w_hi"), r * UNITS + u + 1)
                        v.tensor_tensor(part(o, UNIT), at(o, UNIT), wH[u % HBUF].bitcast(F32), ALU.subtract)\
                            .then_inc(S("w_lo"), 1)
                    if u == 3:
                        dve.wait_ge(S("g_mm"), r * 2 + 2)
                        select(r + 1)
                    if u == 5:
                        dve.wait_ge(S("sg_t"), r + OPEN)
                        for t in range(NL):
                            ins = v.tensor_scalar(selG[:, t, :], iota, posT[:, t, bass.ds(r, 1)],
                                                  gateT[:, t, bass.ds(r, 1)], ALU.is_equal, ALU.mult)
                        ins.then_inc(S("selg"), 1)
                    if u in (9, 17):
                        accumulate(n, u // 17)
                    c, step = (u - 13) // 8, (u - 13) % 8
                    if step == 0 and 0 <= c < 7:
                        dve.wait_ge(S("e_s"), r * 7 + c + 1)
                        v.tensor_tensor(s_e[:, c % 2, :], s_e[:, c % 2, :], pb[2 + c % 2][:, :], ALU.mult)\
                            .then_inc(S("e_a"), 1)
                    if step == 2 and 1 <= c < 8:
                        k = slice(4 * c - 4, 4 * c)
                        dve.wait_ge(S("e_aH"), r * 7 + c)
                        v.tensor_tensor(aL[:, k, :].rearrange("p k c -> p (k c)"), pb[6][:, :],
                                        aH[:, k, :].rearrange("p k c -> p (k c)").bitcast(F32), ALU.subtract)\
                            .then_inc(S("e_aT"), 1)
                    if step == 4 and c == 6:
                        dve.wait_ge(S("hs_h"), r + 2)
                        v.tensor_tensor(hsL, hsN, hsH.bitcast(F32), ALU.subtract).then_inc(S("hs_r"), 1)

            setup()
            ada(0, 12)
            if STOP >= 5:
                dve.wait_ge(S("mod_col"), 12)
                affine(1, 0, (1, 0), 3)
            if STOP >= 3:
                heads0()
            if STOP >= 4:
                attention(units, 0, lambda u: oA[:, u[2], (0 if u[0] == "a" else 512) + HD * u[1]:][:, 0:HD])
            if STOP >= 5:
                gates(0, 2, 2, 0)
                layernorm(0, NT, 0, lambda t: 2 * (t % 2), lambda t: ada(*ADA1[t]))
                dve.wait_ge(S("mod_col"), 24)
                affine(2, 1, (2, 0), 0)
                affine(3, 1, (1, 1), 3)
            if STOP >= 6:
                gates(0, 5, 2, 4)
                for g in range(FK):
                    dve.wait_ge(S("ff_s"), g + 1)
                    v.tensor_tensor(aT0[:, g, :], sil[:, g % 2, :], pb[2 + g % 2][:, :], ALU.mult)\
                        .then_inc(S("ff_a"), 1)
                layernorm(1, NT, NT, lambda t: 2 * t)
            if STOP >= 8:
                proj1()
            if STOP >= 9:
                attention(units1, NU, lambda u: o1[:, u[2], HD * u[1]:][:, 0:HD])
            if STOP >= 10:
                hgrn()
            if STOP >= 11:
                gates(1, 2, 1, 8)
                layernorm(2, NL, 2 * NT, lambda t: 2 * (t % 2))
            if STOP >= 12:
                route()
            if STOP >= 99:
                v.memset(yacc.rearrange("p t d -> p (t d)"), 0.0).then_inc(S("yacc0"), 1)
                dve.wait_ge(S("yacc0"), 1)
                link(v.memset(selGT, 0.0))
                dve.wait_ge(S("o_c"), NU + NU1)
                zero_outputs()
                select(0)
                dve.wait_ge(S("x_ln"), NT + 2 * NL)
                dve.wait_ge(S("hs_h"), 1)
                v.tensor_tensor(hsL, hsN, hsH.bitcast(F32), ALU.subtract).then_inc(S("hs_r"), 1)
                for name in ("e_a", "e_aT"):
                    dve.sem_inc(S(name), OPEN)
                with dve.Fori(0, NE) as r:
                    expert(r, r)
                for t in range(NL):
                    accumulate(NE, t)
                dve.wait_ge(S("sc_a"), 4 * NE + 4)
                many = dve.value_load(nover[0:1, :], min_val=0, max_val=EXTRA)
                with dve.If(many > 0):
                    zero_outputs()
                    with dve.Fori(NE, ROUNDS) as r:
                        expert(r, r + 1)
                    for t in range(NL):
                        accumulate(ROUNDS + 1, t)
                    dve.wait_ge(S("sc_a"), 4 * ROUNDS + 8)
                gates(1, 5, 1, 10)
                layernorm(3, NL, 2 * NT + NL, None)
            if STOP < 99: v.memset(at(small + 401, 1), 0.0).then_inc(S("dbg_go"), 1)

        @block.gpsimd
        def _(pool):
            made = [0]

            def gain_bias(i, tiles, base):
                for t in range(tiles):
                    pool.wait_ge(S("lnrow_in"), 32 * (i + 1))
                    pool.wait_ge(S("x_hat"), base + t + 1)
                    if i < 3:
                        pool.wait_ge(S("tm_t"), TMB[i + 1] + 2 * t + 2)
                    x = xr[:, t if i < 3 else NL + t, :]
                    y = xr[:, t if i < 2 else NL + t, :]
                    made[0] += 1
                    nc.gpsimd.tensor_tensor(y, x, lnrow[:, 0, :], ALU.mult).then_inc(S("x_g"), 1)
                    pool.wait_ge(S("x_g"), made[0])
                    nc.gpsimd.tensor_tensor(y, y, lnrow[:, 1, :], ALU.add).then_inc(S("x_ln"), 1)
            if STOP >= 5:
                gain_bias(0, NT, 0)
            if STOP >= 6:
                gain_bias(1, NL, NT)
            if STOP >= 11:
                gain_bias(2, NL, 2 * NT)
            if STOP >= 99:
                def low_parts(r):
                    for j in range(21):
                        o = slot[j % RING] + UNIT * POOLQ
                        pool.wait_ge(S("w_hi"), r * UNITS + 4 * j + POOLQ + 1)
                        nc.gpsimd.tensor_tensor(part(o, UNIT), at(o, UNIT), wH[(4 * j + POOLQ) % HBUF].bitcast(F32),
                                                ALU.subtract).then_inc(S("w_lo_g"), 1)
                with pool.Fori(0, NE) as r:
                    low_parts(r)
                pool.wait_ge(S("routed"), 1)
                many = pool.value_load(nover[0:1, :], min_val=0, max_val=EXTRA)
                with pool.If(many > 0):
                    with pool.Fori(NE, ROUNDS) as r:
                        low_parts(r)
                gain_bias(3, NL, 2 * NT + NL)
            if made[0]:
                pool.wait_ge(S("x_ln"), made[0])
            if STOP < 99: nc.gpsimd.memset(at(small + 402, 1), 0.0).then_inc(S("dbg_go"), 1)


_NAMES = ["x", "c", "ctx", "c_ctx", "ada_w", "ada_b", "ln1_g", "ln1_b", "ln2_g", "ln2_b", "ev_w_in", "ev_qn_g",
          "ev_kn_g", "ev_cq_g", "ev_ckv_g", "ev_w_uq", "ev_w_ukv", "ev_w_out", "ff_w_gate", "ff_w_up", "ff_w_down",
          "od_w_in", "od_rpb", "od_lb_logits", "od_onorm_g", "od_w_out", "moe_router", "moe_w_gate", "moe_w_up",
          "moe_w_down"]
_PACKED = ["c", "c_ctx", "ada_b", "od_lb_logits", "od_rpb"]


def kernel(_stop=None, _taps=None, **inputs):
    import concourse.bacc as bacc
    from concourse.bass_utils import run_bass_kernel_spmd

    nc = bacc.Bacc("TRN2", target_bir_lowering=False, num_devices=1)
    a = {n: np.ascontiguousarray(inputs[n]) for n in _NAMES}
    arrays = {n: a[n] for n in _NAMES if n not in _PACKED}
    arrays["c_base"], arrays["c_rope"], arrays["c_hg"] = constants()
    arrays["vr1"] = a["ada_b"].reshape(96, P)
    arrays["vr2"] = np.concatenate([a[n].reshape(-1, P) for n in ("ln1_g", "ln1_b", "ln2_g", "ln2_b", "c", "c_ctx",
                                                                  "od_lb_logits")], 0)
    arrays["rpb"] = np.pad(a["od_rpb"][0], ((0, 0), (0, 0), (RPB_PAD, RPB_PAD)))
    feeds, aps = {}, {}
    for n, v in arrays.items():
        feeds[f"in_{n}"] = v
        aps[n] = nc.dram_tensor(f"in_{n}", v.shape, F32, kind="ExternalInput").ap()
    shapes = {"out": (1, SEQ, D)} if _stop is None else _taps
    outs = {n: nc.dram_tensor(f"out_{n}", s, F32, kind="ExternalOutput").ap() for n, s in shapes.items()}
    bass_hybrid_dit(nc, aps, outs.get("out"), _stop, outs)
    r = run_bass_kernel_spmd(nc, [feeds], core_ids=[0])
    got = tuple(r.results[0][f"out_{n}"] for n in shapes)
    return got[0] if _stop is None else got
```

```python
from contextlib import ExitStack

import numpy as np

import concourse.bass as bass
from concourse import mybir

F32 = mybir.dt.float32
F32R = mybir.dt.float32r
I32 = mybir.dt.int32
ALU = mybir.AluOpType
ACT = mybir.ActivationFunctionType
AX = mybir.AxisListType

P = 128
D = 1024
DK = D // P
SEQ = 256
CTX = 256
TOK = SEQ + CTX
NT = TOK // P
NL = SEQ // P
GRID_W = 64
ROWS = SEQ // GRID_W
DEPTH = 2
ALPHA = (2 * DEPTH) ** 0.25
HEADS = 8
HD = 64
KVH = 2
QR = 384
KVR = 256
NOPE = 64
ROPE = 32
QKB = NOPE + ROPE
EV_IN = 1440
DFF = 2816
FK = DFF // P
OD_IN = 4096
NE = 8
DFE = 3584
EK = DFE // P
HGH = 4
NBR_ROWS = 8
NBR_COLS = 16
RPB_W = 2 * NBR_COLS - 1
RPB_PAD = GRID_W - NBR_COLS
RPB_PW = RPB_W + 2 * RPB_PAD
SLOT = 4096
RING = 7
RING0 = 4
CAP = P
EXTRA = (2 * SEQ) // (CAP + 1)
ROUNDS = NE + EXTRA
UNIT = SLOT // 4
POOLQ = 1
HBUF = 4
UNITS = 84
LEVELS = [64, 32, 16, 8, 4, 2, 1]
F_MIN = 2.0 ** -63
NEG = -1e30


def constants():
    ident = np.eye(P, dtype=np.float32)
    iota = np.tile(np.arange(P, dtype=np.float32), (P, 1))
    upper = np.triu(np.ones((P, P), np.float32), 1)
    ones = np.ones((P, P), np.float32)
    flip = np.kron(np.eye(P // GRID_W), np.eye(GRID_W)[::-1]).astype(np.float32)
    base = np.concatenate([ident, iota, upper, ones, flip], 1)
    tabs = []
    t = np.arange(SEQ)
    pos = np.stack([t // GRID_W, t % GRID_W], -1).astype(np.float32)
    for rot in (HD, ROPE):
        ad = rot // 2
        inv = (np.float32(10000.0) ** (-np.arange(0, ad, 2, dtype=np.float32) / ad)).astype(np.float32)
        ang = pos[:, :, None] * inv
        ang = np.concatenate([ang, ang], -1).reshape(SEQ, rot)
        sin = np.sin(ang).reshape(SEQ, 2, 2, ad // 2)
        sin = sin * np.array([-1.0, 1.0], np.float32)[None, None, :, None]
        tabs += [np.cos(ang), sin.reshape(SEQ, rot)]
    rope = np.concatenate(tabs, 1).astype(np.float32)
    cc = np.arange(GRID_W)
    start = np.clip(cc - NBR_COLS // 2, 0, GRID_W - NBR_COLS)
    inside = (cc[None, :] >= start[:, None]) & (cc[None, :] < start[:, None] + NBR_COLS)
    window = np.tile(np.where(inside, 0.0, NEG).astype(np.float32)[::-1], (2, 1))
    s, tt = np.meshgrid(np.arange(P), np.arange(P), indexing="ij")
    masks = []
    for m in LEVELS:
        same = (s // (2 * m)) == (tt // (2 * m))
        fwd = same & (s % (2 * m) < m) & (tt % (2 * m) >= m)
        masks += [fwd, fwd.T]
    masks.append(s == tt)
    hg = np.concatenate([window] + [m.astype(np.float32) for m in masks], 1)
    return base, rope, np.ascontiguousarray(hg)


def bass_hybrid_dit(nc, A, out):
    es = ExitStack()
    with es:
        NMEM = 53200
        start = -(-nc.sbuf_base // 32) * 32
        AREAS = [0, SLOT, 2 * SLOT, 3 * SLOT, 4 * SLOT, 7 * SLOT, 8 * SLOT, 9 * SLOT, 10 * SLOT, 10 * SLOT + 1704, NMEM]
        areas = {}
        pb = [es.enter_context(nc.psum_tensor(f"bank{i}", [P, 512], F32)) for i in range(8)]
        sems = {}

        def S(name):
            if name not in sems:
                sems[name] = es.enter_context(nc.semaphore(name))
            return sems[name]

        def at(a, *dims, parts=P, kind=F32):
            n = int(np.prod(dims))
            i = max(i for i, first in enumerate(AREAS) if first <= a)
            first, end = AREAS[i], AREAS[i + 1]
            assert a + n <= end
            if (i, kind) not in areas:
                name = f"area{i}" if kind == F32 else f"parts{i}"
                areas[i, kind] = nc.alloc_sbuf_tensor_at(name, [P, end - first], kind, offset=start + 4 * first)
            v = areas[i, kind][0:parts, a - first:a - first + n]
            if len(dims) == 2:
                v = v.rearrange("p (a b) -> p a b", a=dims[0])
            if len(dims) == 3:
                v = v.rearrange("p (a b c) -> p a b c", a=dims[0], b=dims[1])
            return v

        def part(a, *dims):
            return at(a, *dims, kind=F32R)

        def bc(ap, *shape):
            return ap.broadcast_to(list(shape))

        slot = [i * SLOT for i in range(RING)]
        ARENA = RING0 * SLOT
        X = RING * SLOT
        HT = X + 4096
        G = HT + 4096
        base_c = G + 4096
        ident = at(base_c, P)
        iota = at(base_c + 128, P)
        upper = at(base_c + 256, P)
        ones = at(base_c + 384, P)
        flip = at(base_c + 512, P)
        c0 = base_c + 640
        vcol = at(c0, 88)
        adab = at(c0 + 88, 96)
        modT = at(c0 + 184, 2, 48, 2)
        AB = at(c0 + 376, 3, 2, 16)
        sT = at(c0 + 472, 16)
        lnst = at(c0 + 488, NT, 16)
        eps_c = at(c0 + 88 + 96 + 192 + 96 + 15 + 1 + 64, 1)
        small = c0 + 560
        BB = small + 504
        xr = at(X, NT, D)
        hT = at(HT, DK, TOK)
        hL = part(HT, DK, TOK)
        hH = [part(a, DK, TOK) for a in (ARENA, BB + 3072, 3 * SLOT)]
        awH = [part(G + UNIT * i, 2, 512) for i in range(2)]
        s_hl = part(c0 + 560 + 420, DK, 4)
        s_h0 = part(c0 + 560 + 452, DK, 4)
        iwH = [part(G + 1984 + UNIT * i, UNIT) for i in range(2)]
        pwH = [part(ARENA + 4096 + UNIT * i, UNIT) for i in range(4)]
        gb = at(G, 2, D)
        lnrow = at(G + 2048, 2, D)

        qTa = at(ARENA, 4, TOK)
        kTa = at(ARENA + 2048, KVH, TOK)
        va = at(ARENA + 3072, NT, P)
        qTb = at(ARENA + 3584, HEADS, TOK)
        kTb = at(ARENA + 7680, HEADS, TOK)
        ropt = at(HT, 640)
        vb = at(BB, NT, 512)
        PJ = BB + 2048
        proj = at(PJ, NT, EV_IN)
        rope_c = at(PJ + 5760, NL, 192)
        gains = at(PJ + 6144, 10, HD)
        cqg = at(PJ + 6784, QR)
        ckvg = at(PJ + 7168, KVR)
        ssq = at(PJ + 7424, NT, 16)
        sqj = at(PJ + 7488, 640)
        qbt = at(G, 2, HEADS, QKB)
        kbt = at(G + 1536, 2, HEADS, QKB)
        latT = at(G + 3072, 5, P)
        kdup = at(G + 3712, KVH, 2, HD)
        oA = at(PJ, NT, D)
        p_sb = at(PJ + 4096, 2, 512)
        pT_sb = at(PJ + 6144, 2, 512)
        oT = hT
        mx = at(small, 4, 4)
        rowbuf = at(PJ + 7424, 2, 512)
        vr1 = at(PJ, P)
        vr2 = at(PJ + 128, P)
        aT0 = at(ARENA, FK, TOK)
        aL0 = part(ARENA, FK, TOK)
        aH0 = part(HT, 8, TOK)
        fwH = [part(BB + 7168 + UNIT * i, UNIT) for i in range(3)]
        sil = at(BB, 2, 512)
        lt = at(BB + 1024, 2, D)
        diag = at(BB + 1024, 2, 512)

        qnT = at(ARENA, 4, SEQ)
        knT = at(ARENA + 1024, 4, TOK)
        vn = at(ARENA + 3072, NT, 512)
        oT1 = at(ARENA + 3072, DK, SEQ)
        qd = at(ARENA + 5120, HGH, SEQ)
        vd = at(ARENA + 6144, NT, 512)
        gd = at(ARENA + 8192, NL, 512)
        kf = at(ARENA + 9216, HGH, TOK)
        qxf = at(ARENA + 11264, HGH, SEQ)
        kb = at(BB, HGH, TOK)
        CW = SEQ + 1
        cum = [at(BB + 2048 + i * 2 * HGH * CW, 2, HGH, CW) for i in range(2)]
        BI = BB + 2048 + 4 * HGH * CW
        bias = at(BI, 2 * HEADS, SEQ)
        AT = at(BI, NL, HGH, SEQ)
        kendT = at(BI + 2048, NL, HGH, P)
        state = at(BI + 3072, 2, HGH, P)
        onorm = at(BI + 4096, P)
        rms1 = at(BI + 4224, NL, HGH)
        forget = at(X + 2048, HGH, TOK)
        p1 = at(HT, 2, 512)
        pT1 = at(HT + 1024, 2, 512)
        qxb = at(HT, HGH, SEQ)
        ksum = at(HT + 1024, HGH, SEQ)
        W = [at(HT + 2048 + 1024 * i, HGH, SEQ) for i in range(2)]
        window = at(G, GRID_W)
        masks = at(G + GRID_W, 2 * len(LEVELS) + 1, P)
        o1 = at(G + 1984, NL, D)
        lbs = at(small + 16, 6, 2 * HGH)
        hsH, hsL = part(BB, DK, P), part(BB + 1024, DK, P)
        yacc = at(BB + 2048, NL, D)
        aH, aL = part(BB + 4096, EK, P), part(G, EK, P)
        s_e = at(BB + 7680, 2, 512)
        sel = at(BB + 8704, NL, P)
        selG = at(BB + 8960, NL, P)
        selGT = at(BB + 9216, SEQ)
        hsN = at(BB + 9472, DK, P)
        y_e = at(BB + 9472, D)
        wH = [part(HT + UNIT * i, UNIT) for i in range(HBUF)]
        router = at(small + 80, DK, NE)
        RT = small + 144
        NR = ROUNDS + 1
        posT = at(RT, NL, NR)
        gateT = at(RT + 24, NL, NR)
        ids = at(RT + 48, NR).bitcast(I32)
        nover = at(RT + 60, 1).bitcast(I32)
        rt = [at(RT + 64 + 16 * i, NL, NE) for i in range(10)]
        r1 = at(RT + 230, 8, NL)

        def rows(ap, pat, **k):
            return ap.rearrange(pat, **k)

        def cols_slot(w, a, b):
            return w.rearrange("(k p) n -> p k n", p=P)[:, :, a:b]

        def rows_slot(w, k0, k1):
            return w.rearrange("(k p) n -> p k n", p=P)[:, k0:k1, :]

        loads = []

        def add(name, src, a, b, *read):
            loads.append((name, src, a, b, read))

        ADA_ATT = 10

        def ada_loads(L, first, last):
            for j in range(first, last):
                add(("ada", L, j), cols_slot(A["ada_w"][L], 512 * j, 512 * j + 512), DK, 512,
                    "mod_mm", 12 * L + j + 1)
        ada_loads(0, 0, 12)
        EVC = [(0, 512), (512, 1024), (1024, EV_IN)]
        for i, (a, b) in enumerate(EVC):
            add(("evin", a), cols_slot(A["ev_w_in"][0], a, b), DK, b - a, "proj_mm", NT * (i + 1))
        add(("uq",), rows_slot(A["ev_w_uq"][0], 0, 3), 3, 768, "up_mm", 2 * NT)
        add(("ukv",), rows_slot(A["ev_w_ukv"][0], 0, 2), 2, 1024, "up_mm", 2 * NT)
        ada_loads(1, 0, ADA_ATT)
        for c in range(2):
            add(("evout", c), cols_slot(A["ev_w_out"][0], 512 * c, 512 * c + 512), DK, 512, "y_mm", NT)
        ada_loads(1, ADA_ATT, 12)
        FC = [(a, min(a + 512, DFF)) for a in range(0, DFF, 512)]
        for a, b in FC:
            add(("fg", a), cols_slot(A["ff_w_gate"][0], a, b), DK, b - a, "fw_mm", 2 * (b // P))
            add(("fu", a), cols_slot(A["ff_w_up"][0], a, b), DK, b - a, "fw_mm", 2 * (b // P))
        FD = [(a, min(a + 4, FK)) for a in range(0, FK, 4)]
        for i, (a, b) in enumerate(FD):
            add(("fd", a), rows_slot(A["ff_w_down"][0], a, b), b - a, D,
                *(("fw_mm", 2 * FK + b) if b <= FK - 3 else ("y_mm", 2 * NT)))
        TOKEN_MAJOR = (2, 4, 7)
        ORDER1 = [5, 6, 3, 0, 1, 2, 4, 7]
        in1 = [(c, i) for c in ORDER1 for i in range(NL if c == 7 else 4)]
        in1_at = [4 * ORDER1.index(c) + (3 if c in TOKEN_MAJOR else i) for c, i in in1]
        for c in ORDER1:
            add(("odin", c), cols_slot(A["od_w_in"][0], 512 * c, 512 * c + 512), DK, 512,
                "in1_mm", max(i for i, u in enumerate(in1) if u[0] == c) + 1)
        for c in range(2):
            add(("odout", c), cols_slot(A["od_w_out"][0], 512 * c, 512 * c + 512), DK, 512, "y_mm", 2 * NT + NL)
        index = {name: n for n, (name, *_) in enumerate(loads)}
        NPRE = len(loads)
        ODIN = index["odin", ORDER1[0]]
        ring_slot = [n % RING0 if n < ODIN else (n - ODIN) % (RING0 - 1) for n in range(NPRE)]
        nth = [ring_slot[:n + 1].count(ring_slot[n]) for n in range(NPRE)]
        base_n = [ring_slot.count(s) for s in range(RING)]

        def view(name, kind=F32):
            n = index[name]
            return at(slot[ring_slot[n]], loads[n][2], loads[n][3], kind=kind)

        def landed(eng, *name):
            n = index[name]
            eng.wait_ge(S(f"w_landed{ring_slot[n]}"), 16 * nth[n])
            return view(name)

        def ada_units(kind=F32):
            return [view(("ada", 1, j), kind)[:, 2 * q:2 * q + 2, :] for j in range(ADA_ATT) for q in range(4)]

        def ada_used(u):
            j, q = u // 4, u % 4
            return (S("mod_mm"), 12 + j + 1) if q == 3 else (S("ada_rows"), 3 * j + q + 1)

        def evin_units(kind=F32):
            return [(i, q, ("evin", a), view(("evin", a), kind)[:, 2 * q:2 * q + 2, :])
                    for i, (a, b) in enumerate(EVC) for q in range(4)]

        def in1_units(kind=F32):
            u = []
            for c in ORDER1:
                w = view(("odin", c), kind)
                u += [(c, q, w[:, 2 * q:2 * q + 2, :] if c in TOKEN_MAJOR else w[:, :, q * P:q * P + P]) for q in range(4)]
            return u

        def in1_hi(u):
            k = 2 if ORDER1[u // 4] in TOKEN_MAJOR else DK
            return iwH[u % 2].rearrange("p (k n) -> p k n", k=k)

        def in1_done(u):
            m, q = u // 4, u % 4
            c = ORDER1[m]
            if c not in TOKEN_MAJOR:
                return S("in1_mm"), 4 * m + q + 1
            if q == 3:
                return S("in1_mm"), 4 * m + (NL if c == 7 else NT)
            return S("in1_rows"), 3 * sum(x in TOKEN_MAJOR for x in ORDER1[:m]) + q + 1

        def ff_units(kind=F32):
            u = [((x, a), view((x, a), kind)[:, :, f * P:f * P + P])
                 for a, b in FC for f in range((b - a) // P) for x in ("fg", "fu")]
            return u + [(("fd", a), view(("fd", a), kind)[:, k - a, :]) for a, b in FD for k in range(a, b)]

        def chain(eng, name):
            count = [0]

            def link(ins):
                count[0] += 1
                ins.then_inc(S(name), 1)
                eng.wait_ge(S(name), count[0])
            return link

        TMB = [0, 2 * NT, 4 * NT, 6 * NT, 6 * NT + 2 * NL]

        ADA_UNITS = 6
        ada_step = {}
        for j in range(ADA_ATT):
            for k in range(DK):
                ada_step.setdefault(("mm", ADA_UNITS * j + k * ADA_UNITS // DK), []).append((j, k))
            for q, at_unit in enumerate((-2, -1, 1, 2)):
                ada_step["hi", max(ADA_UNITS * j + at_unit, -1), q] = 4 * j + q
            ada_step["row", ADA_UNITS * j + ADA_UNITS - 1] = j
            ada_step["col", ADA_UNITS * j + ADA_UNITS + 1] = j
            ada_step["add", ADA_UNITS * j + ADA_UNITS + 2] = j
        TBANK = [4, 4, 0, 4]

        units = [(kind, h, t, 0 if t < NL else SEQ, TOK if t < NL else CTX)
                 for kind in "ab" for h in range(HEADS) for t in range(NT)]
        scale_of = {"a": HD ** -0.5, "b": QKB ** -0.5}
        NU = len(units)
        units1 = [("n", h, t, 0, TOK) for h in range(HEADS) for t in range(NL)]
        scale_of["n"] = 1.0
        NU1 = len(units1)
        levels = [(m, d) for m in [P] + LEVELS for d in range(2)]
        U0 = 2 * FK
        OPEN = 1

        def ln_rows(sp, which):
            g, b = [(A["ln1_g"][0:1], A["ln1_b"][0:1]), (A["ln2_g"][0:1], A["ln2_b"][0:1]),
                    (A["ln1_g"][1:2], A["ln1_b"][1:2]), (A["ln2_g"][1:2], A["ln2_b"][1:2])][which]
            if which == 0:
                sp.wait_ge(S("tp_b"), 2 * HEADS)
            else:
                sp.wait_ge(S("x_ln"), (0, NT, NT + NL, NT + 2 * NL)[which])
            if which == 3:
                sp.wait_ge(S("gb_mm"), 12)
            if which == 2:
                sp.wait_ge(S("oT_t"), 2 * NT + 2 * NL)
            sp.dma_start(lnrow[:, 0, :], bc(g, P, D)).then_inc(S("lnrow_in"), 16)
            sp.dma_start(lnrow[:, 1, :], bc(b, P, D)).then_inc(S("lnrow_in"), 16)

        def layer1_loads(sp):
            sp.wait_ge(S("y_c"), 2 * NT)
            sp.wait_ge(S("x_ln"), NT + NL)
            sp.dma_start(at(G, 1984), A["c_hg"]).then_inc(S("c1_in"), 16)
            sp.dma_start(onorm, bc(A["od_onorm_g"], P, P)).then_inc(S("c1_in"), 16)
            sp.dma_start(router, A["moe_router"][0].rearrange("(k p) e -> p k e", p=P)).then_inc(S("c1_in"), 16)

        def bias_loads(sp):
            sp.wait_ge(S("y_mm"), 2 * NT)
            table = A["rpb"]
            for h in range(HEADS):
                for r in range(ROWS):
                    t, rl = r // 2, r % 2
                    src = bass.AP(table.tensor, (h * (2 * NBR_ROWS - 1) + NBR_ROWS - 1 - r) * RPB_PW,
                                  [[1, GRID_W], [RPB_PW, ROWS], [1, GRID_W]])
                    dst = bias[rl * GRID_W:(rl + 1) * GRID_W, 2 * h + t, :].rearrange("p (i c) -> p i c", i=ROWS)
                    sp.dma_start(dst, src).then_inc(S("bias_in"), 16)

        def expert_load(sp, r, e, j, first=False):
            s = j % RING
            if not first:
                i = j - RING if j >= RING else j + 2 * RING
                rr = r if j >= RING else r - 1
                sp.wait_ge(S("unit_mm"), rr * UNITS + 4 * (i + 1) + HBUF)
            if j < 14:
                w = A[("moe_w_gate", "moe_w_up")[j % 2]][0]
                a = 512 * (j // 2)
                src = w[bass.ds(e, 1), :, a:a + 512].rearrange("o (k p) n -> p (o k) n", p=P)
                dst = at(slot[s], DK, 512)
            else:
                k = 4 * (j - 14)
                src = A["moe_w_down"][0][bass.ds(e, 1), k * P:(k + 4) * P, :].rearrange("o (k p) n -> p (o k) n", p=P)
                dst = at(slot[s], 4, D)
            sp.dma_start(dst, src).then_inc(S(f"w_landed{s}"), 16)

        def experts_loads(sp):
            last = {ring_slot[n]: n for n in range(NPRE)}
            for j in range(21):
                if j < RING:
                    if j < RING0:
                        sp.wait_ge(S(loads[last[j]][4][0]), loads[last[j]][4][1])
                        sp.wait_ge(S("in1_mm"), len(in1))
                    else:
                        sp.wait_ge(S("y_mm"), 2 * NT + NL)
                    expert_load(sp, 0, 0, j, first=True)
                else:
                    expert_load(sp, 0, 0, j)
            with sp.Fori(1, NE) as r:
                for j in range(21):
                    expert_load(sp, r, r, j)
            sp.wait_ge(S("routed"), 1)
            many = sp.value_load(nover[0:1, :], min_val=0, max_val=EXTRA)
            with sp.If(many > 0):
                with sp.Fori(NE, ROUNDS) as r:
                    e = sp.value_load(ids[0:1, bass.ds(r, 1)], min_val=0, max_val=NE - 1)
                    for j in range(21):
                        expert_load(sp, r, e, j)

        block = es.enter_context(nc.Block())

        @block.sync
        def _(sp):
            def small_loads():
                sp.dma_start(at(base_c, 640), A["c_base"]).then_inc(S("c_in"), 16)
                for d, s in ((vr1[0:96, :], A["vr1"]), (vr2[0:88, :], A["vr2"])):
                    sp.dma_start(d, s).then_inc(S("c_in"), 16)

            def token_loads():
                sp.dma_start(xr[:, 0:NL, :], A["x"][0].rearrange("(t p) d -> p t d", p=P)).then_inc(S("x_in"), 16)
                sp.dma_start(xr[:, NL:NT, :], A["ctx"][0].rearrange("(t p) d -> p t d", p=P)).then_inc(S("x_in"), 16)
                sp.dma_start(rope_c, A["c_rope"].rearrange("(t p) d -> p t d", p=P)).then_inc(S("g_in"), 16)
                sp.dma_start(gains[:, 0:8, :], bc(A["ev_qn_g"].unsqueeze(1), P, 8, HD)).then_inc(S("g_in"), 16)
                sp.dma_start(gains[:, 8:10, :], bc(A["ev_kn_g"].unsqueeze(1), P, 2, HD)).then_inc(S("g_in"), 16)
                sp.dma_start(cqg, bc(A["ev_cq_g"], P, QR)).then_inc(S("g_in"), 16)
                sp.dma_start(ckvg, bc(A["ev_ckv_g"], P, KVR)).then_inc(S("g_in"), 16)
            small_loads()

            def load(n):
                s = ring_slot[n]
                before = [i for i in range(n) if ring_slot[i] == s]
                if before:
                    sem, value = loads[before[-1]][4]
                    sp.wait_ge(S(sem), value)
                _, src, a, b, _ = loads[n]
                sp.dma_start(at(slot[s], a, b), src).then_inc(S(f"w_landed{s}"), 16)
            for n in range(NPRE):
                load(n)
                if n == RING0 - 1:
                    token_loads()
                if loads[n][0] == ("ada", 1, 11):
                    ln_rows(sp, 0)
                if loads[n][0] == ("fd", 20):
                    ln_rows(sp, 1)
                if loads[n][0] == ("odin", ORDER1[2]):
                    bias_loads(sp)
                    layer1_loads(sp)
            ln_rows(sp, 2)
            experts_loads(sp)
            ln_rows(sp, 3)
            for t in range(NL):
                sp.wait_ge(S("x_ln"), NT + 2 * NL + t + 1)
                sp.dma_start(out[0, t * P:t * P + P, :], xr[:, NL + t, :]).then_inc(S("out_done"), 16)
            sp.wait_ge(S("out_done"), 16 * NL)
        @block.tensor
        def _(pe):
            mm = nc.tensor.matmul
            tp = nc.tensor.transpose

            def split_mm(bank, a, b, first, last):
                mm(bank, a[0], b[0], start=first, stop=False)
                mm(bank, a[0], b[1], start=False, stop=False)
                return mm(bank, a[1], b[0], start=False, stop=last)

            def setup():
                pe.wait_ge(S("c_in"), 48)
                tp(pb[4][:, 0:96], vr1[0:96, :], ident[0:96, 0:96])
                tp(pb[5][:, 0:88], vr2[0:88, :], ident[0:88, 0:88]).then_inc(S("vec_t"), 1)
                pe.wait_ge(S("silu_c"), 1)

            def ada_mm(bank, L, j, ks):
                sv = sT.rearrange("p (s k) -> p s k", s=2)
                w = landed(pe, "ada", L, j)
                for k in ks:
                    ins = mm(bank[0:2, :], sv[:, :, k], w[:, k, :], start=(k == 0), stop=(k == DK - 1))
                if ks[-1] == DK - 1:
                    ins.then_inc(S("mod_mm"), 1)

            def ada_cols(bank, i):
                for q in range(4):
                    ins = tp(bank[:, 2 * q:2 * q + 2], rowbuf[0:2, i % 2, q * P:q * P + P], ident[0:2, 0:2])
                ins.then_inc(S("mod_t"), 1)

            def ada_split(bank, j, k):
                u = 4 * j + k // 2
                pe.wait_ge(S("ada_lo"), u + 1)
                mm(bank[0:4, :], s_hl[:, k, :], awH[u % 2][:, k % 2, :], start=(k == 0), stop=False)
                ins = mm(bank[0:4, :], s_h0[:, k, :], ada_units(F32R)[u][:, k % 2, :], start=False, stop=(k == DK - 1))
                if k == DK - 1:
                    ins.then_inc(S("mod_mm"), 1)
                elif k % 2:
                    ins.then_inc(S("ada_rows"), 1)

            def ada(L, first, last):
                B = 4 * L
                if L == 1:
                    pe.wait_ge(S("gb_c"), 4)
                for i in range(first, last + 1):
                    if i < last:
                        if i >= first + 2:
                            pe.wait_ge(S("mod_row"), i - 1)
                        ada_mm(pb[B + i % 2], L, i - 12 * L, range(DK))
                    i -= 1
                    if i >= first:
                        pe.wait_ge(S("mod_row"), i + 1)
                        if i >= 2:
                            pe.wait_ge(S("mod_col"), i - 1)
                        ada_cols(pb[B + 2 + i % 2], i)

            def ada_beside(u):
                steps = ada_step.get(("mm", u), [])
                if steps:
                    j = steps[0][0]
                    if steps[0][1] == 0 and j > 0:
                        pe.wait_ge(S("mod_row"), 12 + j)
                    for _, k in steps:
                        ada_split(pb[6], j, k)
                j = ada_step.get(("col", u))
                if j is not None:
                    pe.wait_ge(S("mod_row"), 12 + j + 1)
                    pe.wait_ge(S("mod_col"), 12 + j)
                    for q in range(4):
                        ins = tp(pb[7][:, 4 * q:4 * q + 4], rowbuf[0:4, j % 2, q * P:q * P + P], ident[0:4, 0:4])
                    ins.then_inc(S("mod_t"), 1)

            def transpose_in(n, tiles):
                for t in range(tiles):
                    if n > 0:
                        pe.wait_ge(S("x_hat"), (0, 0, NT, 2 * NT)[n] + t + 1)
                    for half in range(2):
                        g = TMB[n] + 2 * t + half
                        b = TBANK[n] + g % 2
                        if g >= 2:
                            pe.wait_ge(S("hT_half"), g - 1)
                        if n == 0 and g < 2:
                            pe.wait_ge(S("vec_c"), 2)
                        for q in range(4):
                            k = 4 * half + q
                            ins = tp(pb[b][:, q * P:q * P + P], xr[:, t, k * P:k * P + P], ident)
                        ins.then_inc(S("tm_t"), 1)

            def proj0():
                pe.wait_ge(S("h_lo"), TMB[1])
                for u, (i, q, name, lo) in enumerate(evin_units(F32R)):
                    pe.wait_ge(S("pw_lo"), u + 1)
                    n = lo.shape[2]
                    hi = pwH[u % 4][:, 0:2 * n].rearrange("p (k n) -> p k n", k=2)
                    for t in range(NT):
                        if i == 2 and q == 0:
                            pe.wait_ge(S("proj_c"), t + 1)
                        for k in range(2):
                            kk, c = 2 * q + k, slice(t * P, t * P + P)
                            ins = split_mm(pb[4 * (i % 2) + t][:, 0:n], (hH[0][:, kk, c], hL[:, kk, c]),
                                           (hi[:, k, :], lo[:, k, :]), kk == 0, kk == DK - 1)
                        if q == 3:
                            ins.then_inc(S("proj_mm"), 1)
                    if q < 3:
                        ins.then_inc(S("pw_mm"), 1)

            def heads0():
                pe.wait_ge(S("proj_c"), 3 * NT)
                wq = landed(pe, "uq")
                wkv = landed(pe, "ukv")
                for t in range(NT):
                    pe.wait_ge(S("qk_n"), t + 1)
                    if t:
                        pe.wait_ge(S("heads_c"), 5 * t)
                    for h in range(4):
                        ins = tp(pb[2][:, h * P:h * P + P], proj[:, t, h * P:h * P + P], ident)
                    ins.then_inc(S("tp_a"), 1)
                    for i in range(2):
                        tp(pb[3][:, i * P:i * P + P], kdup[:, i].rearrange("p a e -> p (a e)"), ident)
                    for i in range(2):
                        tp(pb[3][:, (2 + i) * P:(3 + i) * P], proj[:, t, 768 + i * P:768 + i * P + P], ident)
                    for i in range(3):
                        ins = tp(pb[4][:, i * P:i * P + P], proj[:, t, 1024 + i * P:1024 + i * P + P], ident)
                    ins.then_inc(S("tp_a"), 1)
                    pe.wait_ge(S("lat_c"), 3 * (t + 1))
                    for c in range(2):
                        for k in range(3):
                            ins = mm(pb[5 + c][:, 0:384], latT[:, k, :], wq[:, k, c * 384:c * 384 + 384],
                                     start=(k == 0), stop=(k == 2))
                    ins.then_inc(S("up_mm"), 1)
                    for c in range(2):
                        for k in range(2):
                            ins = mm(pb[(7, 0)[c]][:, :], latT[:, 3 + k, :], wkv[:, k, c * 512:c * 512 + 512],
                                     start=(k == 0), stop=(k == 1))
                    ins.then_inc(S("up_mm"), 1)
                    pe.wait_ge(S("heads_c"), 5 * t + 1)
                    pe.wait_ge(S("qb_r"), t + 1)
                    for h in range(HEADS):
                        ins = tp(pb[2 + h // 4][0:QKB, (h % 4) * P:(h % 4) * P + P], qbt[:, t % 2, h, :], ident)
                        if h % 4 == 3:
                            ins.then_inc(S("tp_b"), 1)
                    pe.wait_ge(S("kb_r"), t + 1)
                    for h in range(HEADS):
                        ins = tp(pb[(4, 1)[h // 4]][0:QKB, (h % 4) * P:(h % 4) * P + P], kbt[:, t % 2, h, :], ident)
                        if h % 4 == 3:
                            ins.then_inc(S("tp_b"), 1)

            def attention(units, base, p_sb, pT_sb, beside=lambda u: None):
                n = len(units)
                for u in range(base, base + n + 2):
                    if u < base + n:
                        kind, h, t, k0, nk = units[u - base]
                        if u >= 2:
                            pe.wait_ge(S("p_exp"), u - 1)
                        if kind == "a":
                            o = HD * (h % 2)
                            q, k = qTa[o:o + HD, h // 2, t * P:t * P + P], kTa[o:o + HD, h // 4, k0:k0 + nk]
                        elif kind == "b":
                            q, k = qTb[0:QKB, h, t * P:t * P + P], kTb[0:QKB, h, k0:k0 + nk]
                        else:
                            o = HD * (h % 2)
                            q, k = qnT[o:o + HD, h // 2, t * P:t * P + P], knT[o:o + HD, h // 2, :]
                        ins = mm(pb[u % 2][:, 0:nk], q, k, start=True, stop=(kind != "n"))
                        if kind == "n":
                            ins = mm(pb[u % 2][:, 0:SEQ], flip, bias[:, 2 * h + t, :], start=False, stop=True)
                        ins.then_inc(S("s_mm"), 1)
                    if base + 1 <= u <= base + n:
                        v = u - 1
                        _, h, t, k0, nk = units[v - base]
                        pe.wait_ge(S("p_exp"), v + 1)
                        if v >= 2:
                            pe.wait_ge(S("pT_c"), v - 1)
                        for i in range(nk // P):
                            ins = tp(pb[2 + v % 2][:, i * P:i * P + P], p_sb[:, v % 2, i * P:i * P + P], ident)
                        ins.then_inc(S("p_t"), 1)
                    if u >= base + 2:
                        v = u - 2
                        kind, h, t, k0, nk = units[v - base]
                        pe.wait_ge(S("pT_c"), v + 1)
                        if v >= 2:
                            pe.wait_ge(S("o_c"), v - 1)
                        for i in range(nk // P):
                            kt = k0 // P + i
                            o = HD * (h // 4)
                            val = va[:, kt, o:o + HD] if kind == "a" else (vb if kind == "b" else vn)[:, kt, h * HD:h * HD + HD]
                            ins = mm(pb[4 + v % 2][:, 0:HD], pT_sb[:, v % 2, i * P:i * P + P], val,
                                     start=(i == 0), stop=(i == nk // P - 1))
                        ins.then_inc(S("o_mm"), 1)
                    beside(u)

            def out_t(tiles, src, done, base):
                pe.wait_ge(S(done[0]), done[1])
                for t in range(tiles):
                    for half in range(2):
                        g = base + 2 * t + half
                        if g >= 2:
                            pe.wait_ge(S("oT_c"), g - 1)
                        for q in range(4):
                            k = 4 * half + q
                            ins = tp(pb[6 + g % 2][:, q * P:q * P + P], src[:, t, k * P:k * P + P], ident)
                        ins.then_inc(S("oT_t"), 1)

            def gates(streams, n):
                for s in range(streams):
                    for half in range(2):
                        g = n + 2 * s + half
                        pe.wait_ge(S("dg"), g + 1)
                        if g >= 2:
                            pe.wait_ge(S("gb_c"), g - 1)
                        mm(pb[6 + g % 2][:, :], ones, diag[:, g % 2, :], start=True, stop=True).then_inc(S("gb_mm"), 1)

            def out_proj(name, tiles, src, base, ready):
                w = [landed(pe, name, c) for c in range(2)]
                pe.wait_ge(S(ready[0]), ready[1])
                for t in range(tiles):
                    if t >= 2:
                        pe.wait_ge(S("y_c"), base + t - 1)
                    for c in range(2):
                        for k in range(DK):
                            ins = mm(pb[2 * (t % 2) + c][:, :], src[:, k, t * P:t * P + P], w[c][:, k, :],
                                     start=(k == 0), stop=(k == DK - 1))
                    ins.then_inc(S("y_mm"), 1)

            def ffn0():
                lows = ff_units(F32R)

                def down(u, lo, t):
                    k, r = u - U0, slice(t * P, t * P + P)
                    for c in range(2):
                        f = slice(c * 512, c * 512 + 512)
                        ins = split_mm(pb[2 * t + c][:, :], (aH0[:, k % 8, r], aL0[:, k, r]),
                                       (fwH[u % 3][:, f], lo[:, f]), k == 0, k == FK - 1)
                    return ins

                pe.wait_ge(S("h_lo"), TMB[2])
                for u, (name, lo) in enumerate(lows):
                    pe.wait_ge(S("fw_lo"), u + 1)
                    if u < U0:
                        g, o = u // 2, 2 * (u % 2)
                        if g >= 2 and o == 0:
                            pe.wait_ge(S("ff_a"), g - 1)
                        hi = fwH[u % 3].rearrange("p (k f) -> p k f", k=DK)
                        for k in range(DK):
                            ins = split_mm(pb[o + g % 2][:, :], (hi[:, k, :], lo[:, k, :]), (hH[1][:, k, :], hL[:, k, :]),
                                           k == 0, k == DK - 1)
                        ins.then_inc(S("fw_mm"), 1)
                        continue
                    k = u - U0
                    if k == 0:
                        pe.wait_ge(S("ff_a"), FK)
                        pe.wait_ge(S("gb_c"), 8)
                    pe.wait_ge(S("a0_lo"), k + 1)
                    if k < FK - 3:
                        for t in range(NT):
                            ins = down(u, lo, t)
                        ins.then_inc(S("fw_mm"), 1)
                for t in range(NT):
                    for u in range(U0 + FK - 3, U0 + FK):
                        ins = down(u, lows[u][1], t)
                    ins.then_inc(S("y_mm"), 1)

            def proj1():
                pe.wait_ge(S("h_lo"), TMB[3])
                for u, (c, q, lo) in enumerate(in1_units(F32R)):
                    m = u // 4
                    hi = in1_hi(u)
                    pe.wait_ge(S("in1_lo"), u + 1)
                    if c not in TOKEN_MAJOR:
                        n = SEQ if c in (0, 3) else TOK
                        if m >= 2:
                            pe.wait_ge(S("in1_c"), 4 * (m - 2) + q + 1)
                        for k in range(DK):
                            ins = split_mm(pb[4 * (m % 2) + q][:, 0:n], (hi[:, k, :], lo[:, k, :]),
                                           (hH[2][:, k, 0:n], hL[:, k, 0:n]), k == 0, k == DK - 1)
                        ins.then_inc(S("in1_mm"), 1)
                        continue
                    for t in range(NL if c == 7 else NT):
                        if m >= 2 and q == 0:
                            pe.wait_ge(S("in1_c"), 4 * (m - 2) + t + 1)
                        for k in range(2):
                            kk, r = 2 * q + k, slice(t * P, t * P + P)
                            ins = split_mm(pb[4 * (m % 2) + t][:, :], (hH[2][:, kk, r], hL[:, kk, r]),
                                           (hi[:, k, :], lo[:, k, :]), kk == 0, kk == DK - 1)
                        if q == 3:
                            ins.then_inc(S("in1_mm"), 1)
                    if q < 3:
                        ins.then_inc(S("in1_rows"), 1)

            def hgrn():
                for d in range(2):
                    pe.wait_ge(S("kend"), d + 1)
                    pe.wait_ge(S("o_c"), NU + NU1)
                    if d:
                        pe.wait_ge(S("kend_c"), 2)
                        pe.wait_ge(S("state_c"), 1)
                    for i in range(2):
                        for h in range(HGH):
                            ins = tp(pb[i][:, h * P:h * P + P], W[d][:, h, i * P:i * P + P], ident)
                        ins.then_inc(S("kend_t"), 1)
                    pe.wait_ge(S("kend_c"), 2 * d + 2)
                    for h in range(HGH):
                        for i in range(2):
                            ins = mm(pb[2][:, h * P:h * P + P], kendT[:, i, h, :], vd[:, NL + i, h * P:h * P + P],
                                     start=(i == 0), stop=(i == 1))
                    ins.then_inc(S("state_mm"), 1)
                pe.wait_ge(S("ksum"), 1)
                for i in range(NL):
                    for h in range(HGH):
                        c = slice(i * P, i * P + P)
                        ins = mm(pb[4 + i][:, h * P:h * P + P], ksum[:, h, c], qd[:, h, c], start=True, stop=True)
                ins.then_inc(S("same_mm"), 1)
                pe.wait_ge(S("state_c"), 2)
                for n, (m, d) in enumerate(levels):
                    pe.wait_ge(S("hg_w"), n + 1)
                    if n >= 2:
                        pe.wait_ge(S("hg_at"), n - 1)
                    for i in range(1 if m == P else NL):
                        for h in range(HGH):
                            w = W[n % 2][:, h]
                            if m == P:
                                a, b = (w[:, 0:P], w[:, P:SEQ]) if d == 0 else (w[:, P:SEQ], w[:, 0:P])
                            else:
                                a = b = w[:, i * P:i * P + P]
                            ins = mm(pb[2 * (n % 2) + i][:, h * P:h * P + P], a, b, start=True, stop=True)
                    ins.then_inc(S("hg_mm"), 1)
                pe.wait_ge(S("hg_at"), len(levels))
                pe.wait_ge(S("qx"), 2)
                for t in range(NL):
                    c = slice(t * P, t * P + P)
                    for h in range(HGH):
                        f = slice(h * P, h * P + P)
                        terms = [(AT[:, i, h, c], vd[:, i, f]) for i in range(NL)]
                        terms += [(qxf[:, h, c], state[:, 0, h, :]), (qxb[:, h, c], state[:, 1, h, :])]
                        for i, (a, b) in enumerate(terms):
                            ins = mm(pb[6 + t][:, f], a, b, start=(i == 0), stop=(i == 3))
                    ins.then_inc(S("hg_o"), 1)

            def route():
                pe.wait_ge(S("hT_half"), TMB[4])
                pe.wait_ge(S("c1_in"), 48)
                pe.wait_ge(S("gb_c"), 10)
                for t in range(NL):
                    for k in range(DK):
                        ins = mm(pb[6][:, t * NE:t * NE + NE], hT[:, k, t * P:t * P + P], router[:, k, :],
                                 start=(k == 0), stop=(k == DK - 1))
                ins.then_inc(S("logit_mm"), 1)
                pe.wait_ge(S("mask_r"), 1)
                m = rt[5]
                mm(pb[7][:, 0:8], upper, m[:, 0, :], start=True, stop=True)
                mm(pb[7][:, 8:16], upper, m[:, 1, :], start=True, stop=False)
                mm(pb[7][:, 8:16], ones, m[:, 0, :], start=False, stop=True)
                mm(pb[7][:, 16:24], ones, m[:, 0, :], start=True, stop=False)
                mm(pb[7][:, 16:24], ones, m[:, 1, :], start=False, stop=True).then_inc(S("pos_mm"), 1)

            def gather_half(r, half):
                pe.wait_ge(S("sel_r"), r + 1)
                if not (isinstance(r, int) and r == 0 and half == 0):
                    pe.wait_ge(S("bank7"), r * 3 + half)
                for q in range(4):
                    k = 4 * half + q
                    for t in range(NL):
                        ins = mm(pb[7][:, q * P:q * P + P], xr[:, t, k * P:k * P + P], sel[:, t, :],
                                 start=(t == 0), stop=(t == NL - 1))
                ins.then_inc(S("g_mm"), 1)

            def scatter(r, n, t):
                pe.wait_ge(S("y_s"), 2 * n + 2)
                pe.wait_ge(S("bank7"), r * 3 + 2)
                if t:
                    pe.wait_ge(S("sc_a"), 4 * n + 2)
                for c in range(2):
                    mm(pb[4 + c][:, :], selGT[:, t * P:t * P + P], y_e[:, 512 * c:512 * c + 512],
                       start=True, stop=True).then_inc(S("sc_mm"), 1)

            def expert(r, n):
                def unit(j, q):
                    u = 4 * j + q
                    if q == POOLQ:
                        pe.wait_ge(S("w_lo_g"), r * 21 + j + 1)
                    else:
                        pe.wait_ge(S("w_lo"), r * 63 + 3 * j + q - (q > POOLQ) + 1)
                    return wH[u % HBUF], part(slot[j % RING] + UNIT * q, UNIT)

                def transposed(c):
                    pe.wait_ge(S("e_a"), r * 7 + c + 1 + OPEN)
                    pe.wait_ge(S("e_aT"), r * 7 + c + OPEN)
                    for q in range(4):
                        ins = tp(pb[6][:, q * P:q * P + P], s_e[:, c % 2, q * P:q * P + P], ident)
                    ins.then_inc(S("e_t"), 1)

                pe.wait_ge(S("hs_r"), r + 1)
                for c in range(7):
                    pe.wait_ge(S("e_a"), r * 7 + max(c - 1, 0) + OPEN)
                    for i in range(2):
                        for q in range(4):
                            h, l = unit(2 * c + i, q)
                            for k in range(2):
                                f = slice(512 * k, 512 * k + 512)
                                kk = 2 * q + k
                                ins = split_mm(pb[2 * i + c % 2][:, :], (hsH[:, kk, :], hsL[:, kk, :]), (h[:, f], l[:, f]),
                                               kk == 0, kk == DK - 1)
                            ins.then_inc(S("unit_mm"), 1)
                    if c < 2:
                        scatter(r, n, c)
                    if c >= 1:
                        transposed(c - 1)
                    if c == 2:
                        pe.wait_ge(S("selg"), r + 1)
                        pe.wait_ge(S("bank7"), r * 3 + 2)
                        for t in range(NL):
                            ins = tp(pb[7][:, t * P:t * P + P], selG[:, t, :], ident)
                        ins.then_inc(S("sg_t"), 1)
                    if c == 3:
                        gather_half(r + 1, 0)
                    if c == 4:
                        gather_half(r + 1, 1)
                pe.wait_ge(S("sc_a"), 4 * n + 4)
                for d in range(7):
                    pe.wait_ge(S("e_aT"), r * 7 + d + 1 + OPEN)
                    for q in range(4):
                        h, l = unit(14 + d, q)
                        for c in range(2):
                            f = slice(512 * c, 512 * c + 512)
                            k = 4 * d + q
                            ins = split_mm(pb[4 + c][:, :], (aH[:, k, :], aL[:, k, :]), (h[:, f], l[:, f]),
                                           k == 0, k == EK - 1)
                        ins.then_inc(S("unit_mm"), 1)
                    if d == 1:
                        transposed(6)

            setup()
            ada(0, 0, 12)
            transpose_in(0, NT)
            proj0()
            heads0()
            pe.wait_ge(S("heads_c"), 5 * NT)
            pe.wait_ge(S("s_lo"), 2)
            attention(units, 0, p_sb, pT_sb, ada_beside)
            out_t(NT, oA, ("o_c", NU), 0)
            pe.wait_ge(S("oT_c"), 2 * NT)
            gates(2, 0)
            out_proj("evout", NT, oT, 0, ("oT_c", 2 * NT))
            ada(1, 12 + ADA_ATT, 24)
            pe.wait_ge(S("mod_row"), 24)
            transpose_in(1, NT)
            gates(2, 4)
            ffn0()
            transpose_in(2, NT)
            proj1()
            pe.wait_ge(S("in1_c"), len(in1))
            pe.wait_ge(S("bias_r"), 1)
            attention(units1, NU, p1, pT1)
            hgrn()
            out_t(NL, o1, ("y_hg", NL), 2 * NT)
            pe.wait_ge(S("oT_c"), 2 * NT + 2 * NL)
            gates(1, 8)
            out_proj("odout", NL, oT1, 2 * NT, ("oT_c", 2 * NT + 2 * NL))
            transpose_in(3, NL)
            route()
            pe.wait_ge(S("mask_r"), 1)
            gather_half(0, 0)
            gather_half(0, 1)
            for name in ("sg_t", "e_t"):
                pe.sem_inc(S(name), OPEN)
            pe.sem_inc(S("unit_mm"), HBUF)
            with pe.Fori(0, NE) as r:
                expert(r, r)
            for t in range(NL):
                scatter(NE, NE, t)
            pe.wait_ge(S("routed"), 1)
            many = pe.value_load(nover[0:1, :], min_val=0, max_val=EXTRA)
            with pe.If(many > 0):
                with pe.Fori(NE, ROUNDS) as r:
                    expert(r, r + 1)
                for t in range(NL):
                    scatter(ROUNDS, ROUNDS + 1, t)
            gates(1, 10)

        @block.scalar
        def _(act):
            link = chain(act, "act_done")
            fn = nc.scalar.activation

            def copy(out_, in_):
                return fn(out_, in_, ACT.Copy)

            def setup():
                act.wait_ge(S("vec_c"), 1)
                fn(sT, vcol[:, 64:80], ACT.Silu).then_inc(S("silu_c"), 1)
                act.wait_ge(S("silu_c"), 1)
                for x in (s_hl, s_h0):
                    copy(x[:, :, 0:2], sT.rearrange("p (s k) -> p k s", s=2)).then_inc(S("s_hi"), 1)

            def ada(first, last):
                for i in range(first, last):
                    act.wait_ge(S("mod_mm"), i + 1)
                    if i >= 2:
                        act.wait_ge(S("mod_t"), i - 1)
                    copy(rowbuf[0:2, i % 2, :], pb[4 * (i // 12) + i % 2][0:2, :]).then_inc(S("mod_row"), 1)

            def modulate(n, tiles, first=0):
                for t in range(first, tiles):
                    s = t // NL
                    for half in range(2):
                        g = TMB[n] + 2 * t + half
                        act.wait_ge(S("tm_t"), g + 1)
                        if n == 0:
                            act.wait_ge(S("mod_col"), 4)
                        else:
                            act.wait_ge(S("ab_r"), n)
                        for q in range(4):
                            k = 4 * half + q
                            if n == 0:
                                a, b = modT[:, 0, 8 + k, s:s + 1], modT[:, 0, k, s:s + 1]
                            else:
                                a, b = (AB[:, n - 1, i, 2 * k + s:2 * k + s + 1] for i in range(2))
                            ins = fn(hT[:, k, t * P:t * P + P], pb[TBANK[n] + g % 2][:, q * P:q * P + P], ACT.Identity,
                                     bias=b, scale=a)
                        ins.then_inc(S("hT_half"), 1)
                        if n < 3:
                            part_of = (slice(None), slice(4 * half, 4 * half + 4), slice(t * P, t * P + P))
                            act.wait_ge(S("hT_half"), g + 1)
                            copy(hH[n][part_of], hT[part_of]).then_inc(S("h_hi"), 1)

            def proj0():
                units = evin_units()
                for u in range(len(units) + 4):
                    if u >= 4:
                        i, q = units[u - 4][0:2]
                        if q < 3:
                            act.wait_ge(S("pw_mm"), 3 * i + q + 1)
                        else:
                            a, b = EVC[i]
                            for t in range(NT):
                                act.wait_ge(S("proj_mm"), NT * i + t + 1)
                                copy(proj[:, t, a:b], pb[4 * (i % 2) + t][:, 0:b - a]).then_inc(S("proj_c"), 1)
                    if u < len(units):
                        _, q, name, w = units[u]
                        if q == 0:
                            landed(act, *name)
                        n = w.shape[2]
                        copy(pwH[u % 4][:, 0:2 * n].rearrange("p (k n) -> p k n", k=2), w).then_inc(S("pw_hi"), 1)
                act.wait_ge(S("proj_c"), 3 * NT)
                for t in range(NT):
                    copy(va[:, t, :], proj[:, t, 640:768]).then_inc(S("va_c"), 1)

            def heads0():
                def root_mean(t):
                    act.wait_ge(S("ssq"), t + 1)
                    fn(ssq[:, t, 0:12], ssq[:, t, 0:12], ACT.Sqrt).then_inc(S("rms"), 1)
                root_mean(0)
                root_mean(1)
                for t in range(NT):
                    tile = slice(t * P, t * P + P)
                    act.wait_ge(S("tp_a"), 2 * t + 1)
                    copy(qTa[:, :, tile], pb[2].rearrange("p (h c) -> p h c", h=4)).then_inc(S("heads_c"), 1)
                    act.wait_ge(S("up_mm"), 2 * t + 1)
                    for c in range(2):
                        copy(qbt[:, t % 2, 4 * c:4 * c + 4, :], pb[5 + c][:, 0:384].rearrange("p (h c) -> p h c", h=4))\
                            .then_inc(S("qb_c"), 1)
                    act.wait_ge(S("up_mm"), 2 * t + 2)
                    for c in range(2):
                        bank = pb[(7, 0)[c]].rearrange("p (h c) -> p h c", h=4)
                        copy(kbt[:, t % 2, 4 * c:4 * c + 4, 0:NOPE], bank[:, :, 0:NOPE]).then_inc(S("kb_c"), 1)
                        copy(vb[:, t, 256 * c:256 * c + 256].rearrange("p (h c) -> p h c", h=4), bank[:, :, NOPE:])\
                            .then_inc(S("kb_c"), 1)
                    if t + 2 < NT:
                        root_mean(t + 2)
                    for c, (b, dst) in enumerate(((2, qTb), (3, qTb), (4, kTb), (1, kTb))):
                        act.wait_ge(S("tp_b"), 4 * t + c + 1)
                        h = 4 * (c % 2)
                        copy(dst[0:QKB, h:h + 4, tile], pb[b][0:QKB, :].rearrange("p (h c) -> p h c", h=4))\
                            .then_inc(S("heads_c"), 1)

            def ada_beside(u):
                for q in range(4):
                    i = ada_step.get(("hi", u, q))
                    if i is not None:
                        if i >= 2:
                            sem, value = ada_used(i - 2)
                            act.wait_ge(sem, value)
                        landed(act, "ada", 1, i // 4)
                        copy(awH[i % 2], ada_units()[i]).then_inc(S("ada_hi"), 1)
                j = ada_step.get(("row", u))
                if j is not None:
                    act.wait_ge(S("mod_mm"), 12 + j + 1)
                    act.wait_ge(S("mod_t"), 12 + j - 1)
                    copy(rowbuf[0:4, j % 2, :], pb[6][0:4, :]).then_inc(S("mod_row"), 1)

            def attention(units, base, p_sb, pT_sb, beside=lambda u: None):
                n = len(units)
                for u in range(n + 1):
                    g = base + u
                    if u < n:
                        act.wait_ge(S("mx_r"), g + 1)
                        if u >= 2:
                            act.wait_ge(S("p_t"), g - 1)
                        nk = units[u][4]
                        fn(p_sb[:, g % 2, 0:nk], pb[g % 2][:, 0:nk], ACT.Exp, bias=mx[:, g % 4, 1:2],
                           scale=scale_of[units[u][0]], accum_out=mx[:, g % 4, 2:3]).then_inc(S("p_exp"), 1)
                    if u >= 1:
                        v = g - 1
                        act.wait_ge(S("p_t"), v + 1)
                        if u >= 3:
                            act.wait_ge(S("o_mm"), v - 1)
                        nk = units[u - 1][4]
                        copy(pT_sb[:, v % 2, 0:nk], pb[2 + v % 2][:, 0:nk]).then_inc(S("pT_c"), 1)
                    beside(u)

            def out_t(tiles, dst, base):
                for t in range(tiles):
                    for half in range(2):
                        g = base + 2 * t + half
                        act.wait_ge(S("oT_t"), g + 1)
                        copy(dst[:, 4 * half:4 * half + 4, t * P:t * P + P],
                             pb[6 + g % 2].rearrange("p (k c) -> p k c", k=4)).then_inc(S("oT_c"), 1)

            def gates(streams, n, y_read):
                if y_read:
                    act.wait_ge(S("y_c"), y_read)
                for g in range(n, n + 2 * streams):
                    s, half = (g - n) // 2, g % 2
                    act.wait_ge(S("gb_mm"), g + 1)
                    copy(gb[:, s, 512 * half:512 * half + 512], pb[6 + g % 2][:, :]).then_inc(S("gb_c"), 1)

            def root(base, t):
                act.wait_ge(S("var_r"), base + t + 1)
                fn(lnst[:, t, 14:15], lnst[:, t, 13:14], ACT.Sqrt, bias=eps_c).then_inc(S("std_r"), 1)

            def ffn0():
                units = ff_units()
                for u in range(len(units) + 2):
                    if u % 2 == 0 and 4 <= u <= U0 + 2:
                        g = (u - 4) // 2
                        act.wait_ge(S("fw_mm"), 2 * g + 1)
                        if g >= 2:
                            act.wait_ge(S("ff_a"), g - 1)
                        fn(sil[:, g % 2, :], pb[g % 2][:, :], ACT.Silu).then_inc(S("ff_s"), 1)
                    if u >= U0 + 2:
                        k = u - U0 - 2
                        act.wait_ge(S("ff_a"), k + 1)
                        act.wait_ge(S("fw_mm"), U0 + max(k - 7, 0))
                        copy(aH0[:, k % 8, :], aT0[:, k, :]).then_inc(S("a0_hi"), 1)
                    if u < len(units):
                        name, w = units[u]
                        landed(act, *name)
                        if u >= 3:
                            act.wait_ge(S("fw_mm"), u - 2)
                        hi = fwH[u % 3].rearrange("p (k f) -> p k f", k=DK) if u < U0 else fwH[u % 3]
                        copy(hi, w).then_inc(S("fw_hi"), 1)

            def lower_bound():
                act.wait_ge(S("lb_s"), 1)
                fn(lbs[:, 0], lbs[:, 0], ACT.Exp).then_inc(S("lb_e"), 1)

            def proj1():
                def product(g, c, i):
                    act.wait_ge(S("in1_mm"), g + 1)
                    b = pb[4 * (ORDER1.index(c) % 2) + i]
                    if c == 0:
                        ins = fn(qnT[:, i, :], b[:, 0:SEQ], ACT.Copy, scale=HD ** -0.5)
                    elif c == 1:
                        ins = copy(knT[:, i, :], b[:, :])
                    elif c == 2:
                        ins = copy(vn[:, i, :], b[:, :])
                    elif c == 3:
                        ins = fn(qd[:, i, :], b[:, 0:SEQ], ACT.Silu)
                    elif c == 4:
                        ins = copy(vd[:, i, :], b[:, :])
                    elif c == 7:
                        ins = fn(gd[:, i, :], b[:, :], ACT.Silu)
                    else:
                        d = c - 5
                        if d == 1 and i == 0:
                            act.wait_ge(S("cum_r"), 1)
                        fn((kf, kb)[d][:, i, :], b[:, :], ACT.Sigmoid, scale=-1.0).then_inc(S("sig"), 1)
                        fn(forget[:, i, :], b[:, :], ACT.Sigmoid).then_inc(S("sig"), 1)
                        ins = None
                    if ins is None:
                        act.wait_ge(S("sig"), 8 * (c - 5) + 2 * i + 2)
                        act.sem_inc(S("in1_c"), 1)
                        if i == 3:
                            act.wait_ge(S("f_r"), c - 4)
                            fn(forget, forget, ACT.Ln).then_inc(S("ln_f"), 1)
                    else:
                        ins.then_inc(S("in1_c"), 1)

                units = in1_units()
                act.wait_ge(S("x_ln"), NT + NL)
                g = 0
                for u in range(len(units) + 2):
                    if u < len(units):
                        if u >= 2:
                            sem, value = in1_done(u - 2)
                            act.wait_ge(sem, value)
                        landed(act, "odin", units[u][0])
                        copy(in1_hi(u), units[u][2]).then_inc(S("in1_hi"), 1)
                    while g < len(in1) and u >= 2 and in1_at[g] <= u - 2:
                        product(g, *in1[g])
                        g += 1

            def hgrn():
                act.wait_ge(S("cum_r"), 2)
                for h in range(HGH):
                    c = cum[0][:, 1, h]
                    ins = fn(W[0][:, h, :], c[:, 1:CW], ACT.Exp, bias=c[:, SEQ:CW], scale=-1.0)
                ins.then_inc(S("kend_e"), 1)
                fn(W[1], cum[1][:, 1, :, 0:SEQ], ACT.Exp).then_inc(S("kend_e"), 1)
                act.wait_ge(S("o_c"), NU + NU1)
                fn(qxf, cum[0][:, 0, :, 1:CW], ACT.Exp).then_inc(S("qx_e"), 1)
                for h in range(HGH):
                    c = cum[1][:, 0, h]
                    ins = fn(qxb[:, h, :], c[:, 0:SEQ], ACT.Exp, bias=c[:, SEQ:CW], scale=-1.0)
                ins.then_inc(S("qx_e"), 1)
                for d in range(2):
                    for i in range(2):
                        act.wait_ge(S("kend_t"), 2 * d + i + 1)
                        if d:
                            act.wait_ge(S("state_mm"), 1)
                        copy(kendT[:, i].rearrange("p h c -> p (h c)"), pb[i][:, :]).then_inc(S("kend_c"), 1)
                    act.wait_ge(S("state_mm"), d + 1)
                    copy(state[:, d].rearrange("p h c -> p (h c)"), pb[2][:, :]).then_inc(S("state_c"), 1)
                for n, (m, d) in enumerate(levels):
                    act.wait_ge(S("hg_sub"), n + 1)
                    w = W[n % 2].rearrange("p h (b m) -> p (h b) m", m=2 * m)
                    for i, o in enumerate((slice(0, m), slice(m, 2 * m))):
                        ins = fn(w[:, :, o], w[:, :, o], ACT.Exp, scale=(-1.0, 1.0)[i])
                    ins.then_inc(S("hg_exp"), 1)
                for t in range(NL):
                    act.wait_ge(S("hg_ss"), t + 1)
                    fn(rms1[:, t, :], rms1[:, t, :], ACT.Sqrt).then_inc(S("hg_rt"), 1)

            def hs_copy(r, half, quarters=(0, 1, 2, 3)):
                if quarters[0] == 0:
                    act.wait_ge(S("g_mm"), r * 2 + half + 1)
                for q in quarters:
                    k = 4 * half + q
                    ins = fn(hsN[:, k, :], pb[7][:, q * P:q * P + P], ACT.Identity,
                             bias=AB[:, 2, 1, 2 * k:2 * k + 1], scale=AB[:, 2, 0, 2 * k:2 * k + 1])
                if quarters[-1] == 3:
                    ins.then_inc(S("bank7"), 1)

            def outputs(r):
                act.wait_ge(S("unit_mm"), r * UNITS + HBUF)
                act.wait_ge(S("hs_r"), r + 1)
                for c in range(2):
                    copy(y_e[:, 512 * c:512 * c + 512], pb[4 + c][:, :]).then_inc(S("y_s"), 1)

            def expert(r):
                for u in range(UNITS):
                    j, q = u // 4, u % 4
                    s = j % RING
                    if q == 0:
                        act.wait_ge(S(f"w_landed{s}"), r * 48 + 16 * (base_n[s] + j // RING + 1))
                    act.wait_ge(S("unit_mm"), r * UNITS + u + 1)
                    copy(wH[u % HBUF], at(slot[s] + UNIT * q, UNIT)).then_inc(S("w_hi"), 1)
                    if u == 3:
                        outputs(r)
                    c, step = (u - 12) // 8, (u - 12) % 8
                    if step == 0 and 0 <= c < 7:
                        act.wait_ge(S("unit_mm"), r * UNITS + 8 * c + 8 + HBUF)
                        act.wait_ge(S("e_t"), r * 7 + max(c - 1, 0) + OPEN)
                        fn(s_e[:, c % 2, :], pb[c % 2][:, :], ACT.Silu).then_inc(S("e_s"), 1)
                    if step == 2 and 1 <= c < 8:
                        act.wait_ge(S("e_t"), r * 7 + c + OPEN)
                        if c == 1:
                            act.wait_ge(S("unit_mm"), r * UNITS + HBUF)
                        copy(aH[:, 4 * c - 4:4 * c, :].rearrange("p k c -> p (k c)"), pb[6][:, :])\
                            .then_inc(S("e_aH"), 1)
                    if step == 1 and c == 2:
                        act.wait_ge(S("sg_t"), r + 1 + OPEN)
                        copy(selGT, pb[7][:, 0:SEQ]).then_inc(S("bank7"), 1)
                    if c in (3, 4) and step in (1, 3):
                        hs_copy(r + 1, c - 3, (0, 1) if step == 1 else (2, 3))
                    if step == 4 and c == 6:
                        act.wait_ge(S("bank7"), r * 3 + 5)
                        copy(hsH, hsN).then_inc(S("hs_h"), 1)

            setup()
            ada(0, 12)
            modulate(0, NT)
            proj0()
            heads0()
            act.wait_ge(S("tp_b"), 4 * NT)
            ada_beside(-1)
            attention(units, 0, p_sb, pT_sb, ada_beside)
            out_t(NT, oT, 0)
            gates(2, 0, 0)
            for t in range(NT):
                root(0, t)
            ada(12 + ADA_ATT, 24)
            modulate(1, NT)
            gates(2, 4, NT)
            ffn0()
            for t in range(NT):
                root(NT, t)
                if t:
                    modulate(2, t, t - 1)
            modulate(2, NT, NT - 1)
            lower_bound()
            proj1()
            attention(units1, NU, p1, pT1)
            hgrn()
            out_t(NL, oT1, 2 * NT)
            gates(1, 8, 0)
            for t in range(NL):
                root(2 * NT, t)
            modulate(3, NL)
            act.wait_ge(S("top_r"), 1)
            fn(r1[:, 2, :], r1[:, 2, :], ACT.Exp).then_inc(S("top_e"), 1)
            hs_copy(0, 0)
            hs_copy(0, 1)
            act.wait_ge(S("bank7"), 2)
            act.wait_ge(S("gb_mm"), 10)
            copy(hsH, hsN).then_inc(S("hs_h"), 1)
            act.wait_ge(S("logit_mm"), 1)
            act.wait_ge(S("y_zero"), 2)
            with act.Fori(0, NE) as r:
                expert(r)
            outputs(NE)
            act.wait_ge(S("routed"), 1)
            many = act.value_load(nover[0:1, :], min_val=0, max_val=EXTRA)
            with act.If(many > 0):
                act.wait_ge(S("y_zero"), 4)
                with act.Fori(NE, ROUNDS) as r:
                    expert(r)
                outputs(ROUNDS)
            gates(1, 10, 2 * NT + NL)
            for t in range(NL):
                root(2 * NT + NL, t)

        @block.vector
        def _(dve):
            link = chain(dve, "dve_done")
            v = nc.vector

            def setup():
                link(v.memset(eps_c, 1e-6))
                dve.wait_ge(S("vec_t"), 1)
                v.tensor_copy(vcol, pb[5][:, 0:88]).then_inc(S("vec_c"), 1)
                link(v.tensor_copy(adab, pb[4][:, 0:96]))
                cols = adab.rearrange("p (l c k) -> p l c k", l=DEPTH, c=6)
                link(v.tensor_scalar(cols[:, :, 1], cols[:, :, 1], 1.0, None, ALU.add))
                v.tensor_scalar(cols[:, :, 4], cols[:, :, 4], 1.0, None, ALU.add).then_inc(S("vec_c"), 1)
                dve.wait_ge(S("vec_c"), 2)

            def ada(first, last):
                for i in range(first, last):
                    ada_column(i, pb[4 * (i // 12) + 2 + i % 2])

            def rope(x, n, rot, cos, sin, t1, t2):
                half = rot // 4
                link(v.tensor_tensor(t1, x, bc(cos.unsqueeze(1), P, n, rot), ALU.mult))
                xs = x.rearrange("p n (a b) -> p n a b", a=2)
                ts = t2.rearrange("p n (a b) -> p n a b", a=2)
                ss = sin.rearrange("p (a b) -> p a b", a=2)
                for i in range(2):
                    o, f = slice(i * half, i * half + half), slice((1 - i) * half, (1 - i) * half + half)
                    link(v.tensor_tensor(ts[:, :, :, o], xs[:, :, :, f], bc(ss[:, :, o].unsqueeze(1), P, n, 2, half),
                                         ALU.mult))
                return v.tensor_tensor(x, t1, t2, ALU.add)

            def subtract(lo, x, hi):
                return v.tensor_tensor(lo, x, hi.bitcast(F32), ALU.subtract)

            def low_halves(n, first=0, last=NT):
                for g in range(TMB[n] + 2 * first, TMB[n] + 2 * last):
                    t, half = (g - TMB[n]) // 2, g % 2
                    piece = (slice(None), slice(4 * half, 4 * half + 4), slice(t * P, t * P + P))
                    dve.wait_ge(S("h_hi"), g + 1)
                    subtract(hL[piece], hT[piece], hH[n][piece]).then_inc(S("h_lo"), 1)

            def proj0():
                lows = evin_units(F32R)
                for u, (_, _, _, w) in enumerate(evin_units()):
                    dve.wait_ge(S("pw_hi"), u + 1)
                    n = w.shape[2]
                    subtract(lows[u][3], w, pwH[u % 4][:, 0:2 * n].rearrange("p (k n) -> p k n", k=2))\
                        .then_inc(S("pw_lo"), 1)

            def ffn0():
                units, lows = ff_units(), ff_units(F32R)
                for u in range(len(units) + 2):
                    if u % 2 == 0 and 4 <= u <= U0 + 2:
                        g = (u - 4) // 2
                        dve.wait_ge(S("ff_s"), g + 1)
                        dve.wait_ge(S("fw_mm"), 2 * g + 2)
                        v.tensor_tensor(aT0[:, g, :], sil[:, g % 2, :], pb[2 + g % 2][:, :], ALU.mult)\
                            .then_inc(S("ff_a"), 1)
                    if u >= U0 + 2:
                        k = u - U0 - 2
                        dve.wait_ge(S("a0_hi"), k + 1)
                        subtract(aL0[:, k, :], aT0[:, k, :], aH0[:, k % 8, :]).then_inc(S("a0_lo"), 1)
                    if u < len(units):
                        dve.wait_ge(S("fw_hi"), u + 1)
                        hi = fwH[u % 3].rearrange("p (k f) -> p k f", k=DK) if u < U0 else fwH[u % 3]
                        subtract(lows[u][1], units[u][1], hi).then_inc(S("fw_lo"), 1)

            def heads0():
                dve.wait_ge(S("g_in"), 80)

                def squares(t):
                    pt = proj[:, t]
                    dve.wait_ge(S("proj_c"), 2 * NT + t + 1)
                    link(v.tensor_tensor(sqj, pt[:, 0:640], pt[:, 0:640], ALU.mult))
                    link(v.tensor_reduce(ssq[:, t, 0:10], sqj.rearrange("p (h e) -> p h e", e=HD), AX.X, ALU.add))
                    link(v.tensor_scalar(ssq[:, t, 0:10], ssq[:, t, 0:10], 1.0 / HD, 1e-6, ALU.mult, ALU.add))
                    for i, (a, n) in enumerate(((768, QR), (1152, KVR))):
                        c = ssq[:, t, 10 + i:11 + i]
                        link(v.tensor_tensor_reduce(sqj[:, 0:n], pt[:, a:a + n], pt[:, a:a + n], 1.0, 0.0, ALU.mult,
                                                    ALU.add, c))
                        ins = v.tensor_scalar(c, c, 1.0 / n, 1e-6, ALU.mult, ALU.add)
                        if i == 0:
                            link(ins)
                    ins.then_inc(S("ssq"), 1)

                def normalise(t):
                    pt = proj[:, t]
                    r = ssq[:, t]
                    dve.wait_ge(S("rms"), t + 1)
                    link(v.reciprocal(r[:, 0:12], r[:, 0:12]))
                    qk = pt[:, 0:640].rearrange("p (h e) -> p h e", e=HD)
                    link(v.tensor_tensor(qk, qk, bc(r[:, 0:10].unsqueeze(2), P, 10, HD), ALU.mult))
                    link(v.tensor_tensor(qk, qk, gains, ALU.mult))
                    for i, (a, n, g) in enumerate(((768, QR, cqg), (1152, KVR, ckvg))):
                        link(v.scalar_tensor_tensor(out=pt[:, a:a + n], in0=pt[:, a:a + n],
                                                    scalar=r[:, 10 + i:11 + i], in1=g, op0=ALU.mult, op1=ALU.mult))
                    if t < NL:
                        t1, t2 = (x.rearrange("p (h e) -> p h e", e=HD) for x in (ropt[:, 0:640], sqj))
                        link(rope(qk, 10, HD, rope_c[:, t, 0:64], rope_c[:, t, 64:128], t1, t2))
                        link(rope(pt[:, 1408:1440].unsqueeze(1), 1, ROPE, rope_c[:, t, 128:160], rope_c[:, t, 160:192],
                                  ropt[:, 0:ROPE].unsqueeze(1), sqj[:, 0:ROPE].unsqueeze(1)))
                    v.tensor_copy(kdup, bc(pt[:, 512:640].rearrange("p (g e) -> p g e", g=KVH).unsqueeze(2), P, KVH, 2, HD))\
                        .then_inc(S("qk_n"), 1)

                def transposed(t):
                    dve.wait_ge(S("tp_a"), 2 * t + 2)
                    v.tensor_copy(kTa[:, :, t * P:t * P + P], pb[3][:, 0:256].rearrange("p (k c) -> p k c", k=2))\
                        .then_inc(S("lat_c"), 1)
                    v.tensor_copy(latT[:, 0:2, :], pb[3][:, 256:512].rearrange("p (k c) -> p k c", k=2))\
                        .then_inc(S("lat_c"), 1)
                    v.tensor_copy(latT[:, 2:5, :], pb[4][:, 0:384].rearrange("p (k c) -> p k c", k=3))\
                        .then_inc(S("lat_c"), 1)

                def rotate(t):
                    pt = proj[:, t]
                    dve.wait_ge(S("qb_c"), 2 * t + 2)
                    if t < NL:
                        link(rope(qbt[:, t % 2, :, NOPE:], HEADS, ROPE, rope_c[:, t, 128:160], rope_c[:, t, 160:192],
                                  ropt[:, 0:256].rearrange("p (h e) -> p h e", h=HEADS),
                                  sqj[:, 0:256].rearrange("p (h e) -> p h e", h=HEADS)))
                    dve.sem_inc(S("qb_r"), 1)
                    link(v.tensor_copy(kbt[:, t % 2, :, NOPE:], bc(pt[:, 1408:1440].unsqueeze(1), P, HEADS, ROPE)))
                    dve.wait_ge(S("kb_c"), 4 * t + 4)
                    dve.sem_inc(S("kb_r"), 1)

                squares(0)
                squares(1)
                normalise(0)
                for t in range(NT):
                    transposed(t)
                    if t + 1 < NT:
                        normalise(t + 1)
                    if t + 2 < NT:
                        squares(t + 2)
                    rotate(t)

            def ada_column(i, bank):
                L, j = i // 12, i % 12
                dve.wait_ge(S("mod_t"), i + 1)
                v.tensor_tensor(modT[:, L, 4 * j:4 * j + 4, :], bank[:, 0:8].rearrange("p (c s) -> p c s", s=2),
                                bc(adab[:, 48 * L + 4 * j:48 * L + 4 * j + 4].unsqueeze(2), P, 4, 2),
                                ALU.add).then_inc(S("mod_col"), 1)

            def ada_beside(u):
                j = ada_step.get(("add", u))
                if j is not None:
                    dve.wait_ge(S("mod_t"), 12 + j + 1)
                    m = modT[:, 1, 4 * j:4 * j + 4, :]
                    cols = pb[7][:, 0:16].rearrange("p (c s) -> p c s", s=4)
                    link(v.tensor_tensor(m, cols[:, :, 0:2], bc(adab[:, 48 + 4 * j:52 + 4 * j].unsqueeze(2), P, 4, 2),
                                         ALU.add))
                    v.tensor_tensor(m, m, cols[:, :, 2:4], ALU.add).then_inc(S("mod_col"), 1)

            def attention(units, base, col, beside=lambda u: None):
                n = len(units)
                for u in range(n + 2):
                    g = base + u
                    if u < n:
                        nk = units[u][4]
                        dve.wait_ge(S("s_mm"), g + 1)
                        link(v.tensor_reduce(mx[:, g % 4, 0:1], pb[g % 2][:, 0:nk], AX.X, ALU.max))
                        v.tensor_scalar(mx[:, g % 4, 1:2], mx[:, g % 4, 0:1], -scale_of[units[u][0]], None, ALU.mult)\
                            .then_inc(S("mx_r"), 1)
                    if u >= 2:
                        w = g - 2
                        unit = units[u - 2]
                        dve.wait_ge(S("o_mm"), w + 1)
                        dve.wait_ge(S("p_exp"), w + 1)
                        link(v.reciprocal(mx[:, w % 4, 3:4], mx[:, w % 4, 2:3]))
                        v.tensor_scalar(col(unit), pb[4 + w % 2][:, 0:HD], mx[:, w % 4, 3:4], None, ALU.mult)\
                            .then_inc(S("o_c"), 1)
                    beside(u)

            def gates(L, chunk, streams, n):
                for g in range(n, n + 2 * streams):
                    s, half = (g - n) // 2, g % 2
                    if g - n >= 2:
                        dve.wait_ge(S("gb_mm"), g - 1)
                    col = modT[:, L, 8 * chunk + 4 * half:8 * chunk + 4 * half + 4, s]
                    v.tensor_tensor(diag[:, g % 2, :].rearrange("p (q c) -> p q c", q=4), bc(ident.unsqueeze(1), P, 4, P),
                                    bc(col.unsqueeze(2), P, 4, P), ALU.mult).then_inc(S("dg"), 1)

            def layernorm(i, tiles, base, bank, between=lambda t: None):
                dve.wait_ge(S("gb_mm"), (4, 8, 10, 12)[i])
                dve.wait_ge(S("gb_c"), (4, 8, 10, 12)[i])
                ltb = lt if i < 3 else at(BB + 4096, 2, D)
                for t in range(tiles):
                    s = t // NL
                    if i < 3:
                        dve.wait_ge(S("y_mm"), base + t + 1)
                    for c in range(2):
                        h = slice(512 * c, 512 * c + 512)
                        y = pb[bank(t) + c][:, :] if i < 3 else yacc[:, t, h]
                        ins = v.tensor_tensor(ltb[:, t % 2, h], y, gb[:, s, h], ALU.mult)
                        if c == 0:
                            link(ins)
                    ins.then_inc(S("y_c"), 1)
                    dve.wait_ge(S("y_c"), base + t + 1)
                    if i == 0:
                        dve.wait_ge(S("x_in"), 32)
                        dve.wait_ge(S("tm_t"), 2 * NT)
                    else:
                        dve.wait_ge(S("x_ln"), (0, NT, NT + NL, NT + 2 * NL)[i])
                    x = xr[:, t if i < 3 else NL + t, :]
                    link(v.scalar_tensor_tensor(out=x, in0=x, scalar=ALPHA, in1=ltb[:, t % 2, :], op0=ALU.mult,
                                                op1=ALU.add))
                    for c in range(2):
                        link(v.bn_stats(lnst[:, t, 6 * c:6 * c + 6], x[:, 512 * c:512 * c + 512]))
                    v.bn_aggr(lnst[:, t, 12:14], lnst[:, t, 0:12]).then_inc(S("var_r"), 1)
                    dve.wait_ge(S("std_r"), base + t + 1)
                    link(v.reciprocal(lnst[:, t, 15:16], lnst[:, t, 14:15]))
                    v.tensor_scalar(x, x, lnst[:, t, 12:13], lnst[:, t, 15:16], ALU.subtract, ALU.mult)\
                        .then_inc(S("x_hat"), 1)
                    between(t)

            def affine(n, L, ln, chunk):
                def vc(a):
                    return bc(vcol[:, a:a + 8].unsqueeze(2), P, 8, 2)
                a, b = (AB[:, n - 1, i].rearrange("p (k s) -> p k s", s=2) for i in range(2))
                scale, shift = modT[:, L, 8 * chunk + 8:8 * chunk + 16, :], modT[:, L, 8 * chunk:8 * chunk + 8, :]
                link(v.tensor_tensor(a, vc(32 * (ln[0] - 1) + 8 * ln[1]), scale, ALU.mult))
                link(v.tensor_tensor(b, vc(32 * (ln[0] - 1) + 16 + 8 * ln[1]), scale, ALU.mult))
                v.tensor_tensor(b, b, shift, ALU.add).then_inc(S("ab_r"), 1)

            def proj1():
                lb, oml = lbs[:, 3], lbs[:, 4]
                lo = vcol[:, 80:88]
                link(v.tensor_tensor(lbs[:, 0], lo, lo, ALU.subtract))
                dve.sem_inc(S("lb_s"), 1)
                dve.wait_ge(S("lb_e"), 1)
                link(v.reciprocal(lbs[:, 1], lbs[:, 0]))
                link(v.tensor_tensor(lbs[:, 2], lbs[:, 0], lbs[:, 1], ALU.mult))
                link(v.tensor_tensor(lb, lbs[:, 2], lbs[:, 2], ALU.subtract))
                link(v.tensor_scalar(oml, lb, -1.0, 1.0, ALU.mult, ALU.add))
                for d in range(2):
                    link(v.memset(cum[d][:, :, :, 0:1], 0.0))
                for d in range(2):
                    k = (kf, kb)[d]
                    for h in range(HGH):
                        c = slice(HGH * d + h, HGH * d + h + 1)
                        dve.wait_ge(S("sig"), 8 * d + 2 * h + 2)
                        link(v.tensor_scalar(k[:, h, :], k[:, h, :], oml[:, c], None, ALU.mult))
                        link(v.tensor_scalar(forget[:, h, :], forget[:, h, :], oml[:, c], lb[:, c], ALU.mult, ALU.add))
                        ins = v.tensor_scalar(forget[:, h, :], forget[:, h, :], F_MIN, None, ALU.max)
                        if h < HGH - 1:
                            link(ins)
                    ins.then_inc(S("f_r"), 1)
                    dve.wait_ge(S("ln_f"), d + 1)
                    for h in range(HGH):
                        for seg in range(2):
                            ins = v.tensor_tensor_scan(cum[d][:, seg, h, 1:CW], bc(ones[:, 0:1], P, SEQ),
                                                       forget[:, h, seg * SEQ:seg * SEQ + SEQ], 0.0, ALU.mult, ALU.add)
                            if (h, seg) != (HGH - 1, 1):
                                link(ins)
                    ins.then_inc(S("cum_r"), 1)
                dve.wait_ge(S("cum_r"), 2)
                dve.wait_ge(S("bias_in"), 16 * HEADS * ROWS)
                dve.wait_ge(S("c1_in"), 48)
                b = bias.rearrange("p u (i c) -> p (u i) c", c=GRID_W)
                v.tensor_tensor(b, b, bc(window.unsqueeze(1), P, 2 * HEADS * ROWS, GRID_W), ALU.add)\
                    .then_inc(S("bias_r"), 1)

            def hgrn():
                kl = [kf[:, :, 0:SEQ], kb[:, :, 0:SEQ]]
                for d in range(2):
                    dve.wait_ge(S("kend_e"), d + 1)
                    v.tensor_tensor(W[d], W[d], (kf, kb)[d][:, :, SEQ:TOK], ALU.mult).then_inc(S("kend"), 1)
                for d, q in enumerate((qxf, qxb)):
                    dve.wait_ge(S("qx_e"), d + 1)
                    dve.wait_ge(S("in1_c"), len(in1))
                    v.tensor_tensor(q, q, qd, ALU.mult).then_inc(S("qx"), 1)
                v.tensor_tensor(ksum, kl[0], kl[1], ALU.add).then_inc(S("ksum"), 1)
                dve.wait_ge(S("same_mm"), 1)
                dve.wait_ge(S("s_mm"), NU + NU1)
                for i in range(NL):
                    link(v.tensor_copy(AT[:, i, :, i * P:i * P + P], pb[4 + i].rearrange("p (h c) -> p h c", h=HGH)))
                N = len(levels)
                for n in range(N + 2):
                    if 1 <= n <= N:
                        m, d = levels[n - 1]
                        dve.wait_ge(S("hg_exp"), n)
                        for i in range(2):
                            o = slice(i * m, i * m + m)
                            x = qd if i != d else kl[d]
                            w = W[(n - 1) % 2].rearrange("p h (b m) -> p h b m", m=2 * m)[:, :, :, o]
                            ins = v.tensor_tensor(w, w, x.rearrange("p h (b m) -> p h b m", m=2 * m)[:, :, :, o], ALU.mult)
                        ins.then_inc(S("hg_w"), 1)
                    if n >= 2:
                        m, d = levels[n - 2]
                        dve.wait_ge(S("hg_mm"), n - 1)
                        if n >= 3:
                            dve.wait_ge(S("hg_at"), n - 2)
                        for i in range(1 if m == P else NL):
                            b = pb[2 * (n % 2) + i].rearrange("p (h c) -> p h c", h=HGH)
                            if m == P:
                                dst = AT[:, 0, :, P:SEQ] if d == 0 else AT[:, 1, :, 0:P]
                                ins = v.tensor_copy(dst, b)
                            else:
                                k = masks[:, 2 * LEVELS.index(m) + d, :].bitcast(I32).unsqueeze(1)
                                ins = v.copy_predicated(AT[:, i, :, i * P:i * P + P], bc(k, P, HGH, P), b)
                        ins.then_inc(S("hg_at"), 1)
                for t in range(NL):
                    y = o1[:, t, 512:D]
                    yh = y.rearrange("p (h e) -> p h e", h=HGH)
                    sq = W[t].rearrange("p h c -> p (h c)")[:, 0:512]
                    dve.wait_ge(S("hg_o"), t + 1)
                    link(v.tensor_copy(y, pb[6 + t][:, :]))
                    link(v.tensor_tensor(sq, y, y, ALU.mult))
                    link(v.tensor_reduce(rms1[:, t, :], sq.rearrange("p (h e) -> p h e", h=HGH), AX.X, ALU.add))
                    v.tensor_scalar(rms1[:, t, :], rms1[:, t, :], 1.0 / P, 1e-6, ALU.mult, ALU.add)\
                        .then_inc(S("hg_ss"), 1)
                for t in range(NL):
                    y = o1[:, t, 512:D]
                    yh = y.rearrange("p (h e) -> p h e", h=HGH)
                    dve.wait_ge(S("hg_rt"), t + 1)
                    link(v.reciprocal(rms1[:, t, :], rms1[:, t, :]))
                    link(v.tensor_tensor(yh, yh, bc(rms1[:, t, :].unsqueeze(2), P, HGH, P), ALU.mult))
                    link(v.tensor_tensor(yh, yh, bc(onorm.unsqueeze(1), P, HGH, P), ALU.mult))
                    v.tensor_tensor(y, y, gd[:, t, :], ALU.mult).then_inc(S("y_hg"), 1)

            def route():
                L, oh = rt[0], (rt[1], rt[2])
                key, gate, mask, pos = rt[3], rt[4], rt[5], rt[6]
                cnt, over, rank, tmp = (rt[7 + i // 2][:, i % 2] for i in range(4))
                rk = at(RT + 246, NE)
                top, first, e2 = r1[:, 0:2], r1[:, 3:5], r1[:, 2]

                def cols(x):
                    return bc(x.unsqueeze(2), P, NL, NE)
                dve.wait_ge(S("x_hat"), 2 * NT + NL)
                link(v.memset(yacc.rearrange("p t d -> p (t d)"), 0.0))
                link(v.memset(selGT, 0.0))
                dve.wait_ge(S("o_c"), NU + NU1)
                dve.wait_ge(S("logit_mm"), 1)
                link(v.tensor_copy(L, pb[6][:, 0:NL * NE].rearrange("p (t e) -> p t e", t=NL)))
                link(v.tensor_scalar(rk, iota[:, 0:NE], -1.0, float(NE), ALU.mult, ALU.add))
                for j in range(2):
                    link(v.tensor_reduce(top[:, j], L, AX.X, ALU.max))
                    link(v.tensor_tensor(key, L, cols(top[:, j]), ALU.is_equal))
                    link(v.tensor_tensor(key, key, bc(rk.unsqueeze(1), P, NL, NE), ALU.mult))
                    link(v.tensor_reduce(first[:, j], key, AX.X, ALU.max))
                    link(v.tensor_tensor(oh[j], key, cols(first[:, j]), ALU.is_equal))
                    if j == 0:
                        link(v.scalar_tensor_tensor(out=L, in0=oh[0], scalar=NEG, in1=L, op0=ALU.mult, op1=ALU.add))
                v.tensor_tensor(mask, oh[0], oh[1], ALU.add).then_inc(S("mask_r"), 1)
                v.tensor_tensor(e2, top[:, 1], top[:, 0], ALU.subtract).then_inc(S("top_r"), 1)
                dve.wait_ge(S("top_e"), 1)
                w0, w1 = r1[:, 5], r1[:, 6]
                link(v.tensor_scalar(w0, e2, 1.0, None, ALU.add))
                link(v.reciprocal(w0, w0))
                link(v.tensor_tensor(w1, e2, w0, ALU.mult))
                link(v.tensor_tensor(gate, oh[0], cols(w0), ALU.mult))
                link(v.tensor_tensor(key, oh[1], cols(w1), ALU.mult))
                link(v.tensor_tensor(gateT[:, :, 0:NE], gate, key, ALU.add))
                dve.wait_ge(S("pos_mm"), 1)
                link(v.tensor_copy(pos, pb[7][:, 0:16].rearrange("p (t e) -> p t e", t=NL)))
                link(v.tensor_copy(cnt, pb[7][:, 16:24]))
                link(v.scalar_tensor_tensor(out=pos, in0=pos, scalar=1.0, in1=mask, op0=ALU.add, op1=ALU.mult))
                link(v.tensor_scalar(posT[:, :, 0:NE], pos, -1.0, None, ALU.add))
                select(0)
                zero_outputs()

            def route_rest():
                key, pos = rt[3], rt[6]
                cnt, over, rank, tmp = (rt[7 + i // 2][:, i % 2] for i in range(4))
                first = r1[:, 3:5]
                link(v.tensor_scalar(over, cnt, float(CAP), None, ALU.is_gt))
                link(v.tensor_tensor_scan(rank, bc(ones[:, 0:1], P, NE), over, 0.0, ALU.mult, ALU.add))
                link(v.tensor_copy(nover, rank[:, NE - 1:NE]))
                link(v.tensor_copy(ids[:, 0:NE], iota[:, 0:NE]))
                link(v.memset(posT[:, :, NR - 1:NR], -1.0))
                link(v.memset(gateT[:, :, NR - 1:NR], 0.0))
                link(v.memset(at(RT + 48 + NR - 1, 1), 0.0))
                for x in range(EXTRA):
                    link(v.tensor_scalar(tmp, rank, float(x + 1), None, ALU.is_equal))
                    link(v.tensor_tensor(tmp, tmp, over, ALU.mult))
                    tb = bc(tmp.unsqueeze(1), P, NL, NE)
                    link(v.scalar_tensor_tensor(out=key, in0=pos, scalar=float(-CAP), in1=tb, op0=ALU.add, op1=ALU.mult))
                    link(v.tensor_reduce(first[:, 0], key, AX.X, ALU.add))
                    link(v.tensor_scalar(posT[:, :, NE + x], first[:, 0], -1.0, None, ALU.add))
                    link(v.tensor_tensor(key, gateT[:, :, 0:NE], tb, ALU.mult))
                    link(v.tensor_reduce(gateT[:, :, NE + x], key, AX.X, ALU.add))
                    link(v.tensor_tensor(tmp, tmp, iota[:, 0:NE], ALU.mult))
                    link(v.tensor_reduce(first[:, 1, 0:1], tmp, AX.X, ALU.add))
                    link(v.tensor_copy(ids[:, NE + x:NE + x + 1], first[:, 1, 0:1]))
                dve.sem_inc(S("routed"), 1)

            def select(r):
                for t in range(NL):
                    ins = v.tensor_scalar(sel[:, t, :], iota, posT[:, t, bass.ds(r, 1)], None, ALU.is_equal)
                ins.then_inc(S("sel_r"), 1)

            def accumulate(n, t):
                for c in range(2):
                    dve.wait_ge(S("sc_mm"), 4 * n + 2 * t + c + 1)
                    y = yacc[:, t, 512 * c:512 * c + 512]
                    v.tensor_tensor(y, y, pb[4 + c][:, :], ALU.add).then_inc(S("sc_a"), 1)

            def zero_outputs():
                for c in range(2):
                    v.memset(pb[4 + c][:, :], 0.0).then_inc(S("y_zero"), 1)

            def expert(r, n):
                for u in range(UNITS):
                    j, q = u // 4, u % 4
                    o = slot[j % RING] + UNIT * q
                    if q != POOLQ:
                        dve.wait_ge(S("w_hi"), r * UNITS + u + 1)
                        v.tensor_tensor(part(o, UNIT), at(o, UNIT), wH[u % HBUF].bitcast(F32), ALU.subtract)\
                            .then_inc(S("w_lo"), 1)
                    if u == 3:
                        dve.wait_ge(S("g_mm"), r * 2 + 2)
                        select(r + 1)
                    if u == 5:
                        dve.wait_ge(S("sg_t"), r + OPEN)
                        for t in range(NL):
                            ins = v.tensor_scalar(selG[:, t, :], iota, posT[:, t, bass.ds(r, 1)],
                                                  gateT[:, t, bass.ds(r, 1)], ALU.is_equal, ALU.mult)
                        ins.then_inc(S("selg"), 1)
                    if u in (9, 17):
                        accumulate(n, u // 17)
                    c, step = (u - 13) // 8, (u - 13) % 8
                    if step == 0 and 0 <= c < 7:
                        dve.wait_ge(S("e_s"), r * 7 + c + 1)
                        v.tensor_tensor(s_e[:, c % 2, :], s_e[:, c % 2, :], pb[2 + c % 2][:, :], ALU.mult)\
                            .then_inc(S("e_a"), 1)
                    if step == 2 and 1 <= c < 8:
                        k = slice(4 * c - 4, 4 * c)
                        dve.wait_ge(S("e_aH"), r * 7 + c)
                        v.tensor_tensor(aL[:, k, :].rearrange("p k c -> p (k c)"), pb[6][:, :],
                                        aH[:, k, :].rearrange("p k c -> p (k c)").bitcast(F32), ALU.subtract)\
                            .then_inc(S("e_aT"), 1)
                    if step == 4 and c == 6:
                        dve.wait_ge(S("hs_h"), r + 2)
                        v.tensor_tensor(hsL, hsN, hsH.bitcast(F32), ALU.subtract).then_inc(S("hs_r"), 1)

            setup()
            s_col = sT.rearrange("p (s k) -> p k s", s=2)
            dve.wait_ge(S("s_hi"), 2)
            subtract(s_hl[:, :, 2:4], s_col, s_hl[:, :, 0:2]).then_inc(S("s_lo"), 1)
            v.tensor_tensor(s_h0[:, :, 2:4], s_col, s_col, ALU.subtract).then_inc(S("s_lo"), 1)
            ada(0, 12)
            dve.wait_ge(S("mod_col"), 12)
            affine(1, 0, (1, 0), 3)
            low_halves(0)
            proj0()
            heads0()
            attention(units, 0, lambda u: oA[:, u[2], (0 if u[0] == "a" else 512) + HD * u[1]:][:, 0:HD],
                      ada_beside)
            gates(0, 2, 2, 0)
            layernorm(0, NT, 0, lambda t: 2 * (t % 2))
            ada(12 + ADA_ATT, 24)
            dve.wait_ge(S("mod_col"), 24)
            affine(2, 1, (2, 0), 0)
            affine(3, 1, (1, 1), 3)
            gates(0, 5, 2, 4)
            low_halves(1)
            ffn0()
            layernorm(1, NT, NT, lambda t: 2 * t, lambda t: low_halves(2, t - 2, t - 1) if t >= 2 else None)
            low_halves(2, NT - 2)
            proj1()
            attention(units1, NU, lambda u: o1[:, u[2], HD * u[1]:][:, 0:HD])
            hgrn()
            gates(1, 2, 1, 8)
            layernorm(2, NL, 2 * NT, lambda t: 2 * (t % 2))
            route()
            route_rest()
            dve.wait_ge(S("x_ln"), NT + 2 * NL)
            dve.wait_ge(S("hs_h"), 1)
            v.tensor_tensor(hsL, hsN, hsH.bitcast(F32), ALU.subtract).then_inc(S("hs_r"), 1)
            for name in ("e_a", "e_aT"):
                dve.sem_inc(S(name), OPEN)
            with dve.Fori(0, NE) as r:
                expert(r, r)
            for t in range(NL):
                accumulate(NE, t)
            dve.wait_ge(S("sc_a"), 4 * NE + 4)
            many = dve.value_load(nover[0:1, :], min_val=0, max_val=EXTRA)
            with dve.If(many > 0):
                zero_outputs()
                with dve.Fori(NE, ROUNDS) as r:
                    expert(r, r + 1)
                for t in range(NL):
                    accumulate(ROUNDS + 1, t)
                dve.wait_ge(S("sc_a"), 4 * ROUNDS + 8)
            gates(1, 5, 1, 10)
            layernorm(3, NL, 2 * NT + NL, None)

        @block.gpsimd
        def _(pool):
            made = [0]

            def gain_bias(i, tiles, base):
                for t in range(tiles):
                    pool.wait_ge(S("lnrow_in"), 32 * (i + 1))
                    pool.wait_ge(S("x_hat"), base + t + 1)
                    if i < 3:
                        pool.wait_ge(S("tm_t"), TMB[i + 1] + 2 * t + 2)
                    x = xr[:, t if i < 3 else NL + t, :]
                    y = xr[:, t if i < 2 else NL + t, :]
                    made[0] += 1
                    nc.gpsimd.tensor_tensor(y, x, lnrow[:, 0, :], ALU.mult).then_inc(S("x_g"), 1)
                    pool.wait_ge(S("x_g"), made[0])
                    nc.gpsimd.tensor_tensor(y, y, lnrow[:, 1, :], ALU.add).then_inc(S("x_ln"), 1)
            lows = ada_units(F32R)
            for u, w in enumerate(ada_units()):
                pool.wait_ge(S("ada_hi"), u + 1)
                nc.gpsimd.tensor_tensor(lows[u], w, awH[u % 2].bitcast(F32), ALU.subtract).then_inc(S("ada_lo"), 1)
            gain_bias(0, NT, 0)
            gain_bias(1, NL, NT)
            lows = in1_units(F32R)
            for u, (_, _, w) in enumerate(in1_units()):
                pool.wait_ge(S("in1_hi"), u + 1)
                nc.gpsimd.tensor_tensor(lows[u][2], w, in1_hi(u).bitcast(F32), ALU.subtract).then_inc(S("in1_lo"), 1)
            pool.wait_ge(S("kend"), 2)
            for n, (m, d) in enumerate(levels):
                c = cum[d][:, 0]
                if n < 2:
                    pool.wait_ge(S("kend_t"), 2 * n + 2)
                else:
                    pool.wait_ge(S("hg_mm"), n - 1)
                nb = SEQ // (2 * m)
                for h in ([None] if nb == 1 else range(HGH)):
                    if h is None:
                        ins = nc.gpsimd.tensor_tensor(W[n % 2], c[:, :, 1 - d:1 - d + SEQ],
                                              bc(c[:, :, m:m + 1], P, HGH, SEQ), ALU.subtract)
                    else:
                        ins = nc.gpsimd.tensor_tensor(W[n % 2][:, h].rearrange("p (b m) -> p b m", b=nb),
                                              c[:, h, 1 - d:1 - d + SEQ].rearrange("p (b m) -> p b m", b=nb),
                                              bc(c[:, h, m:SEQ:2 * m].unsqueeze(2), P, nb, 2 * m), ALU.subtract)
                ins.then_inc(S("hg_sub"), 1)
            gain_bias(2, NL, 2 * NT)
            def low_parts(r):
                for j in range(21):
                    o = slot[j % RING] + UNIT * POOLQ
                    pool.wait_ge(S("w_hi"), r * UNITS + 4 * j + POOLQ + 1)
                    nc.gpsimd.tensor_tensor(part(o, UNIT), at(o, UNIT), wH[(4 * j + POOLQ) % HBUF].bitcast(F32),
                                            ALU.subtract).then_inc(S("w_lo_g"), 1)
            with pool.Fori(0, NE) as r:
                low_parts(r)
            pool.wait_ge(S("routed"), 1)
            many = pool.value_load(nover[0:1, :], min_val=0, max_val=EXTRA)
            with pool.If(many > 0):
                with pool.Fori(NE, ROUNDS) as r:
                    low_parts(r)
            gain_bias(3, NL, 2 * NT + NL)
            if made[0]:
                pool.wait_ge(S("x_ln"), made[0])


_NAMES = ["x", "c", "ctx", "c_ctx", "ada_w", "ada_b", "ln1_g", "ln1_b", "ln2_g", "ln2_b", "ev_w_in", "ev_qn_g",
          "ev_kn_g", "ev_cq_g", "ev_ckv_g", "ev_w_uq", "ev_w_ukv", "ev_w_out", "ff_w_gate", "ff_w_up", "ff_w_down",
          "od_w_in", "od_rpb", "od_lb_logits", "od_onorm_g", "od_w_out", "moe_router", "moe_w_gate", "moe_w_up",
          "moe_w_down"]
_PACKED = ["c", "c_ctx", "ada_b", "od_lb_logits", "od_rpb"]


def kernel(**inputs):
    import concourse.bacc as bacc
    from concourse.bass_utils import run_bass_kernel_spmd

    nc = bacc.Bacc("TRN2", target_bir_lowering=False, num_devices=1)
    a = {n: np.ascontiguousarray(inputs[n]) for n in _NAMES}
    arrays = {n: a[n] for n in _NAMES if n not in _PACKED}
    arrays["c_base"], arrays["c_rope"], arrays["c_hg"] = constants()
    arrays["vr1"] = a["ada_b"].reshape(96, P)
    arrays["vr2"] = np.concatenate([a[n].reshape(-1, P) for n in ("ln1_g", "ln1_b", "ln2_g", "ln2_b", "c", "c_ctx",
                                                                  "od_lb_logits")], 0)
    arrays["rpb"] = np.pad(a["od_rpb"][0], ((0, 0), (0, 0), (RPB_PAD, RPB_PAD)))
    feeds, aps = {}, {}
    for n, v in arrays.items():
        feeds[f"in_{n}"] = v
        aps[n] = nc.dram_tensor(f"in_{n}", v.shape, F32, kind="ExternalInput").ap()
    out = nc.dram_tensor("out_x", (1, SEQ, D), F32, kind="ExternalOutput").ap()
    bass_hybrid_dit(nc, aps, out)
    r = run_bass_kernel_spmd(nc, [feeds], core_ids=[0])
    return r.results[0]["out_x"]
```
